# Optimizing a Trainium2 kernel written in Bass

```python
import math
import jax, jax.numpy as jnp
from jax import lax
import numpy as np

D_MODEL = 1024
BATCH = 1
SEQ = 512
DEPTH = 1

EPS = 1e-6
NEG_INF = -1e30

A_HEADS = 8
A_HEAD_DIM = 64
A_WIDTH = A_HEADS * A_HEAD_DIM
DILATED_PATTERNS = ((128, 1), (512, 4), (2048, 16))
A_BLOCK = 64

REL_BUCKETS = 32
REL_MAX_DISTANCE = 1024

B_HEADS = 8
B_Q_LORA = 256
B_KV_LORA = 128
B_QK_NOPE = 64
B_QK_ROPE = 32
B_V_DIM = 64
B_WIDTH = B_HEADS * B_V_DIM
ROPE_THETA = 10000.0
B_Q_BLOCK = 128

MIX_WIDTH = A_WIDTH + B_WIDTH
IN_PROJ_WIDTH = 3 * A_WIDTH + B_Q_LORA + B_KV_LORA + B_QK_ROPE

N_GROUPS = 4
EXPERTS_PER_GROUP = 8
N_EXPERTS = N_GROUPS * EXPERTS_PER_GROUP
TOP_K_IN_GROUP = 2
EXPERT_FF = 256
MOE_BLOCK = 128


def rmsnorm(x, g):
    xf = x.astype(jnp.float32)
    y = xf * lax.rsqrt(jnp.mean(xf * xf, axis=-1, keepdims=True) + EPS)
    return (y * g.astype(jnp.float32)).astype(x.dtype)

def t5_relative_bucket(rel):
    half = REL_BUCKETS // 2
    max_exact = half // 2
    n = np.abs(rel)
    large = max_exact + (np.log(np.maximum(n, 1) / max_exact)
                         / math.log(REL_MAX_DISTANCE / max_exact) * (half - max_exact)).astype(np.int32)
    large = np.minimum(large, half - 1)
    return (np.where(rel > 0, half, 0) + np.where(n < max_exact, n, large)).astype(np.int32)

def dilated_window_attention(q, k, v, rel_bias, dilation, half_steps):
    b, h, s, dh = q.shape
    L = s // dilation
    qb = math.gcd(L, A_BLOCK)
    nb = L // qb
    span = qb + 2 * half_steps

    def to_residue(t):
        return t.reshape(b, h, L, dilation, dh).transpose(0, 1, 3, 2, 4)

    qr, kr, vr = to_residue(q), to_residue(k), to_residue(v)
    pad = ((0, 0), (0, 0), (0, 0), (half_steps, half_steps), (0, 0))
    kp, vp = jnp.pad(kr, pad), jnp.pad(vr, pad)
    key_idx = np.arange(nb)[:, None] * qb + np.arange(span)[None, :]
    kb = jnp.take(kp, key_idx, axis=3)
    vb = jnp.take(vp, key_idx, axis=3)
    qblk = qr.reshape(b, h, dilation, nb, qb, dh)
    scores = jnp.einsum('bhrnqd,bhrnkd->bhrnqk', qblk, kb,
                        preferred_element_type=jnp.float32) * (dh ** -0.5)
    rel_steps = np.arange(span)[None, :] - half_steps - np.arange(qb)[:, None]
    buckets = t5_relative_bucket(rel_steps * dilation)
    bias = rel_bias[buckets].astype(jnp.float32).transpose(2, 0, 1)
    key_pos = key_idx - half_steps
    valid = ((np.abs(rel_steps) <= half_steps)[None]
             & (key_pos >= 0)[:, None, :] & (key_pos < L)[:, None, :])
    scores = jnp.where(valid[None, None, None], scores + bias[None, :, None, None], NEG_INF)
    m = jnp.max(scores, axis=-1, keepdims=True)
    p = jnp.exp(scores - m)
    l = jnp.sum(p, axis=-1, keepdims=True)
    o = jnp.einsum('bhrnqk,bhrnkd->bhrnqd', p, vb, preferred_element_type=jnp.float32) / l
    lse = (m + jnp.log(l))[..., 0]
    o = o.reshape(b, h, dilation, L, dh).transpose(0, 1, 3, 2, 4).reshape(b, h, s, dh)
    lse = lse.reshape(b, h, dilation, L).transpose(0, 1, 3, 2).reshape(b, h, s)
    return o, lse

def mixer_dilated(q, k, v, rel_bias):
    outs, lses = [], []
    for window, dilation in DILATED_PATTERNS:
        o, lse = dilated_window_attention(q, k, v, rel_bias, dilation, window // (2 * dilation))
        outs.append(o)
        lses.append(lse)
    w = jax.nn.softmax(jnp.stack(lses, 0), axis=0)
    return jnp.einsum('pbhs,pbhsd->bhsd', w, jnp.stack(outs, 0))

def apply_rope(x):
    s, d = x.shape[1], x.shape[-1]
    half = d // 2
    inv_freq = ROPE_THETA ** (-(jnp.arange(half, dtype=jnp.float32) / half))
    ang = jnp.arange(s, dtype=jnp.float32)[:, None] * inv_freq[None, :]
    cos, sin = jnp.cos(ang)[None, :, None, :], jnp.sin(ang)[None, :, None, :]
    x1, x2 = x[..., :half].astype(jnp.float32), x[..., half:].astype(jnp.float32)
    return jnp.concatenate([x1 * cos - x2 * sin, x1 * sin + x2 * cos], axis=-1).astype(x.dtype)

def mixer_mla(c_q, c_kv, k_rope, g_q_latent, w_q_up, g_kv_latent, w_kv_up):
    b, s, _ = c_q.shape
    q = (rmsnorm(c_q, g_q_latent) @ w_q_up).reshape(b, s, B_HEADS, B_QK_NOPE + B_QK_ROPE)
    q_nope, q_rope = q[..., :B_QK_NOPE], apply_rope(q[..., B_QK_NOPE:])
    kv = (rmsnorm(c_kv, g_kv_latent) @ w_kv_up).reshape(b, s, B_HEADS, B_QK_NOPE + B_V_DIM)
    k_nope, v = kv[..., :B_QK_NOPE], kv[..., B_QK_NOPE:].astype(jnp.float32)
    k_r = apply_rope(k_rope[:, :, None, :])[:, :, 0]
    scale = (B_QK_NOPE + B_QK_ROPE) ** -0.5
    nb = s // B_Q_BLOCK

    def block(args):
        qn, qr = args
        sc = (jnp.einsum('bqhd,bkhd->bhqk', qn, k_nope, preferred_element_type=jnp.float32)
              + jnp.einsum('bqhd,bkd->bhqk', qr, k_r, preferred_element_type=jnp.float32)) * scale
        p = jax.nn.softmax(sc, axis=-1)
        return jnp.einsum('bhqk,bkhd->bqhd', p, v)

    qn_b = q_nope.reshape(b, nb, B_Q_BLOCK, B_HEADS, B_QK_NOPE).transpose(1, 0, 2, 3, 4)
    qr_b = q_rope.reshape(b, nb, B_Q_BLOCK, B_HEADS, B_QK_ROPE).transpose(1, 0, 2, 3, 4)
    o = lax.map(block, (qn_b, qr_b))
    return o.transpose(1, 0, 2, 3, 4).reshape(b, s, B_WIDTH)

def hierarchical_moe(t, w_router_group, b_router_group, w_router_expert, b_router_expert,
                     w_gate, w_up, w_down):
    n_tok, d = t.shape
    group_logits = jnp.dot(t, w_router_group, preferred_element_type=jnp.float32) + b_router_group.astype(jnp.float32)
    group_probs = jax.nn.softmax(group_logits, axis=-1)
    group_idx = jnp.argmax(group_probs, axis=-1)
    group_gate = jnp.take_along_axis(group_probs, group_idx[:, None], axis=-1)
    expert_logits = (jnp.dot(t, w_router_expert, preferred_element_type=jnp.float32)
                     + b_router_expert.astype(jnp.float32)).reshape(n_tok, N_GROUPS, EXPERTS_PER_GROUP)
    in_group = jnp.take_along_axis(expert_logits, group_idx[:, None, None], axis=1)[:, 0]
    top_p, top_i = lax.top_k(jax.nn.softmax(in_group, axis=-1), TOP_K_IN_GROUP)
    gates = group_gate * top_p / jnp.sum(top_p, axis=-1, keepdims=True)
    expert_ids = group_idx[:, None] * EXPERTS_PER_GROUP + top_i

    n_assign = n_tok * TOP_K_IN_GROUP
    flat_expert = expert_ids.reshape(-1)
    flat_token = jnp.repeat(jnp.arange(n_tok), TOP_K_IN_GROUP)
    flat_gate = gates.reshape(-1)
    order = jnp.argsort(flat_expert)
    s_expert, s_token, s_gate = flat_expert[order], flat_token[order], flat_gate[order]
    counts = jnp.bincount(flat_expert, length=N_EXPERTS)
    starts = jnp.cumsum(counts) - counts
    padded = (counts + MOE_BLOCK - 1) // MOE_BLOCK * MOE_BLOCK
    padded_ends = jnp.cumsum(padded)
    padded_starts = padded_ends - padded
    dest = padded_starts[s_expert] + jnp.arange(n_assign) - starts[s_expert]
    n_blocks = -(-n_assign // MOE_BLOCK) + N_EXPERTS
    buf = jnp.zeros((n_blocks * MOE_BLOCK, d), t.dtype).at[dest].set(t[s_token])
    block_expert = jnp.minimum(
        jnp.searchsorted(padded_ends, jnp.arange(n_blocks) * MOE_BLOCK, side='right'), N_EXPERTS - 1)

    def expert_block(args):
        xb, e = args
        hb = jax.nn.silu(xb @ w_gate[e]) * (xb @ w_up[e])
        return hb @ w_down[e]

    out = lax.map(expert_block, (buf.reshape(n_blocks, MOE_BLOCK, d), block_expert))
    contrib = out.reshape(n_blocks * MOE_BLOCK, d)[dest].astype(jnp.float32) * s_gate[:, None]
    return jax.ops.segment_sum(contrib, s_token, num_segments=n_tok)

def first_inputs(seed: int = 0) -> dict:
    key = jax.random.key(seed)
    ks = jax.random.split(key, 24)
    f32 = jnp.float32
    nrm = lambda k, shape, fan_in: jax.random.normal(k, shape, f32) * (fan_in ** -0.5)
    gain = lambda k, shape: 1.0 + 0.02 * jax.random.normal(k, shape, f32)
    return {
        "x": jax.random.normal(ks[0], (BATCH, SEQ, D_MODEL), f32),
        "g_attn_norm": gain(ks[1], (DEPTH, D_MODEL)),
        "w_in": nrm(ks[2], (DEPTH, D_MODEL, IN_PROJ_WIDTH), D_MODEL),
        "rel_bias": 0.5 * jax.random.normal(ks[3], (REL_BUCKETS, A_HEADS), f32),
        "g_q_latent": gain(ks[4], (DEPTH, B_Q_LORA)),
        "w_q_up": nrm(ks[5], (DEPTH, B_Q_LORA, B_HEADS * (B_QK_NOPE + B_QK_ROPE)), B_Q_LORA),
        "g_kv_latent": gain(ks[6], (DEPTH, B_KV_LORA)),
        "w_kv_up": nrm(ks[7], (DEPTH, B_KV_LORA, B_HEADS * (B_QK_NOPE + B_V_DIM)), B_KV_LORA),
        "g_out_a": gain(ks[8], (DEPTH, A_WIDTH)),
        "g_out_b": gain(ks[9], (DEPTH, B_WIDTH)),
        "w_out": nrm(ks[10], (DEPTH, MIX_WIDTH, D_MODEL), MIX_WIDTH),
        "g_ffn_norm": gain(ks[11], (DEPTH, D_MODEL)),
        "w_router_group": nrm(ks[12], (DEPTH, D_MODEL, N_GROUPS), D_MODEL),
        "b_router_group": 0.01 * jax.random.normal(ks[13], (DEPTH, N_GROUPS), f32),
        "w_router_expert": nrm(ks[14], (DEPTH, D_MODEL, N_EXPERTS), D_MODEL),
        "b_router_expert": 0.01 * jax.random.normal(ks[15], (DEPTH, N_EXPERTS), f32),
        "w_gate": nrm(ks[16], (DEPTH, N_EXPERTS, D_MODEL, EXPERT_FF), D_MODEL),
        "w_up": nrm(ks[17], (DEPTH, N_EXPERTS, D_MODEL, EXPERT_FF), D_MODEL),
        "w_down": nrm(ks[18], (DEPTH, N_EXPERTS, EXPERT_FF, D_MODEL), EXPERT_FF),
        "g_final": gain(ks[19], (D_MODEL,)),
    }

def first_block(x, g_attn_norm, w_in, rel_bias, g_q_latent, w_q_up, g_kv_latent, w_kv_up,
              g_out_a, g_out_b, w_out, g_ffn_norm, w_router_group, b_router_group,
              w_router_expert, b_router_expert, w_gate, w_up, w_down, g_final):
    b, s, d = x.shape
    splits = list(np.cumsum([A_WIDTH, A_WIDTH, A_WIDTH, B_Q_LORA, B_KV_LORA]))
    for l in range(DEPTH):
        h = rmsnorm(x, g_attn_norm[l])
        proj = h @ w_in[l]
        q_a, k_a, v_a, c_q, c_kv, k_rope = jnp.split(proj, splits, axis=-1)
        heads = lambda t: t.reshape(b, s, A_HEADS, A_HEAD_DIM).transpose(0, 2, 1, 3)
        out_a = mixer_dilated(heads(q_a), heads(k_a), heads(v_a), rel_bias)
        out_a = out_a.transpose(0, 2, 1, 3).reshape(b, s, A_WIDTH)
        out_b = mixer_mla(c_q, c_kv, k_rope, g_q_latent[l], w_q_up[l], g_kv_latent[l], w_kv_up[l])
        mixed = jnp.concatenate([rmsnorm(out_a, g_out_a[l]), rmsnorm(out_b, g_out_b[l])], axis=-1)
        x = x + (mixed.astype(x.dtype) @ w_out[l])
        h2 = rmsnorm(x, g_ffn_norm[l]).reshape(b * s, d)
        y = hierarchical_moe(h2, w_router_group[l], b_router_group[l], w_router_expert[l],
                             b_router_expert[l], w_gate[l], w_up[l], w_down[l])
        x = x + y.reshape(b, s, d).astype(x.dtype)
    return rmsnorm(x, g_final)


HG_HEADS = 8
HG_DK = 128
HG_DV = D_MODEL // HG_HEADS
HG_DIM_K = HG_HEADS * HG_DK
HG_DIM_V = HG_HEADS * HG_DV
RET_HEADS = 4
RET_DK = 256
RET_DV = 256
RET_DIM_K = RET_HEADS * RET_DK
RET_DIM_V = RET_HEADS * RET_DV
ROPE_BASE = 10000.0
MAX_POS_OFFSET = 4096
CHUNK = 64
PROJ_WIDTHS = (HG_DIM_K, HG_DIM_K, HG_DIM_K, HG_DIM_V, HG_DIM_V, RET_DIM_K, RET_DIM_K, RET_DIM_V, RET_DIM_V, D_MODEL, D_MODEL)
PROJ_DIM = HG_DIM_K * 3 + HG_DIM_V * 2 + RET_DIM_K * 2 + RET_DIM_V * 2 + D_MODEL * 2
N_EXPERTS_2 = N_GROUPS * EXPERTS_PER_GROUP
TOP_K = 2
D_EXPERT = 512
DEEPNORM_ALPHA = (2 * DEPTH) ** 0.25
DEEPNORM_BETA = (8 * DEPTH) ** -0.25
LN_EPS = 1e-5
RMS_EPS = 1e-6


def _layer_norm(x, g, b):
    xf = x.astype(jnp.float32)
    mu = jnp.mean(xf, -1, keepdims=True)
    var = jnp.mean(jnp.square(xf - mu), -1, keepdims=True)
    return ((xf - mu) * lax.rsqrt(var + LN_EPS) * g + b).astype(x.dtype)

def _rms_norm_heads(o, g):
    of = o.astype(jnp.float32)
    of = of * lax.rsqrt(jnp.mean(of * of, -1, keepdims=True) + RMS_EPS)
    return of.reshape(*o.shape[:-2], -1) * g

def _to_chunks(t):
    b, l, h, d = t.shape
    return t.reshape(b, l // CHUNK, CHUNK, h, d).transpose(1, 0, 3, 2, 4)

def _from_chunks(t):
    n, b, h, c, d = t.shape
    return t.transpose(1, 0, 3, 2, 4).reshape(b, n * c, h, d)

def _hgrn2_scan(q, k, v, log_f):
    dt = v.dtype
    qc, kc, vc, lfc = (_to_chunks(t.astype(jnp.float32)) for t in (q, k, v, log_f))
    b, h, dk, dv = qc.shape[1], qc.shape[2], qc.shape[-1], vc.shape[-1]
    causal = jnp.tril(jnp.ones((CHUNK, CHUNK), bool))[:, :, None]

    def step(S, inp):
        qb, kb, vb, lf = inp
        G = jnp.cumsum(lf, axis=2)
        g_last = G[:, :, -1:, :]
        decay = jnp.exp(jnp.where(causal, G[:, :, :, None, :] - G[:, :, None, :, :], -jnp.inf))
        attn = jnp.einsum('bhtd,bhsd,bhtsd->bhts', qb, kb, decay)
        o = jnp.einsum('bhts,bhsv->bhtv', attn, vb) + jnp.einsum('bhtd,bhdv->bhtv', qb * jnp.exp(G), S)
        S = jnp.exp(g_last[:, :, 0, :, None]) * S + jnp.einsum('bhsd,bhsv->bhdv', kb * jnp.exp(g_last - G), vb)
        return S, o

    S0 = jnp.zeros((b, h, dk, dv), jnp.float32)
    _, o = lax.scan(step, S0, (qc, kc, vc, lfc))
    return _from_chunks(o).astype(dt)

def _retention_scan(q, k, v, log_gamma):
    dt = v.dtype
    qc, kc, vc = (_to_chunks(t.astype(jnp.float32)) for t in (q, k, v))
    b, h, dk, dv = qc.shape[1], qc.shape[2], qc.shape[-1], vc.shape[-1]
    idx = jnp.arange(CHUNK, dtype=jnp.float32)
    rel = idx[:, None] - idx[None, :]
    lg = log_gamma[:, None]
    decay = jnp.where(rel >= 0, jnp.exp(jnp.maximum(rel, 0.0) * log_gamma[:, None, None]), 0.0)
    cross = jnp.exp((idx + 1.0) * lg)[:, :, None]
    k_dec = jnp.exp((CHUNK - 1.0 - idx) * lg)[:, :, None]
    chunk_dec = jnp.exp(CHUNK * log_gamma)[:, None, None]

    def step(R, inp):
        qb, kb, vb = inp
        inner = jnp.einsum('bhtd,bhsd->bhts', qb, kb) * decay
        o = jnp.einsum('bhts,bhsv->bhtv', inner, vb) + cross * jnp.einsum('bhtd,bhdv->bhtv', qb, R)
        R = chunk_dec * R + jnp.einsum('bhsd,bhsv->bhdv', kb * k_dec, vb)
        return R, o

    R0 = jnp.zeros((b, h, dk, dv), jnp.float32)
    _, o = lax.scan(step, R0, (qc, kc, vc))
    return _from_chunks(o).astype(dt)

def _rotary(t, positions):
    d = t.shape[-1]
    inv = 1.0 / (ROPE_BASE ** jnp.linspace(0.0, 1.0, d // 2, dtype=jnp.float32))
    ang = positions.astype(jnp.float32)[..., None] * inv
    sin, cos = jnp.sin(ang)[:, :, None, :], jnp.cos(ang)[:, :, None, :]
    tf = t.astype(jnp.float32)
    t1, t2 = tf[..., 0::2], tf[..., 1::2]
    out = jnp.stack([t1 * cos - t2 * sin, t1 * sin + t2 * cos], axis=-1).reshape(t.shape)
    return out.astype(t.dtype)

def _token_mixer(x, positions, w_in, lb, hg_norm_g, ret_norm_g, w_branch_hg, w_branch_ret, w_out):
    b, l, _ = x.shape
    proj = x @ w_in
    hq, hf_fwd, hf_bwd, hi, hgate, rq, rk, rv, rgate, ga, gb = jnp.split(proj, np.cumsum(PROJ_WIDTHS)[:-1].tolist(), axis=-1)
    heads = lambda t, n: t.reshape(b, l, n, -1)
    flip = lambda t: jnp.flip(t, axis=1)

    q_h = heads(jax.nn.silu(hq), HG_HEADS)
    v_h = heads(hi, HG_HEADS)

    def hgrn_direction(f_logits, qd, vd):
        f = lb + (1.0 - lb) * jax.nn.sigmoid(f_logits.astype(jnp.float32))
        return _hgrn2_scan(qd, heads(1.0 - f, HG_HEADS), vd, heads(jnp.log(f), HG_HEADS))

    o_hg = hgrn_direction(hf_fwd, q_h, v_h) + flip(hgrn_direction(flip(hf_bwd), flip(q_h), flip(v_h)))
    o_hg = _rms_norm_heads(o_hg, hg_norm_g) * jax.nn.silu(hgate.astype(jnp.float32))
    y_hg = o_hg.astype(x.dtype) @ w_branch_hg

    rq_h = _rotary(heads(rq, RET_HEADS), positions)
    rk_h = _rotary(heads(rk, RET_HEADS), positions) * RET_DK ** -0.5
    rv_h = heads(rv, RET_HEADS)
    log_gamma = jnp.log(1.0 - 2.0 ** (-5.0 - jnp.arange(RET_HEADS, dtype=jnp.float32)))
    o_ret = _retention_scan(rq_h, rk_h, rv_h, log_gamma) + flip(_retention_scan(flip(rq_h), flip(rk_h), flip(rv_h), log_gamma))
    o_ret = _rms_norm_heads(o_ret, ret_norm_g) * jax.nn.silu(rgate.astype(jnp.float32))
    y_ret = o_ret.astype(x.dtype) @ w_branch_ret

    merged = jax.nn.sigmoid(ga) * y_hg + jax.nn.sigmoid(gb) * y_ret
    return merged @ w_out

def _hier_moe(x, w_group, b_group, w_router, b_router, w1, w3, w2):
    t, d = x.shape
    g_logits = (x @ w_group).astype(jnp.float32) + b_group
    grp = jnp.argmax(g_logits, -1)
    p_grp = jnp.take_along_axis(jax.nn.softmax(g_logits, -1), grp[:, None], -1)
    e_logits = ((x @ w_router).astype(jnp.float32) + b_router).reshape(t, N_GROUPS, EXPERTS_PER_GROUP)
    e_logits = jnp.take_along_axis(e_logits, grp[:, None, None], 1)[:, 0]
    top_p, top_i = lax.top_k(jax.nn.softmax(e_logits, -1), TOP_K)
    top_p = top_p / jnp.sum(top_p, -1, keepdims=True)
    wts = (p_grp * top_p).reshape(-1)
    eid = (grp[:, None] * EXPERTS_PER_GROUP + top_i).reshape(-1)
    n_assign = t * TOP_K
    tok = jnp.arange(n_assign, dtype=jnp.int32) // TOP_K

    order = jnp.argsort(eid)
    e_sorted = eid[order]
    counts = jnp.zeros((N_EXPERTS_2,), jnp.int32).at[eid].add(1)
    start = jnp.cumsum(counts) - counts
    padded = (counts + MOE_BLOCK - 1) // MOE_BLOCK * MOE_BLOCK
    pend = jnp.cumsum(padded)
    pstart = pend - padded
    dest = pstart[e_sorted] + (jnp.arange(n_assign, dtype=jnp.int32) - start[e_sorted])
    n_blocks = -(-n_assign // MOE_BLOCK) + N_EXPERTS_2
    rows = jnp.full((n_blocks * MOE_BLOCK,), t, jnp.int32).at[dest].set(tok[order])
    row_w = jnp.zeros((n_blocks * MOE_BLOCK,), jnp.float32).at[dest].set(wts[order])
    block_expert = jnp.clip(jnp.searchsorted(pend, jnp.arange(n_blocks, dtype=jnp.int32) * MOE_BLOCK, side='right'), 0, N_EXPERTS_2 - 1)
    x_pad = jnp.concatenate([x, jnp.zeros((1, d), x.dtype)], 0)
    xb = x_pad[rows].reshape(n_blocks, MOE_BLOCK, d)

    def expert_block(args):
        xs, e = args
        return (jax.nn.silu(xs @ w1[e]) * (xs @ w3[e])) @ w2[e]

    yb = lax.map(expert_block, (xb, block_expert))
    y = yb.reshape(-1, d) * row_w[:, None].astype(x.dtype)
    return jax.ops.segment_sum(y, rows, num_segments=t + 1)[:t]

def second_inputs(seed: int = 0) -> dict:
    key = jax.random.key(seed)
    ks = jax.random.split(key, 20)
    nrm = lambda k, shape, s: jax.random.normal(k, shape, jnp.float32) * s
    beta = DEEPNORM_BETA
    x = nrm(ks[0], (BATCH, SEQ, D_MODEL), 1.0)
    positions = jax.random.randint(ks[1], (BATCH, 1), 0, MAX_POS_OFFSET, jnp.int32) + jnp.arange(SEQ, dtype=jnp.int32)[None, :]
    col_scales = (1.0, 1.0, 1.0, beta, 1.0, 1.0, 1.0, beta, 1.0, 1.0, 1.0)
    col_scale = jnp.concatenate([jnp.full((w,), s, jnp.float32) for w, s in zip(PROJ_WIDTHS, col_scales)])
    w_in = nrm(ks[2], (DEPTH, D_MODEL, PROJ_DIM), D_MODEL ** -0.5) * col_scale
    hg_lb_logits = nrm(ks[3], (DEPTH + 1, HG_DIM_K), 0.5)
    hg_norm_g = 1.0 + nrm(ks[4], (DEPTH, HG_DIM_V), 0.02)
    ret_norm_g = 1.0 + nrm(ks[5], (DEPTH, RET_DIM_V), 0.02)
    w_branch_hg = nrm(ks[6], (DEPTH, HG_DIM_V, D_MODEL), HG_DIM_V ** -0.5 * beta)
    w_branch_ret = nrm(ks[7], (DEPTH, RET_DIM_V, D_MODEL), RET_DIM_V ** -0.5 * beta)
    w_out = nrm(ks[8], (DEPTH, D_MODEL, D_MODEL), D_MODEL ** -0.5 * beta)
    ln1_g = 1.0 + nrm(ks[9], (DEPTH, D_MODEL), 0.02)
    ln1_b = nrm(ks[10], (DEPTH, D_MODEL), 0.02)
    w_group = nrm(ks[11], (DEPTH, D_MODEL, N_GROUPS), D_MODEL ** -0.5)
    b_group = nrm(ks[12], (DEPTH, N_GROUPS), 0.01)
    w_router = nrm(ks[13], (DEPTH, D_MODEL, N_EXPERTS_2), D_MODEL ** -0.5)
    b_router = nrm(ks[14], (DEPTH, N_EXPERTS_2), 0.01)
    w1 = nrm(ks[15], (DEPTH, N_EXPERTS_2, D_MODEL, D_EXPERT), D_MODEL ** -0.5)
    w3 = nrm(ks[16], (DEPTH, N_EXPERTS_2, D_MODEL, D_EXPERT), D_MODEL ** -0.5)
    w2 = nrm(ks[17], (DEPTH, N_EXPERTS_2, D_EXPERT, D_MODEL), D_EXPERT ** -0.5 * beta)
    ln2_g = 1.0 + nrm(ks[18], (DEPTH, D_MODEL), 0.02)
    ln2_b = nrm(ks[19], (DEPTH, D_MODEL), 0.02)
    return {'x': x, 'positions': positions, 'w_in': w_in, 'hg_lb_logits': hg_lb_logits,
            'hg_norm_g': hg_norm_g, 'ret_norm_g': ret_norm_g, 'w_branch_hg': w_branch_hg,
            'w_branch_ret': w_branch_ret, 'w_out': w_out, 'ln1_g': ln1_g, 'ln1_b': ln1_b,
            'w_group': w_group, 'b_group': b_group, 'w_router': w_router, 'b_router': b_router,
            'w1': w1, 'w3': w3, 'w2': w2, 'ln2_g': ln2_g, 'ln2_b': ln2_b}

def second_block(x, positions, w_in, hg_lb_logits, hg_norm_g, ret_norm_g, w_branch_hg, w_branch_ret,
              w_out, ln1_g, ln1_b, w_group, b_group, w_router, b_router, w1, w3, w2, ln2_g, ln2_b):
    lb_cum = jnp.cumsum(jax.nn.softmax(hg_lb_logits.astype(jnp.float32), axis=0), axis=0)
    for layer in range(DEPTH):
        lb = lb_cum[layer + 1] - lb_cum[0]
        mix = _token_mixer(x, positions, w_in[layer], lb, hg_norm_g[layer], ret_norm_g[layer],
                           w_branch_hg[layer], w_branch_ret[layer], w_out[layer])
        x = _layer_norm(DEEPNORM_ALPHA * x + mix, ln1_g[layer], ln1_b[layer])
        moe = _hier_moe(x.reshape(-1, D_MODEL), w_group[layer], b_group[layer], w_router[layer],
                        b_router[layer], w1[layer], w3[layer], w2[layer]).reshape(x.shape)
        x = _layer_norm(DEEPNORM_ALPHA * x + moe, ln2_g[layer], ln2_b[layer])
    return x


_first_inputs = second_inputs


def second_inputs(seed=0):
    import zlib

    import numpy as np

    out = dict(_first_inputs(seed))
    spreads = {}
    factors = {'hg_lb_logits': 7.239,
     'hg_norm_g': 8.0,
     'ret_norm_g': 8.0,
     'b_group': 8.0,
     'b_router': 8.0,
     'ln2_g': 2.912,
     'ln2_b': 2.842}
    for name, (base, spread) in spreads.items():
        noise = np.random.default_rng([zlib.crc32(name.encode()), seed]).standard_normal(out[name].shape)
        drawn = base * np.exp(spread * noise) if base else spread * noise
        out[name] = __import__('jax').numpy.asarray(drawn.astype(out[name].dtype))
    for name, factor in factors.items():
        out[name] = (out[name] * factor).astype(out[name].dtype)
    return out


_narrow_inputs = second_inputs


def second_inputs(seed=0):

    out = dict(_narrow_inputs(seed))
    wider = {'hg_norm_g': 4.96, 'ret_norm_g': 3.95, 'ln2_g': 3.27, 'ln2_b': 3.28}
    for name, times in wider.items():
        mean = out[name].mean()
        out[name] = (mean + times * (out[name] - mean)).astype(out[name].dtype)
    return out


def setup_inputs(seed=0):
    out = dict(first_inputs(seed))
    for name, value in second_inputs(seed + 1).items():
        if name != "x":
            out[name + "_2"] = value
    return out


def reference(
    x, g_attn_norm, w_in, rel_bias, g_q_latent, w_q_up, g_kv_latent, w_kv_up, g_out_a, g_out_b,
    w_out, g_ffn_norm, w_router_group, b_router_group, w_router_expert, b_router_expert, w_gate,
    w_up, w_down, g_final, positions_2, w_in_2, hg_lb_logits_2, hg_norm_g_2, ret_norm_g_2,
    w_branch_hg_2, w_branch_ret_2, w_out_2, ln1_g_2, ln1_b_2, w_group_2, b_group_2, w_router_2,
    b_router_2, w1_2, w3_2, w2_2, ln2_g_2, ln2_b_2,
):
    x = first_block(
        x, g_attn_norm, w_in, rel_bias, g_q_latent, w_q_up, g_kv_latent, w_kv_up, g_out_a,
        g_out_b, w_out, g_ffn_norm, w_router_group, b_router_group, w_router_expert,
        b_router_expert, w_gate, w_up, w_down, g_final,
    )
    return second_block(
        x, positions_2, w_in_2, hg_lb_logits_2, hg_norm_g_2, ret_norm_g_2, w_branch_hg_2,
        w_branch_ret_2, w_out_2, ln1_g_2, ln1_b_2, w_group_2, b_group_2, w_router_2, b_router_2,
        w1_2, w3_2, w2_2, ln2_g_2, ln2_b_2,
    )


_drawn_inputs = setup_inputs


def setup_inputs(seed=0):
    import zlib

    import numpy as np

    out = dict(_drawn_inputs(seed))
    spreads = {}
    factors = {'b_router_group': 4.236, 'b_router_expert': 5.145, 'b_group_2': 3.414}
    for name, (base, spread) in spreads.items():
        noise = np.random.default_rng([zlib.crc32(name.encode()), seed]).standard_normal(out[name].shape)
        drawn = base * np.exp(spread * noise) if base else spread * noise
        out[name] = __import__('jax').numpy.asarray(drawn.astype(out[name].dtype))
    for name, factor in factors.items():
        out[name] = (out[name] * factor).astype(out[name].dtype)
    return out
```

```python
from contextlib import ExitStack

import numpy as np
import concourse.bass as bass
from concourse import mybir

F32 = mybir.dt.float32
I32 = mybir.dt.int32
ALU = mybir.AluOpType
ACT = mybir.ActivationFunctionType
AX_X = mybir.AxisListType.X

P = 128
SEQ = 512
NT = SEQ // P
D = 1024
KD = D // P
EPS = 1e-6
LN_EPS = 1e-5
HUGE = 3.0e38
NEG = -1.0e30

A_HEADS, A_DIM = 8, 64
A_WIDTH = A_HEADS * A_DIM
PATTERNS = ((128, 1), (512, 4), (2048, 16))
REL_BUCKETS, REL_MAX = 32, 1024
B_HEADS, Q_LORA, KV_LORA, NOPE, ROPE, V_DIM = 8, 256, 128, 64, 32, 64
C_WIDTH = Q_LORA + KV_LORA + ROPE
PAIRS = A_HEADS // 2

G_HEADS = 8
LEVELS = 7
R_HEADS, R_DIM = 4, 256
ALPHA = 2.0 ** 0.25
HG_COLS = (0, D, 2 * D, 4 * D, 3 * D)
R_COLS = (5 * D, 6 * D, 8 * D, 7 * D)
M_COLS = (9 * D, 10 * D)
TWO_PI = (6.28125, 1.9350051879882812e-3, 3.0199159819567e-7)
ROUND = 12582912.0
PI_BELOW = 3.1415925

GROUPS, PER_GROUP = 4, 8
EXPERTS = GROUPS * PER_GROUP
LOGITS = GROUPS + EXPERTS
SLOTS = 64
BLOCKS_PER_EXPERT = SEQ // SLOTS
SPARE = 2 * SEQ // (SLOTS + 1)
ROWS = (EXPERTS + SPARE) * SLOTS
STEPS = 2 * NT
TOEP = SEQ + SEQ - P


class Count:

    def __init__(self, sem):
        self.sem, self.base, self.n = sem, 0, 0

    def up(self, k=1):
        self.n += k
        return self.sem, k

    def now(self):
        return self.sem, self.base + self.n

    def loop(self, i, per_turn):
        self.start, self.per_turn = self.base + self.n, per_turn
        self.base, self.n = i * per_turn + self.start, 0

    def loop_end(self, turns):
        assert self.n == self.per_turn, (self.n, self.per_turn)
        self.base, self.n = 0, self.start + turns * self.per_turn



def bucket_table():
    rel = (SEQ - 1) - np.arange(2 * SEQ)
    half, exact = REL_BUCKETS // 2, REL_BUCKETS // 4
    n = np.abs(rel)
    large = exact + (np.log(np.maximum(n, 1) / exact) / np.log(REL_MAX / exact) * (half - exact)).astype(np.int32)
    bucket = np.where(rel > 0, half, 0) + np.where(n < exact, n, np.minimum(large, half - 1))
    reach = sum(((rel % d == 0) & (n <= w // 2)).astype(np.float64) for w, d in PATTERNS)
    out = np.zeros((REL_BUCKETS + 1, 2 * SEQ), np.float32)
    out[bucket, np.arange(2 * SEQ)] = 1.0
    out[REL_BUCKETS] = np.where(reach > 0, np.log(np.maximum(reach, 1)), NEG)
    return out


def rope_tables():
    half = ROPE // 2
    inv = (10000.0 ** (-(np.arange(half) / half))).astype(np.float32)
    ang = (np.arange(SEQ, dtype=np.float32)[:, None] * inv).astype(np.float64)
    cos, sin = np.cos(ang).astype(np.float32), np.sin(ang).astype(np.float32)
    q = np.zeros((P, SEQ), np.float32)
    q[64:80], q[80:96], q[96:112], q[112:128] = cos.T, cos.T, -sin.T, sin.T
    k = np.stack([cos, sin], 1).reshape(NT, P, 2, half).transpose(1, 0, 2, 3)
    return q, np.ascontiguousarray(k)


def route_rows():
    e = np.arange(EXPERTS)
    row = np.concatenate([EXPERTS - e, GROUPS - np.arange(GROUPS), e * SLOTS,
                          np.arange(1, BLOCKS_PER_EXPERT) * SLOTS, np.arange(SPARE)]).astype(np.float32)
    return np.broadcast_to(row, (P, row.size)).copy()


def level_masks():
    x = np.arange(P)
    out = np.zeros((P, LEVELS, P), np.int32)
    for n in range(LEVELS):
        b = 1 << n
        out[:, n] = (x[:, None] // (2 * b) == x // (2 * b)) & (x[:, None] // b != x // b)
    return out


def retention_decay():
    away = np.abs(np.arange(TOEP) - (SEQ - P) - np.arange(P)[:, None])
    gamma = 1.0 - 2.0 ** (-5.0 - np.arange(R_HEADS))
    d = gamma[:, None, None] ** away * np.where(away == 0, 2.0, 1.0) * R_DIM ** -0.5
    return d.astype(np.float32)


def rotary_rates():
    rate = np.float32(1.0) / (np.float32(10000.0) ** np.linspace(0.0, 1.0, R_DIM // 2).astype(np.float32))
    return rate.astype(np.float32).reshape(P, 1)


def constants():
    rope_q, rope_k = rope_tables()
    return {
        "c_before": np.triu(np.ones((P, P), np.float32), 1),
        "c_route": route_rows(),
        "c_token": np.arange(SEQ, dtype=np.int32).reshape(NT, P).T.copy(),
        "c_masks": level_masks(),
        "c_decay": retention_decay(),
        "c_rates": rotary_rates(),
        "c_ident": np.eye(P, dtype=np.float32),
        "c_bucket": bucket_table(),
        "c_rope_q": rope_q,
        "c_rope_k": rope_k,
    }


def build(nc, A, out, stop="all"):
    ctx = ExitStack()
    with ctx:
        def sb(name, shape, dt=F32):
            return ctx.enter_context(nc.sbuf_tensor(name, shape, dt))

        def sem(name):
            return ctx.enter_context(nc.semaphore(name))

        bank = [ctx.enter_context(nc.psum_tensor(f"bank{b}", [P, 512], F32)) for b in range(8)]
        table_dram = nc.dram_tensor("bias_table_dram", (A_HEADS, 2 * SEQ), F32, kind="Internal").ap()

        ident = sb("ident", [P, P])
        xres = sb("xres", [P, NT, D])
        hT = sb("hT", [P, KD, SEQ])
        gains = sb("gains", [P, 3, KD])
        stat = sb("stat", [P, 64])
        stream = sb("stream", [P, 96 * 256])
        work = sb("work", [P, 19 * 1024])

        w_pair = stream[:, 0:KD * 3 * P].rearrange("p (k c n) -> p k c n", k=KD, c=3)
        w_c = stream[:, 3072:3072 + KD * C_WIDTH].rearrange("p (k n) -> p k n", k=KD)
        w_up_q = stream[:, 6400:6400 + 2 * 2 * P].rearrange("p (c j m) -> p c j m", c=2, j=2)
        w_up_k = stream[:, 6912:6912 + 2 * NOPE].rearrange("p (j m) -> p j m", j=2)
        w_up_v = stream[:, 7168:7168 + B_HEADS * V_DIM]
        w_o = stream[:, 8192:8192 + KD * D].rearrange("p (k n) -> p k n", k=KD)

        def cut(start, *shape):
            n = int(np.prod(shape))
            ap = work[:, start:start + n]
            if len(shape) == 1:
                return ap, start + n
            letters = "abcd"[:len(shape)]
            spec = f"p ({' '.join(letters)}) -> p {' '.join(letters)}"
            return ap.rearrange(spec, **{l: s for l, s in zip(letters, shape)}), start + n

        at = 0
        outAB, at = cut(at, NT, D)
        ctok, _ = cut(at, NT, C_WIDTH)
        toep, at = cut(at, 2, TOEP)
        qT, at = cut(at, 2, SEQ)
        kT, at = cut(at, 2, SEQ)
        v, at = cut(at, NT, A_WIDTH)
        xn_at = at
        sc, at = cut(at, 2, SEQ)
        prob, at = cut(at, 2, SEQ)
        probT, at = cut(at, 2, NT, P)
        cn, at = cut(at, NT, Q_LORA + KV_LORA + 96)
        cqT, at = cut(at, 3, SEQ)
        zeros, at = cut(at, SEQ)
        rope_q, at = cut(at, SEQ)
        rope_k, at = cut(at, NT, 2, ROPE // 2)
        rope_t, at = cut(at, NT, 4, ROPE // 2)
        rsum = sb("rsum", [P, 8])
        rinv = sb("rinv", [P, 8])
        held = sb("held", [P, STEPS])
        nmax = sb("nmax", [P, 8])
        xn = work[:, xn_at:xn_at + 2 * D].rearrange("p (a d) -> p a d", a=2)
        rope_s, at = cut(at, 2, SEQ)
        gains_c = sb("gains_c", [P, 3])
        v_pair = v[:, :, 0:P]

        def v_mla(pair, j, kc):
            return v[:, kc, bass.ds(pair * P + j * V_DIM, V_DIM)]

        def toep_tile(j, i):
            ap = toep[:, j, i * P:i * P + SEQ]
            return bass.AP(ap.tensor, ap.offset + SEQ - 1, [list(ap.ap[0]), [-1, SEQ]])

        onehot = work[0:REL_BUCKETS + 1, 0:2 * SEQ]
        table = work[0:A_HEADS, 2 * SEQ:4 * SEQ]
        relb = work[0:REL_BUCKETS + 1, 4 * SEQ:4 * SEQ + A_HEADS]
        junk = probT[:, :, :, :].rearrange("p a b c -> p (a b c)")

        ones = sb("ones", [P, P])
        before = stream[:, 22528:22656]
        route = stream[:, 22656:22656 + 121 + 1][:, 0:LOGITS + EXPERTS + BLOCKS_PER_EXPERT - 1 + SPARE]
        token = sb("token", [P, NT], I32)
        w_r1 = stream[:, 22784:22784 + KD * LOGITS].rearrange("p (k n) -> p k n", k=KD)
        b_r1 = stream[:, 23072:23072 + LOGITS]
        g_row = stream[:, 23552:24576]

        x_out = [sem(f"x_out{i}") for i in range(NT)]
        (r_in, lg_done, exp_in, exp_out, picked, rank_done, routed, list_zero, zero_ready, listed, list_in, rows_out, yg_in,
         cleared, passed, stored, mixed) = (sem(n) for n in (
            "r_in lg_done exp_in exp_out picked rank_done routed list_zero zero_ready listed list_in rows_out yg_in cleared"
            " passed stored mixed").split())
        masks = sb("masks", [P, LEVELS, P], mybir.dt.uint8)
        masks_wide = hT[:, 0:2, :].rearrange("p a b -> p (a b)")[:, 0:LEVELS * P].bitcast(I32)
        head_row = sb("head_row", [P, 6, G_HEADS])

        oTh, at = cut(0, G_HEADS, SEQ)
        oTr, at = cut(at, 2 * R_HEADS, SEQ)
        stage_at = at
        x_at = at
        X, at = cut(at, 4, SEQ)
        t_at = at
        T, at = cut(at, 2, SEQ)
        ksum, at = cut(at, SEQ)
        Q, at = cut(at, SEQ)
        F, at = cut(at, 2, SEQ)
        sig, at = cut(at, SEQ)
        sqr, at = cut(at, SEQ)
        root, at = cut(at, SEQ)
        gate, at = cut(at, SEQ)
        V, at = cut(at, NT, P)
        attn_at = at
        attnT, at = cut(at, NT, SEQ)
        assert at <= 19 * 1024
        rq, at = cut(stage_at, 2, SEQ)
        rk, at = cut(at, 2, SEQ)
        rV, at = cut(at, NT, R_DIM)
        rgate, at = cut(at, 2, SEQ)
        decay, at = cut(at, TOEP)
        cosr, at = cut(at, SEQ)
        sinr, at = cut(at, SEQ)
        rtmp, at = cut(at, 2, SEQ)
        rsq, at = cut(at, 2, SEQ)
        rroot, at = cut(at, SEQ)
        rattn, at = cut(at, NT, SEQ)
        assert at <= 19 * 1024
        merged, at = cut(stage_at, KD, SEQ)
        msig, at = cut(at, 2, 2, SEQ)
        mtmp, at = cut(at, 2, 2, SEQ)
        w_hg = stream[:, 6144:6144 + 5 * D].rearrange("p (c k n) -> p c k n", c=5, k=KD)
        w_ret = stream[:, 11264:11264 + 8 * D].rearrange("p (c k n) -> p c k n", c=4, k=KD)
        w_mrg = stream[:, 0:8 * D].rearrange("p (s c k n) -> p s c k n", s=2, c=4, k=KD)
        w_o2 = stream[:, 8192:8192 + 8 * D].rearrange("p (k n) -> p k n", k=KD)
        ln_row = [g_row, stream[:, 19456:20480]]
        bn = sb("bn", [P, NT, 2, 6])
        mv = sb("mv", [P, NT, 2])
        rates = sb("rates", [P, 1])

        lb_in, h_copy, r_tmp = sem("lb_in"), sem("h_copy"), sem("r_tmp")
        hg_in = [sem(f"hg_in{c}") for c in range(5)]
        lb_ready = sem("lb_ready")
        (hp_done, h_sig, h_F, h_V, h_q, h_gate, h_init, l_done, h_upd, h_base, h_far, h_av, h_sq, h_nm, h_var,
         h_root, h_fin) = (sem(n) for n in ("hp_done h_sig h_F h_V h_q h_gate h_init l_done h_upd h_base h_far h_av"
                                            " h_sq h_nm h_var h_root h_fin").split())
        ret_in = [sem(f"ret_in{c}") for c in range(4)]
        (decay_in, pos_in, ang_ready, rot_ready, rp_done, rr_q, rr_k, r_sig, r_gate, r_V, rs_done, r_dec, r_av, r_sq, r_nm,
         r_var, r_root, r_fin) = (sem(n) for n in ("decay_in pos_in ang_ready rot_ready rp_done rr_q rr_k r_sig r_gate r_V"
                                  " rs_done r_dec r_av r_sq r_nm r_var r_root r_fin").split())
        mrg_in = [sem("mrg_in0"), sem("mrg_in1")]
        w_o2_in, ln_in, ln2_in, m_done, m_sig, m_ready, ln_ready = (
            sem(n) for n in "w_o2_in ln_in ln2_in m_done m_sig m_ready ln_ready".split())
        zeros_ready = sem("zeros_ready")
        route_in, g_row_in, ones_ready, fin_ready = sem("route_in"), sem("g_row_in"), sem("ones_ready"), sem("fin_ready")
        x_in = [sem(f"x_in{i}") for i in range(NT)]
        gains_in, rope_in = sem("gains_in"), sem("rope_in")
        bias_in, table_out, toep_in = sem("bias_in"), sem("table_out"), sem("toep_in")
        w_pair_in, w_c_in, w_up_in, w_o_in = (sem(n) for n in ("w_pair_in", "w_c_in", "w_up_in", "w_o_in"))
        dve_own, act_own = Count(sem("dve_own")), Count(sem("act_own"))
        ones_row, table_mm, table_ready = sem("ones_row"), sem("table_mm"), sem("table_ready")
        sq_ready, normed, tr_done, hT_ready = (sem(n) for n in ("sq_ready", "normed", "tr_done", "hT_ready"))
        var_ready, root_ready = sem("var_ready"), sem("root_ready")
        proj_done, q_ready, k_ready, v_ready = (sem(n) for n in ("proj_done", "q_ready", "k_ready", "v_ready"))
        s_done, biased, exp_done, pT_done, pT_ready, av_done, o_ready = (
            sem(n) for n in ("s_done", "biased", "exp_done", "pT_done", "pT_ready", "av_done", "o_ready"))
        c_done, c_ready, cn_ready, ct_done, ct_ready = (
            sem(n) for n in ("c_done", "c_ready", "cn_ready", "ct_done", "ct_ready"))
        rope_done, q_roped = sem("rope_done"), sem("q_roped")
        up_done, vb_done, vb_ready = sem("up_done"), sem("vb_done"), sem("vb_ready")
        wo_done, x1_ready, final_out = sem("wo_done"), sem("x1_ready"), sem("final_out")

        block = ctx.enter_context(nc.Block())


        def core_pe(pe, pair, done, keys, inputs):
            lhs, rhs, vcols = keys
            for m in range(STEPS + 3):
                if m < STEPS:
                    j, i = divmod(m, NT)
                    base = pair * STEPS + done
                    if m == 0:
                        inputs()
                    if m >= 2:
                        pe.wait_ge(biased, base + m - 1)
                    pe.matmul(bank[m % 2][:, :], lhs(j, i), rhs(j), start=True, stop=True).then_inc(s_done, 1)
                n = m - 2
                if 0 <= n < STEPS:
                    pe.wait_ge(exp_done, base + n + 1)
                    if n >= 2:
                        pe.wait_ge(pT_ready, base + n - 1)
                    for kc in range(NT):
                        last = pe.transpose(bank[2 + n % 2][:, kc * P:(kc + 1) * P],
                                            prob[:, n % 2, kc * P:(kc + 1) * P], ident[:, :])
                    last.then_inc(pT_done, 1)
                n = m - 3
                if 0 <= n < STEPS:
                    pe.wait_ge(pT_ready, base + n + 1)
                    if n >= 2:
                        pe.wait_ge(o_ready, base + n - 1)
                    for kc in range(NT):
                        last = pe.matmul(bank[4 + n % 2][:, 0:A_DIM], probT[:, n % 2, kc, :], vcols(n // NT, kc),
                                         start=kc == 0, stop=kc == NT - 1)
                    last.then_inc(av_done, 1)

        def core_dve(dve, pair, done, bias, scale):
            base = pair * STEPS + done
            for m in range(STEPS + 2):
                if m < STEPS:
                    dve.wait_ge(s_done, base + m + 1)
                    if m >= 2:
                        dve.wait_ge(exp_done, base + m - 1)
                    dve.memset(held[:, m:m + 1], 0.0)
                    dve.tensor_tensor_reduce(sc[:, m % 2, :], bank[m % 2][:, :], bias(m // NT, m % NT),
                                             -scale, HUGE, ALU.add, ALU.min,
                                             nmax[:, m:m + 1]).then_inc(biased, 1)
                n = m - 2
                if 0 <= n < STEPS:
                    dve.wait_ge(exp_done, base + n + 1)
                    dve.reciprocal(rinv[:, n:n + 1], rsum[:, n:n + 1])
                    dve.wait_ge(pT_done, base + n + 1)
                    if n >= 2:
                        dve.wait_ge(av_done, base + n - 1)
                    dve.tensor_copy(probT[:, n % 2, :, :],
                                    bank[2 + n % 2][:, :].rearrange("p (a b) -> p a b", a=NT)).then_inc(pT_ready, 1)

        def core_act(act, pair, done, col):
            base = pair * STEPS + done
            for m in range(STEPS + 2):
                if m < STEPS:
                    act.wait_ge(biased, base + m + 1)
                    if m >= 2:
                        act.wait_ge(pT_done, base + m - 1)
                    act.activation(prob[:, m % 2, :], sc[:, m % 2, :], ACT.Exp, bias=nmax[:, m:m + 1], scale=-1.0,
                                   accum_out=rsum[:, m:m + 1]).then_inc(exp_done, 1)
                n = m - 2
                if 0 <= n < STEPS:
                    act.wait_ge(av_done, base + n + 1)
                    act.wait_ge(pT_ready, base + n + 1)
                    act.activation(outAB[:, n % NT, bass.ds(col + (n // NT) * A_DIM, A_DIM)], bank[4 + n % 2][:, 0:A_DIM],
                                   ACT.Copy, scale=rinv[:, n:n + 1]).then_inc(o_ready, 1)


        def norm_act(act, r, src, groups, waits, junk=junk):
            w = D // groups
            for i in range(NT):
                waits(act, i)
                for g in range(groups):
                    act.activation(junk[:, 0:w], src(i)[:, g * w:(g + 1) * w], ACT.Square,
                                   accum_out=stat[:, i * groups + g:i * groups + g + 1]).then_inc(*act_own.up())
                    act.wait_ge(*act_own.now())
            act.sem_inc(sq_ready, 1)
            root_act(act, r, NT * groups)

        def root_act(act, s, cols):
            act.wait_ge(var_ready, s + 1)
            act.activation(stat[:, 0:cols], stat[:, 0:cols], ACT.Sqrt).then_inc(root_ready, 1)

        def root_dve(dve, s, cols, w, eps):
            dve.wait_ge(sq_ready, s + 1)
            dve.tensor_scalar(stat[:, 0:cols], stat[:, 0:cols], 1.0 / w, eps, ALU.mult, ALU.add).then_inc(var_ready, 1)
            dve.wait_ge(root_ready, s + 1)
            dve.reciprocal(stat[:, 0:cols], stat[:, 0:cols]).then_inc(*dve_own.up())
            dve.wait_ge(*dve_own.now())

        def norm_dve(dve, s, r, src, groups, gain, free=lambda i: None):
            w = D // groups
            root_dve(dve, r, NT * groups, w, EPS)
            for i in range(NT):
                if i >= 2:
                    dve.wait_ge(tr_done, (s * NT + i - 2) * 2 + 2)
                    free(i)
                for g in range(groups):
                    last = dve.tensor_scalar(xn[:, i % 2, g * w:(g + 1) * w], src(i)[:, g * w:(g + 1) * w],
                                             stat[:, i * groups + g:i * groups + g + 1], None, ALU.mult)
                last.then_inc(normed, 1)
                if i >= 1:
                    fold_dve(dve, s, i - 1, gain)
            fold_dve(dve, s, NT - 1, gain)

        def fold_dve(dve, s, i, gain):
            for h in range(2):
                dve.wait_ge(tr_done, (s * NT + i) * 2 + h + 1)
                src = bank[4 + (i % 2) * 2 + h][:, :].rearrange("p (a b) -> p a b", a=NT)
                dst = hT[:, 4 * h:4 * h + 4, i * P:(i + 1) * P]
                if gain is None:
                    dve.tensor_copy(dst, src).then_inc(hT_ready, 1)
                else:
                    dve.tensor_tensor(dst, src, gain[:, 4 * h:4 * h + 4].unsqueeze(2).to_broadcast([P, 4, P]),
                                      ALU.mult).then_inc(hT_ready, 1)

        def norm_pe(pe, s, src, waits):
            for i in range(NT):
                waits(pe, i)
                for h in range(2):
                    if i >= 2:
                        pe.wait_ge(hT_ready, (s * NT + i - 2) * 2 + h + 1)
                    for k in range(4):
                        last = pe.transpose(bank[4 + (i % 2) * 2 + h][:, k * P:(k + 1) * P],
                                            src(i)[:, 4 * h + k:D:KD], ident[:, :])
                    last.then_inc(tr_done, 1)

        def xn_ready(s):
            return lambda pe, i: pe.wait_ge(normed, s * NT + i + 1)


        class Moe:

            def __init__(m, layer, ff, weights, slot_at, smalls, pool_at):
                m.layer, m.ff, m.fc = layer, ff, ff // P
                m.w_gate, m.w_up, m.w_down = (A[w] for w in weights)
                size = 3 * KD * ff
                m.wg = [stream[:, a:a + KD * ff].rearrange("p (k f) -> p k f", k=KD) for a in slot_at]
                m.wu = [stream[:, a + KD * ff:a + 2 * KD * ff].rearrange("p (k f) -> p k f", k=KD) for a in slot_at]
                m.wd = [stream[:, a + 2 * KD * ff:a + size].rearrange("p (c n) -> p c n", c=m.fc) for a in slot_at]
                m.w_r, m.b_r = smalls
                at = pool_at
                m.xg, at = cut(at, 2, D)
                m.xgT, at = cut(at, 2, KD, SLOTS)
                m.sg, at = cut(at, 2, SLOTS)
                m.h, at = cut(at, 2, m.fc, SLOTS)
                m.y, at = cut(at, 2, D)
                m.yg, at = cut(at, 2 * NT, D)
                m.lg, at = cut(at, NT, LOGITS)
                m.a1, at = cut(at, NT, EXPERTS)
                m.a2, at = cut(at, NT, EXPERTS)
                m.aa, at = cut(at, NT, EXPERTS)
                m.me, at = cut(at, NT, EXPERTS)
                m.t1, at = cut(at, NT, EXPERTS)
                m.goh, at = cut(at, NT, GROUPS)
                m.gt, at = cut(at, NT, GROUPS)
                m.ex, at = cut(at, NT, 5)
                m.mx, at = cut(at, 8, NT)
                m.gate, at = cut(at, 2, NT)
                m.cnt, at = cut(at, EXPERTS)
                m.nov, at = cut(at, EXPERTS)
                m.ove, at = cut(at, EXPERTS)
                m.dif, at = cut(at, EXPERTS)
                m.cmp, at = cut(at, EXPERTS, BLOCKS_PER_EXPERT - 1)
                m.cmb, at = cut(at, SPARE, EXPERTS)
                m.dest, at = cut(at, 2, NT)
                m.blk, at = cut(at, SPARE + 1)
                m.one, at = cut(at, EXPERTS)
                m.dest_i, at = cut(at, 2 * NT)
                m.blk_i, at = cut(at, SPARE + 1)
                m.list_i, at = cut(at, EXPERTS + SPARE)
                m.zero_i, at = cut(at, SLOTS)
                m.rows, at = cut(at, 2, D)
                assert at <= 19 * 1024, at
                m.dest_i, m.blk_i, m.list_i, m.zero_i = (x.bitcast(I32) for x in (m.dest_i, m.blk_i, m.list_i, m.zero_i))
                m.x_dram = nc.dram_tensor(f"x_rows{layer}", (SEQ, D), F32, kind="Internal").ap()
                m.y_dram = nc.dram_tensor(f"y_rows{layer}", (ROWS, D), F32, kind="Internal").ap()
                m.list_dram = nc.dram_tensor(f"token_list{layer}", (ROWS, 1), I32, kind="Internal").ap()
                (m.xt_done, m.xt_ready, m.gu_done, m.sg_ready, m.h_ready, m.d_done, m.y_ready) = (
                    sem(f"{n}_{layer}") for n in "xt_done xt_ready gu_done sg_ready h_ready d_done y_ready".split())
                m.xg_in, m.w_in, m.y_out = ([sem(f"{n}{i}_{layer}") for i in range(2)] for n in ("xg_in", "w_in", "y_out"))
                m.past = layer - 1

        moe1 = Moe(1, 256, ("w_gate", "w_up", "w_down"), (16384, 0), (w_r1, b_r1), 0)
        moe1.gain = gains[:, 2, :]
        moe2 = Moe(2, 512, ("w1_2", "w3_2", "w2_2"), (0, 12288), (w_r1, b_r1), 0)
        moe2.gain = None
        r_key = route[:, 0:EXPERTS]
        r_gkey = route[:, EXPERTS:LOGITS]
        r_first = route[:, LOGITS:LOGITS + EXPERTS]
        r_limit = route[:, LOGITS + EXPERTS:LOGITS + EXPERTS + BLOCKS_PER_EXPERT - 1]
        r_block = route[:, LOGITS + EXPERTS + BLOCKS_PER_EXPERT - 1:]

        def route_pe(pe, m):
            pe.wait_ge(r_in, 48 * m.past + 48)
            for i in range(NT):
                for k in range(KD):
                    last = pe.matmul(bank[0][:, i * LOGITS:(i + 1) * LOGITS], hT[:, k, i * P:(i + 1) * P], m.w_r[:, k, :],
                                     start=k == 0, stop=k == KD - 1)
            last.then_inc(lg_done, 1)
            pe.wait_ge(picked, m.past + 1)
            for i in range(NT):
                for j in range(i + 1):
                    pe.matmul(bank[1][:, i * EXPERTS:(i + 1) * EXPERTS], before[:, :] if j == i else ones[:, :],
                              m.aa[:, j, :], start=j == 0, stop=j == i)
            for j in range(NT):
                last = pe.matmul(bank[1][:, NT * EXPERTS:(NT + 1) * EXPERTS], ones[:, :], m.aa[:, j, :], start=j == 0,
                                 stop=j == NT - 1)
            last.then_inc(rank_done, 1)

        def route_act(act, m):
            act.wait_ge(exp_in, m.past + 1)
            act.activation(m.ex[:, :, :], m.ex[:, :, :], ACT.Exp).then_inc(exp_out, 1)

        def route_dve(dve, m):
            def step(ins):
                ins.then_inc(*dve_own.up())
                dve.wait_ge(*dve_own.now())

            def over(x, n):
                return x.unsqueeze(2).to_broadcast([P, NT, n])

            def rows(r, n):
                return r.unsqueeze(1).to_broadcast([P, NT, n])

            def first_of_equals(out, x, top, key, n, tmp):
                step(dve.tensor_reduce(top, x, AX_X, ALU.max))
                step(dve.tensor_tensor(tmp, x, over(top, n), ALU.is_equal))
                step(dve.tensor_tensor(tmp, tmp, rows(key, n), ALU.mult))
                step(dve.tensor_reduce(m.mx[:, 7, :], tmp, AX_X, ALU.max))
                step(dve.tensor_tensor(out, rows(key, n), over(m.mx[:, 7, :], n), ALU.is_equal))

            gl, el = m.lg[:, :, 0:GROUPS], m.lg[:, :, GROUPS:]
            dve.wait_ge(lg_done, m.past + 1)
            dve.wait_ge(r_in, 48 * m.past + 48)
            step(dve.tensor_tensor(m.lg[:, :, :], bank[0][:, 0:NT * LOGITS].rearrange("p (a b) -> p a b", a=NT),
                                   rows(m.b_r, LOGITS), ALU.add))
            first_of_equals(m.goh, gl, m.mx[:, 0, :], r_gkey, GROUPS, m.gt)
            step(dve.tensor_tensor(m.ex[:, :, 0:GROUPS], gl, over(m.mx[:, 0, :], GROUPS), ALU.subtract))
            step(dve.tensor_scalar(m.gt, m.goh, -NEG, NEG, ALU.mult, ALU.add))
            four = lambda x: x.rearrange("p a (g e) -> p a g e", g=GROUPS)
            wide = lambda x: x.unsqueeze(3).to_broadcast([P, NT, GROUPS, PER_GROUP])
            step(dve.tensor_tensor(four(m.me), four(el), wide(m.goh), ALU.mult))
            step(dve.tensor_tensor(four(m.me), four(m.me), wide(m.gt), ALU.add))
            first_of_equals(m.a1, m.me, m.mx[:, 1, :], r_key, EXPERTS, m.t1)
            step(dve.tensor_scalar(m.t1, m.a1, 2 * NEG, None, ALU.mult))
            step(dve.tensor_tensor(m.me, m.me, m.t1, ALU.add))
            first_of_equals(m.a2, m.me, m.mx[:, 2, :], r_key, EXPERTS, m.t1)
            dve.tensor_tensor(m.aa, m.a1, m.a2, ALU.add).then_inc(picked, 1)
            dve.tensor_tensor(m.ex[:, :, GROUPS], m.mx[:, 2, :], m.mx[:, 1, :], ALU.subtract).then_inc(exp_in, 1)
            dve.wait_ge(exp_out, m.past + 1)
            step(dve.tensor_reduce(m.mx[:, 3, :], m.ex[:, :, 0:GROUPS], AX_X, ALU.add))
            step(dve.tensor_scalar(m.mx[:, 4, :], m.ex[:, :, GROUPS], 1.0, None, ALU.add))
            step(dve.tensor_tensor(m.mx[:, 3, :], m.mx[:, 3, :], m.mx[:, 4, :], ALU.mult))
            step(dve.reciprocal(m.gate[:, 0, :], m.mx[:, 3, :]))
            step(dve.tensor_tensor(m.gate[:, 1, :], m.gate[:, 0, :], m.ex[:, :, GROUPS], ALU.mult))
            dve.wait_ge(rank_done, m.past + 1)
            rank = bank[1][:, 0:NT * EXPERTS].rearrange("p (a b) -> p a b", a=NT)
            step(dve.tensor_copy(m.cnt, bank[1][:, NT * EXPERTS:(NT + 1) * EXPERTS]))
            lim = BLOCKS_PER_EXPERT - 1
            step(dve.tensor_tensor(m.cmp, m.cnt.unsqueeze(2).to_broadcast([P, EXPERTS, lim]),
                                   r_limit.unsqueeze(1).to_broadcast([P, EXPERTS, lim]), ALU.is_gt))
            step(dve.tensor_reduce(m.nov, m.cmp, AX_X, ALU.add))
            step(dve.memset(m.one, 1.0))
            step(dve.tensor_tensor_scan(m.ove, m.one, m.nov, 0.0, ALU.mult, ALU.add))
            step(dve.tensor_tensor(m.cmb, m.ove.unsqueeze(1).to_broadcast([P, SPARE, EXPERTS]),
                                   r_block.unsqueeze(2).to_broadcast([P, SPARE, EXPERTS]), ALU.is_le))
            step(dve.tensor_reduce(m.blk[:, 0:SPARE], m.cmb, AX_X, ALU.add))
            step(dve.tensor_scalar(m.blk[:, 0:SPARE], m.blk[:, 0:SPARE], EXPERTS - 1.0, None, ALU.min))
            step(dve.tensor_copy(m.blk[:, SPARE:SPARE + 1], m.ove[:, EXPERTS - 1:EXPERTS]))
            step(dve.tensor_copy(m.blk_i, m.blk))
            step(dve.tensor_tensor(m.dif, m.ove, m.nov, ALU.subtract))
            step(dve.tensor_scalar(m.dif, m.dif, float(SLOTS), float((EXPERTS - 1) * SLOTS), ALU.mult, ALU.add))
            step(dve.tensor_tensor(m.dif, m.dif, r_first, ALU.subtract))
            step(dve.tensor_scalar(m.t1, rank, float(SLOTS), None, ALU.is_ge))
            step(dve.tensor_tensor(m.t1, m.t1, rows(m.dif, EXPERTS), ALU.mult))
            step(dve.tensor_tensor(m.t1, m.t1, rank, ALU.add))
            step(dve.tensor_tensor(m.t1, m.t1, rows(r_first, EXPERTS), ALU.add))
            for c, a in enumerate((m.a1, m.a2)):
                step(dve.tensor_tensor(m.me, m.t1, a, ALU.mult))
                step(dve.tensor_reduce(m.dest[:, c, :], m.me, AX_X, ALU.add))
            dve.tensor_copy(m.dest_i, m.dest.rearrange("p a b -> p (a b)")).then_inc(routed, 1)

        def route_pool(pool, m):
            pool.wait_ge(routed, m.past + 1)
            pool.wait_ge(list_zero, 16 * m.past + 16)
            pool.wait_ge(route_in, 48)
            for c in range(2):
                for i in range(NT):
                    pool.indirect_dma_start(
                        out=m.list_dram, out_offset=bass.IndirectOffsetOnAxis(ap=m.dest_i[:, c * NT + i:c * NT + i + 1], axis=0),
                        in_=token[:, i:i + 1], in_offset=None).then_inc(listed, 16)

        def list_sp(sp, m):
            sp.wait_ge(zero_ready, m.past + 1)
            sp.dma_start(m.list_dram.rearrange("(e s) a -> e (s a)", s=SLOTS), m.zero_i[0:EXPERTS + SPARE, :]).then_inc(list_zero, 16)
            sp.wait_ge(listed, 32 * NT * (m.past + 1))
            sp.dma_start(m.list_i[0:SLOTS, :], m.list_dram.rearrange("(e s) a -> s (e a)", s=SLOTS),
                         allow_slow_non_contiguous=True).then_inc(list_in, 16)

        def clear_spare_rows(sp, m):
            rows = m.y_dram[EXPERTS * SLOTS:, :].rearrange("(p r) (a n) -> p (r a n)", p=P // 2, n=SEQ)
            sp.dma_start(rows.rearrange("p (r n) -> p r n", n=SEQ),
                         zeros[0:P // 2, :].unsqueeze(1).to_broadcast([P // 2, SPARE * SLOTS * D // SEQ * 2 // P, SEQ])
                         ).then_inc(cleared, 16)

        def load_expert(sp, m, e, s):
            wide = lambda w: w[bass.ds(e, 1)].rearrange("a (p k) f -> (a p) k f", k=KD)
            sp.dma_start(m.wg[s], wide(m.w_gate)).then_inc(m.w_in[s], 16)
            sp.dma_start(m.wu[s], wide(m.w_up)).then_inc(m.w_in[s], 16)
            sp.dma_start(m.wd[s], m.w_down[bass.ds(e, 1)].rearrange("a (p c) n -> (a p) c n", c=m.fc)).then_inc(m.w_in[s], 16)

        def turns(eng, body):
            for s in range(2):
                body(0, s, True, False)
            with eng.Fori(1, EXPERTS // 2 - 1) as i:
                for s in range(2):
                    body(i, s, False, False)
            for s in range(2):
                body(EXPERTS // 2 - 1, s, False, True)

        def spare(eng, m, body):
            eng.wait_ge(routed, m.past + 1)
            need = eng.value_load(m.blk_i[0:1, SPARE:SPARE + 1], min_val=0, max_val=SPARE)
            with eng.Fori(0, SPARE) as b:
                with eng.If(need > b):
                    body(b)

        def experts_sp(sp, m):
            def body(i, s, first, last):
                e = i * 2 + s
                sp.wait_ge(m.y_ready, e * 2 + 2)
                sp.dma_start(m.y_dram[bass.ds(e * SLOTS, SLOTS), :], m.y[0:SLOTS, s, :]).then_inc(m.y_out[s], 16)
                if not last:
                    load_expert(sp, m, e + 2, s)

            turns(sp, body)

            def further(b):
                e = sp.value_load(m.blk_i[0:1, bass.ds(b, 1)], min_val=0, max_val=EXPERTS - 1)
                load_expert(sp, m, e, 0)
                sp.wait_ge(m.y_ready, b * 2 + 2 * EXPERTS + 2)
                sp.dma_start(m.y_dram[bass.ds(b * SLOTS + EXPERTS * SLOTS, SLOTS), :], m.y[0:SLOTS, 0, :]).then_inc(m.y_out[0], 16)
                sp.wait_ge(m.y_out[0], b * 16 + 16 * EXPERTS // 2 + 16)
                sp.sem_inc(stored, 1)

            sp.wait_ge(cleared, 32)
            spare(sp, m, further)
            for s in range(2):
                sp.wait_ge(m.y_out[s], 16 * EXPERTS // 2)
            sp.sem_inc(rows_out, 1)

        def experts_pool(pool, m):
            pool.wait_ge(list_in, 16 * m.past + 16)
            for tile_out in x_out:
                pool.wait_ge(tile_out, 16 * m.past + 16)
            for n in range(EXPERTS):
                if n >= 2:
                    pool.wait_ge(m.xt_done, n - 1)
                pool.indirect_dma_start(
                    out=m.xg[0:SLOTS, n % 2, :], out_offset=None, in_=m.x_dram,
                    in_offset=bass.IndirectOffsetOnAxis(ap=m.list_i[0:SLOTS, n:n + 1], axis=0)).then_inc(m.xg_in[n % 2], 16)
            need = pool.value_load(m.blk_i[0:1, SPARE:SPARE + 1], min_val=0, max_val=SPARE)
            for b in range(SPARE):
                with pool.If(need > b):
                    pool.wait_ge(m.xt_done, EXPERTS + b)
                    pool.indirect_dma_start(
                        out=m.xg[0:SLOTS, 0, :], out_offset=None, in_=m.x_dram,
                        in_offset=bass.IndirectOffsetOnAxis(ap=m.list_i[0:SLOTS, EXPERTS + b:EXPERTS + b + 1],
                                                            axis=0)).then_inc(m.xg_in[0], 16)
            pool.wait_ge(rows_out, m.past + 1)
            for c in range(2):
                for i in range(NT):
                    pool.indirect_dma_start(
                        out=m.yg[:, c * NT + i, :], out_offset=None, in_=m.y_dram,
                        in_offset=bass.IndirectOffsetOnAxis(ap=m.dest_i[:, c * NT + i:c * NT + i + 1], axis=0)
                    ).then_inc(yg_in, 16)

        def tokens_pe(pe, m, s):
            for k in range(KD):
                last = pe.transpose(bank[s][:, k * SLOTS:(k + 1) * SLOTS], m.xg[0:SLOTS, s, k:D:KD], ident[0:SLOTS, 0:SLOTS])
            last.then_inc(m.xt_done, 1)

        def hidden_pe(pe, m, s, n, waited):
            for c in range(m.fc):
                if not (waited and c < 2):
                    pe.wait_ge(m.h_ready, n * m.fc + c - 1)
                for w, at in ((m.wg, 0), (m.wu, 256)):
                    for k in range(KD):
                        last = pe.matmul(bank[2 + c % 2][:, at:at + SLOTS], w[s][:, k, c::m.fc], m.xgT[:, s, k, :],
                                         start=k == 0, stop=k == KD - 1)
                last.then_inc(m.gu_done, 1)

        def down_pe(pe, m, s, n, waited):
            if not waited:
                pe.wait_ge(m.y_ready, n * 2)
            for c in range(m.fc):
                pe.wait_ge(m.h_ready, n * m.fc + c + 1)
                for half in range(2):
                    last = pe.matmul(bank[4 + half][0:SLOTS, :], m.h[:, s, c, :], m.wd[s][:, c, half * 512:(half + 1) * 512],
                                     start=c == 0, stop=c == m.fc - 1)
            last.then_inc(m.d_done, 1)

        def experts_pe(pe, m):
            pe.wait_ge(m.xg_in[0], 16)
            tokens_pe(pe, m, 0)

            def body(i, s, first, last):
                e = i * 2 + s
                if not (last and s == 1):
                    pe.wait_ge(m.xg_in[1 - s], (i + s) * 16 + 16)
                pe.wait_ge(m.xt_ready, e + 1)
                pe.wait_ge(m.w_in[s], i * 48 + 48)
                hidden_pe(pe, m, s, e, first and s == 0)
                if not (last and s == 1):
                    tokens_pe(pe, m, 1 - s)
                down_pe(pe, m, s, e, first and s == 0)

            turns(pe, body)

            def further(b):
                n = b + EXPERTS
                pe.wait_ge(m.xg_in[0], b * 16 + 16 * EXPERTS // 2 + 16)
                pe.sem_inc(passed, 1)
                tokens_pe(pe, m, 0)
                pe.wait_ge(m.xt_ready, n + 1)
                pe.wait_ge(m.w_in[0], b * 48 + 48 * EXPERTS // 2 + 48)
                hidden_pe(pe, m, 0, n, False)
                down_pe(pe, m, 0, n, False)

            spare(pe, m, further)

        def block_act(act, m, s, n, y_free, waited):
            for c in range(m.fc):
                act.wait_ge(m.gu_done, n * m.fc + c + 1)
                if not (waited and c < 2):
                    act.wait_ge(m.h_ready, n * m.fc + c - 1)
                act.activation(m.sg[:, c % 2, :], bank[2 + c % 2][:, 0:SLOTS], ACT.Silu).then_inc(m.sg_ready, 1)
            act.wait_ge(m.d_done, n + 1)
            y_free(act)
            act.activation(m.y[0:SLOTS, s, 0:512], bank[4][0:SLOTS, :], ACT.Copy).then_inc(m.y_ready, 1)

        def tokens_dve(dve, m, s, n):
            dve.wait_ge(m.xt_done, n + 1)
            src = bank[s][:, :].rearrange("p (k t) -> p k t", k=KD)
            if m.gain is None:
                dve.tensor_copy(m.xgT[:, s, :, :], src).then_inc(m.xt_ready, 1)
            else:
                dve.tensor_tensor(m.xgT[:, s, :, :], src, m.gain.unsqueeze(2).to_broadcast([P, KD, SLOTS]),
                                  ALU.mult).then_inc(m.xt_ready, 1)

        def block_dve(dve, m, s, n, y_free, tokens):
            for c in range(m.fc):
                dve.wait_ge(m.sg_ready, n * m.fc + c + 1)
                dve.tensor_tensor(m.h[:, s, c, :], bank[2 + c % 2][:, 256:256 + SLOTS], m.sg[:, c % 2, :],
                                  ALU.mult).then_inc(m.h_ready, 1)
            tokens()
            dve.wait_ge(m.d_done, n + 1)
            y_free(dve)
            dve.tensor_copy(m.y[0:SLOTS, s, 512:D], bank[5][0:SLOTS, :]).then_inc(m.y_ready, 1)

        def experts_act(act, m):
            def body(i, s, first, last):
                free = (lambda e: None) if first else (lambda e: e.wait_ge(m.y_out[s], i * 16))
                block_act(act, m, s, i * 2 + s, free, first and s == 0)

            turns(act, body)
            spare(act, m, lambda b: block_act(act, m, 0, b + EXPERTS,
                                              lambda e: e.wait_ge(m.y_out[0], b * 16 + 16 * EXPERTS // 2), False))

        def experts_dve(dve, m):
            tokens_dve(dve, m, 0, 0)

            def body(i, s, first, last):
                free = (lambda e: None) if first else (lambda e: e.wait_ge(m.y_out[s], i * 16))
                e = i * 2 + s
                block_dve(dve, m, s, e, free, (lambda: None) if last and s == 1 else lambda: tokens_dve(dve, m, 1 - s, e + 1))

            turns(dve, body)

            def further(b):
                n = b + EXPERTS
                tokens_dve(dve, m, 0, n)
                block_dve(dve, m, 0, n, lambda e: e.wait_ge(m.y_out[0], b * 16 + 16 * EXPERTS // 2), lambda: None)

            spare(dve, m, further)


        def view(start, *dims):
            one = work[:, start:start + 1]
            return bass.AP(one.tensor, one.offset, [list(one.ap[0])] + [list(d) for d in dims])

        def half(ap, b, tile, h):
            return ap[:, tile * P:(tile + 1) * P].rearrange("p (m h b) -> p m h b", h=2, b=b)[:, :, h, :]

        def all_halves(start, b, step):
            return view(start, (SEQ, 2), (2 * b, SEQ // (2 * b)), (step, b))

        tiles_diag = view(attn_at, (SEQ + P, NT), (1, P))
        pairs_off = view(attn_at + P, (2 * SEQ + 2 * P, 2), (SEQ - P, 2), (1, P))
        four_tiles = lambda b: b[:, :].rearrange("p (a t) -> p a t", a=NT)

        def hg_proj(pe, x, c, part, parts):
            if part == 0:
                pe.wait_ge(hg_in[c], x * 16 + 16)
            if c < 4:
                n = KD // parts
                for k in range(part * n, part * n + n):
                    last = pe.matmul(bank[4 + c % 2][:, :], w_hg[:, c, k, :], hT[:, k, :], start=k == 0, stop=k == KD - 1)
            else:
                n = NT // parts
                for i in range(part * n, part * n + n):
                    for k in range(KD):
                        last = pe.matmul(bank[6][:, i * P:(i + 1) * P], hT[:, k, i * P:(i + 1) * P], w_hg[:, c, k, :],
                                         start=k == 0, stop=k == KD - 1)
            if part == parts - 1:
                last.then_inc(hp_done, 1)

        def hg_pe(pe):
            hg_proj(pe, 0, 0, 0, 1)
            hg_proj(pe, 0, 1, 0, 1)
            pe.wait_ge(h_q, 1)
            hg_proj(pe, 0, 2, 0, 1)
            pe.wait_ge(h_F, 1)
            hg_proj(pe, 0, 3, 0, 1)
            hg_proj(pe, 0, 4, 0, 1)

            def head(h, more):
                x = h + 1
                if more:
                    pe.wait_ge(h_F, x * 2)
                    hg_proj(pe, x, 0, 0, 2)
                pe.wait_ge(h_init, h + 1)
                for i in range(NT):
                    last = pe.matmul(bank[0][:, i * P:(i + 1) * P], ksum[:, i * P:(i + 1) * P], Q[:, i * P:(i + 1) * P],
                                     start=True, stop=True)
                last.then_inc(l_done, 1)
                if more:
                    hg_proj(pe, x, 0, 1, 2)
                for n in range(1, LEVELS + 1):
                    b = 1 << (n - 1)
                    if n == 2:
                        pe.wait_ge(h_base, h + 1)
                    if n >= 2:
                        pe.wait_ge(h_upd, h * 8 + n - 1)
                    for i in range(NT):
                        pe.matmul(half(bank[n % 2][:, :], b, i, 1), X[:, 0, i * P:(i + 1) * P], half(X[:, 2, :], b, i, 1),
                                  start=True, stop=True)
                        last = pe.matmul(half(bank[n % 2][:, :], b, i, 0), X[:, 3, i * P:(i + 1) * P],
                                         half(X[:, 1, :], b, i, 0), start=True, stop=True)
                    last.then_inc(l_done, 1)
                    if more:
                        c, part = divmod(n + 1, 2)
                        if n == 1:
                            pe.wait_ge(h_gate, h + 1)
                        if n == 3:
                            pe.wait_ge(h_q, x + 1)
                        if n == 5:
                            pe.wait_ge(h_F, x * 2 + 1)
                        if n == 7:
                            pe.wait_ge(h_V, x)
                            hg_proj(pe, x, 4, 0, 4)
                            hg_proj(pe, x, 4, 1, 4)
                        else:
                            hg_proj(pe, x, c, part, 2)
                pe.wait_ge(h_upd, h * 8 + 7)
                for m, (a, t, arrays) in enumerate(((0, 1, (0, 2)), (1, 0, (3, 1)), (2, 3, (0, 2)), (3, 2, (3, 1)))):
                    last = pe.matmul(bank[0][:, m * P:(m + 1) * P], X[:, arrays[0], a * P:(a + 1) * P],
                                     X[:, arrays[1], t * P:(t + 1) * P], start=True, stop=True)
                last.then_inc(l_done, 1)
                if more:
                    hg_proj(pe, x, 4, 2, 4)
                pe.wait_ge(h_upd, h * 8 + 8)
                for a in range(NT):
                    back = a // 2
                    last = pe.matmul(bank[1 + back][:, (a % 2) * 256:(a % 2 + 1) * 256], X[:, 3 * back, a * P:(a + 1) * P],
                                     X[:, 2 - back, (1 - back) * 256:(2 - back) * 256], start=True, stop=True)
                    if a % 2:
                        last.then_inc(l_done, 1)
                pe.wait_ge(h_copy, h * LEVELS + LEVELS)
                pe.wait_ge(h_far, h * 3 + 3)
                pe.wait_ge(h_V, h + 1)
                for a in range(NT):
                    last = pe.matmul(bank[3][:, :], V[:, a, :], attnT[:, a, :], start=a == 0, stop=a == NT - 1)
                last.then_inc(h_av, 1)
                if more:
                    hg_proj(pe, x, 4, 3, 4)
                pe.wait_ge(h_sq, h + 1)
                pe.matmul(bank[2][:, :], ones[:, :], sqr, start=True, stop=True).then_inc(h_nm, 1)

            with pe.Fori(0, G_HEADS - 1) as h:
                head(h, True)
            head(G_HEADS - 1, False)

        def hg_act(act):
            act.wait_ge(lb_ready, 1)
            act.activation(head_row[:, 0, :], head_row[:, 4, :], ACT.Sigmoid).then_inc(lb_ready, 1)

            def sig_q(x, first):
                if not first:
                    act.wait_ge(h_gate, x)
                act.wait_ge(hp_done, x * 5 + 1)
                act.activation(sig, bank[4][:, :], ACT.Sigmoid).then_inc(h_sig, 1)

            def sig_f(x, c):
                act.wait_ge(hp_done, x * 5 + 2 + c)
                act.activation(F[:, c, :], bank[5 - c][:, :], ACT.Sigmoid).then_inc(h_F, 1)

            def sig_gate(x):
                act.wait_ge(h_q, x + 1)
                act.wait_ge(hp_done, x * 5 + 4)
                act.activation(sig, bank[5][:, :], ACT.Sigmoid).then_inc(h_sig, 1)

            def values(x):
                act.wait_ge(hp_done, x * 5 + 5)
                act.activation(V, four_tiles(bank[6]), ACT.Copy).then_inc(h_V, 1)

            sig_q(0, True)
            sig_f(0, 0)
            sig_f(0, 1)
            sig_gate(0)
            values(0)

            def head(h, more):
                act.wait_ge(l_done, h * 11 + 1)
                act.activation(tiles_diag, four_tiles(bank[0]), ACT.Copy).then_inc(h_base, 1)
                if more:
                    sig_q(h + 1, False)
                    sig_f(h + 1, 0)
                    sig_f(h + 1, 1)
                    sig_gate(h + 1)
                act.wait_ge(l_done, h * 11 + 9)
                act.activation(pairs_off, bank[0][:, :].rearrange("p (a b t) -> p a b t", a=2, b=2), ACT.Copy).then_inc(h_far, 1)
                for back in range(2):
                    act.wait_ge(l_done, h * 11 + 10 + back)
                    act.activation(attnT[:, 2 * back:2 * back + 2, (1 - back) * 256:(2 - back) * 256],
                                   bank[1 + back][:, :].rearrange("p (a t) -> p a t", a=2), ACT.Copy).then_inc(h_far, 1)
                act.wait_ge(h_av, h + 1)
                act.activation(sqr, bank[3][:, :], ACT.Square).then_inc(h_sq, 1)
                if more:
                    values(h + 1)
                act.wait_ge(h_var, h + 1)
                act.activation(root, root, ACT.Sqrt).then_inc(h_root, 1)

            with act.Fori(0, G_HEADS - 1) as h:
                head(h, True)
            head(G_HEADS - 1, False)

        def hg_dve(dve):
            dve.wait_ge(lb_in, 64)
            dve.tensor_tensor(head_row[:, 4, :], head_row[:, 5, :], head_row[:, 4, :], ALU.subtract).then_inc(lb_ready, 1)
            dve.wait_ge(lb_ready, 2)
            dve.tensor_scalar(head_row[:, 1, :], head_row[:, 0, :], -1.0, 1.0, ALU.mult, ALU.add).then_inc(*dve_own.up())
            dve.wait_ge(*dve_own.now())

            def query(x):
                dve.wait_ge(h_sig, x * 2 + 1)
                dve.tensor_tensor(Q, bank[4][:, :], sig, ALU.mult).then_inc(h_q, 1)

            def gates(x):
                dve.wait_ge(h_sig, x * 2 + 2)
                dve.scalar_tensor_tensor(gate, bank[5][:, :], head_row[:, 2, bass.ds(x, 1)], sig, ALU.mult,
                                         ALU.mult).then_inc(h_gate, 1)

            query(0)
            gates(0)

            def head(h, more, own):
                dve.wait_ge(h_F, h * 2 + 2)
                dve.wait_ge(h_q, h + 1)
                dve.tensor_scalar(T, F, head_row[:, 1, bass.ds(h, 1)], head_row[:, 0, bass.ds(h, 1)], ALU.mult,
                                  ALU.add).then_inc(*own.up())
                dve.wait_ge(*own.now())
                dve.tensor_scalar(view(x_at, (3 * SEQ, 2), (1, SEQ)), T, -1.0, 1.0, ALU.mult, ALU.add).then_inc(*own.up())
                dve.tensor_tensor(X[:, 2, :], T[:, 0, :], Q, ALU.mult)
                dve.tensor_tensor(X[:, 1, :], T[:, 1, :], Q, ALU.mult)
                dve.wait_ge(*own.now())
                dve.tensor_tensor(ksum, X[:, 0, :], X[:, 3, :], ALU.add).then_inc(h_init, 1)
                for n in range(1, LEVELS + 2):
                    b = 1 << (n - 1)
                    dve.wait_ge(l_done, h * 11 + n + 1)
                    if n >= 2:
                        dve.wait_ge(*own.now())
                        dve.wait_ge(h_upd, h * 8 + n - 1)
                    else:
                        dve.wait_ge(h_init, h + 1)
                    if n == 1:
                        dve.wait_ge(h_base, h + 1)
                    elif n <= LEVELS:
                        dve.wait_ge(h_copy, h * LEVELS + n - 1)
                    up, low = x_at + 2 * SEQ + b, x_at
                    dve.tensor_tensor(all_halves(up, b, 1), all_halves(up, b, 1), all_halves(t_at, b, 0), ALU.mult)
                    dve.tensor_tensor(all_halves(low, b, 1), all_halves(low, b, 1), all_halves(t_at + b, b, 0),
                                      ALU.mult).then_inc(h_upd, 1)
                    if n <= LEVELS:
                        dve.copy_predicated(tiles_diag, masks[:, n - 1, :].unsqueeze(1).to_broadcast([P, NT, P]),
                                            four_tiles(bank[n % 2])).then_inc(h_copy, 1)
                        dve.wait_ge(h_upd, h * 8 + n)
                        starts = view(t_at, (SEQ, 2), (2 * b, SEQ // (2 * b)))
                        dve.tensor_tensor(starts, starts, view(t_at + b, (SEQ, 2), (2 * b, SEQ // (2 * b))),
                                          ALU.mult).then_inc(*own.up())
                    if n == 3 and more:
                        query(h + 1)
                dve.wait_ge(h_nm, h + 1)
                dve.tensor_scalar(root, bank[2][:, :], 1.0 / P, EPS, ALU.mult, ALU.add).then_inc(h_var, 1)
                dve.tensor_tensor(sqr, bank[3][:, :], gate, ALU.mult).then_inc(*own.up())
                dve.wait_ge(h_root, h + 1)
                dve.reciprocal(root, root).then_inc(*own.up())
                dve.wait_ge(*own.now())
                dve.tensor_tensor(oTh[:, bass.ds(h, 1), :], sqr.unsqueeze(1), root.unsqueeze(1), ALU.mult).then_inc(h_fin, 1)
                if more:
                    gates(h + 1)

            with dve.Fori(0, G_HEADS - 1) as h:
                dve_own.loop(h, 4 + LEVELS)
                head(h, True, dve_own)
            dve_own.loop_end(G_HEADS - 1)
            head(G_HEADS - 1, False, dve_own)


        def ret_proj(pe, x, n):
            c = (0, 0, 1, 1, 2, 2, 3)[n]
            if n in (0, 2, 4, 6):
                pe.wait_ge(ret_in[c], x * 16 + 16)
            if n < 6:
                cols = slice(n % 2, R_DIM, 2) if n < 4 else slice((n - 4) * P, (n - 3) * P)
                for k in range(KD):
                    last = pe.matmul(bank[4 + n % 4][:, :], w_ret[:, c, k, cols], hT[:, k, :], start=k == 0, stop=k == KD - 1)
            else:
                for i in range(NT):
                    for k in range(KD):
                        last = pe.matmul(bank[6 + i // 2][:, (i % 2) * R_DIM:(i % 2 + 1) * R_DIM], hT[:, k, i * P:(i + 1) * P],
                                         w_ret[:, c, k, :], start=k == 0, stop=k == KD - 1)
            last.then_inc(rp_done, 1)

        def ret_pe(pe):
            for n in range(4):
                ret_proj(pe, 0, n)
            pe.wait_ge(rr_q, 1)
            ret_proj(pe, 0, 4)
            ret_proj(pe, 0, 5)
            pe.wait_ge(rr_k, 1)
            ret_proj(pe, 0, 6)

            def head(h, more):
                x = h + 1
                if more:
                    pe.wait_ge(r_gate, x * 2)
                    ret_proj(pe, x, 0)
                pe.wait_ge(rr_k, h + 1)
                pe.wait_ge(r_fin, h + 1)
                for a in range(NT):
                    for e in range(2):
                        last = pe.matmul(bank[a][:, :], rk[:, e, a * P:(a + 1) * P], rq[:, e, :], start=e == 0, stop=e == 1)
                    last.then_inc(rs_done, 1)
                if more:
                    ret_proj(pe, x, 1)
                    pe.wait_ge(r_V, x)
                    ret_proj(pe, x, 2)
                    ret_proj(pe, x, 3)
                pe.wait_ge(r_dec, h * 4 + 4)
                pe.wait_ge(r_V, h + 1)
                for v in range(2):
                    for a in range(NT):
                        last = pe.matmul(bank[v][:, :], rV[:, a, v * P:(v + 1) * P], rattn[:, a, :], start=a == 0,
                                         stop=a == NT - 1)
                    last.then_inc(r_av, 1)
                if more:
                    pe.wait_ge(rr_q, x + 1)
                    ret_proj(pe, x, 4)
                    ret_proj(pe, x, 5)
                pe.wait_ge(r_sq, h * 2 + 2)
                for v in range(2):
                    last = pe.matmul(bank[2][:, :], ones[:, :], rtmp[:, v, :], start=v == 0, stop=v == 1)
                last.then_inc(r_nm, 1)
                if more:
                    pe.wait_ge(rr_k, x + 1)
                    ret_proj(pe, x, 6)

            with pe.Fori(0, R_HEADS - 1) as h:
                head(h, True)
            head(R_HEADS - 1, False)

        def ret_act(act):
            act.wait_ge(ang_ready, 1)
            act.activation(sinr, sinr, ACT.Sin)
            act.activation(cosr, cosr, ACT.Sin).then_inc(rot_ready, 1)

            def sig_gates(x):
                for v in range(2):
                    act.wait_ge(rp_done, x * 7 + 5 + v)
                    act.activation(rsq[:, v, :], bank[4 + v][:, :], ACT.Sigmoid).then_inc(r_sig, 1)

            def values(x):
                act.wait_ge(rp_done, x * 7 + 7)
                for v in range(2):
                    last = act.activation(rV[:, 2 * v:2 * v + 2, :], bank[6 + v][:, :].rearrange("p (a n) -> p a n", a=2), ACT.Copy)
                last.then_inc(r_V, 1)

            sig_gates(0)
            values(0)

            def head(h, more):
                for v in range(2):
                    act.wait_ge(r_av, h * 2 + 1 + v)
                    if v == 0:
                        act.wait_ge(r_tmp, h + 1 + more)
                    act.activation(rtmp[:, v, :], bank[v][:, :], ACT.Square).then_inc(r_sq, 1)
                if more:
                    sig_gates(h + 1)
                act.wait_ge(r_var, h + 1)
                act.activation(rroot, rroot, ACT.Sqrt).then_inc(r_root, 1)
                if more:
                    values(h + 1)

            with act.Fori(0, R_HEADS - 1) as h:
                head(h, 1)
            head(R_HEADS - 1, 0)

        def ret_dve(dve):
            def step(ins):
                ins.then_inc(*dve_own.up())
                dve.wait_ge(*dve_own.now())

            dve.wait_ge(pos_in, 16)
            ang, turns_, pos_f = rtmp[:, 0, :], rtmp[:, 1, :], cosr
            step(dve.tensor_copy(pos_f, rroot.bitcast(I32)))
            step(dve.tensor_scalar(ang, pos_f, rates[:, 0:1], None, ALU.mult))
            step(dve.tensor_scalar(turns_, ang, 1.0 / (2.0 * np.pi), None, ALU.mult))
            step(dve.tensor_scalar(turns_, turns_, ROUND, None, ALU.add))
            step(dve.tensor_scalar(turns_, turns_, -ROUND, None, ALU.add))
            for part in TWO_PI:
                step(dve.scalar_tensor_tensor(ang, turns_, -part, ang, ALU.mult, ALU.add))
            step(dve.tensor_scalar(sinr, ang, PI_BELOW, -PI_BELOW, ALU.min, ALU.max))
            step(dve.tensor_scalar(cosr, ang, float(np.pi / 2), None, ALU.add))
            step(dve.tensor_scalar(turns_, cosr, PI_BELOW, float(2.0 * np.pi), ALU.is_gt, ALU.mult))
            step(dve.tensor_tensor(cosr, cosr, turns_, ALU.subtract))
            dve.tensor_scalar(cosr, cosr, PI_BELOW, -PI_BELOW, ALU.min, ALU.max).then_inc(ang_ready, 1)
            dve.sem_inc(r_fin, 1)
            dve.sem_inc(r_tmp, 1)
            dve.wait_ge(rot_ready, 1)

            def rotate(x, own, first, out, done, is_k):
                even, odd = bank[first], bank[first + 1]
                dve.wait_ge(rp_done, x * 7 + 2 + 2 * is_k)
                for o, (ce, co, op) in enumerate(((cosr, sinr, ALU.subtract), (sinr, cosr, ALU.add))):
                    dve.tensor_tensor(out[:, o, :], even[:, :], ce, ALU.mult).then_inc(*own.up())
                    dve.tensor_tensor(rtmp[:, o, :], odd[:, :], co, ALU.mult).then_inc(*own.up())
                    dve.wait_ge(*own.now())
                    last = dve.tensor_tensor(out[:, o, :], out[:, o, :], rtmp[:, o, :], op)
                    if o == 0:
                        last.then_inc(*own.up())
                last.then_inc(done, 1)
                dve.wait_ge(done, x + 1)

            def gates(x):
                for v in range(2):
                    dve.wait_ge(r_sig, x * 2 + 1 + v)
                    dve.scalar_tensor_tensor(rgate[:, v, :], bank[4 + v][:, :], head_row[:, 3, bass.ds(x * 2 + v, 1)],
                                             rsq[:, v, :], ALU.mult, ALU.mult).then_inc(r_gate, 1)

            rotate(0, dve_own, 4, rq, rr_q, 0)
            rotate(0, dve_own, 6, rk, rr_k, 1)
            gates(0)

            def head(h, more, own):
                dve.wait_ge(decay_in, h * 16 + 16)
                for a in range(NT):
                    dve.wait_ge(rs_done, h * 4 + a + 1)
                    dve.tensor_tensor(rattn[:, a, :], bank[a][:, :], decay[:, SEQ - P - a * P:2 * SEQ - P - a * P],
                                      ALU.mult).then_inc(r_dec, 1)
                if more:
                    rotate(h + 1, own, 4, rq, rr_q, 0)
                    rotate(h + 1, own, 6, rk, rr_k, 1)
                    dve.sem_inc(r_tmp, 1)
                dve.wait_ge(r_nm, h + 1)
                dve.tensor_scalar(rroot, bank[2][:, :], 1.0 / R_DIM, EPS, ALU.mult, ALU.add).then_inc(r_var, 1)
                for v in range(2):
                    dve.tensor_tensor(rtmp[:, v, :], bank[v][:, :], rgate[:, v, :], ALU.mult).then_inc(*own.up())
                dve.wait_ge(r_root, h + 1)
                dve.reciprocal(rroot, rroot).then_inc(*own.up())
                dve.wait_ge(*own.now())
                dve.tensor_tensor(oTr[:, bass.ds(h * 2, 2), :], rtmp, rroot.unsqueeze(1).to_broadcast([P, 2, SEQ]),
                                  ALU.mult).then_inc(r_fin, 1)
                if more:
                    dve.wait_ge(r_fin, h + 2)
                    gates(h + 1)

            with dve.Fori(0, R_HEADS - 1) as h:
                dve_own.loop(h, 13)
                head(h, True, dve_own)
            dve_own.loop_end(R_HEADS - 1)
            head(R_HEADS - 1, False, dve_own)


        def merge_pe(pe):
            pe.wait_ge(h_fin, G_HEADS)
            pe.wait_ge(r_fin, R_HEADS + 1)
            with pe.Fori(0, KD // 2) as i:
                for s in range(2):
                    pe.wait_ge(mrg_in[s], i * 64 + 64)
                    pe.wait_ge(m_ready, i * 2 + s + 1)
                    for c, src in enumerate((hT, hT, oTh, oTr)):
                        for k in range(KD):
                            last = pe.matmul(bank[4 * s + c][:, :], w_mrg[:, s, c, k, :], src[:, k, :], start=k == 0,
                                             stop=k == KD - 1)
                        last.then_inc(m_done, 1)
            pe.wait_ge(m_ready, KD + 2)
            pe.wait_ge(w_o2_in, 16)
            for i in range(NT):
                for h in range(2):
                    n = 2 * i + h
                    if n >= 4:
                        pe.wait_ge(x1_ready, 2 * NT + n - 3)
                    for k in range(KD):
                        last = pe.matmul(bank[n % 4][:, :], merged[:, k, i * P:(i + 1) * P], w_o2[:, k, h * 512:(h + 1) * 512],
                                         start=k == 0, stop=k == KD - 1)
                    last.then_inc(wo_done, 1)

        def merge_act(act):
            with act.Fori(0, KD // 2) as i:
                for s in range(2):
                    for c in range(2):
                        act.wait_ge(m_done, i * 8 + 4 * s + c + 1)
                        act.wait_ge(m_ready, i * 2 + s + 1)
                        act.activation(msig[:, s, c, :], bank[4 * s + c][:, :], ACT.Sigmoid).then_inc(m_sig, 1)

        def merge_dve(dve):
            dve.sem_inc(m_ready, 2)
            with dve.Fori(0, KD // 2) as i:
                dve_own.loop(i, 4)
                for s in range(2):
                    for c in range(2):
                        dve.wait_ge(m_done, i * 8 + 4 * s + c + 3)
                        dve.wait_ge(m_sig, i * 4 + 2 * s + c + 1)
                        dve.tensor_tensor(mtmp[:, s, c, :], bank[4 * s + 2 + c][:, :], msig[:, s, c, :], ALU.mult).then_inc(*dve_own.up())
                    dve.wait_ge(*dve_own.now())
                    dve.tensor_tensor(merged[:, bass.ds(i * 2 + s, 1), :], mtmp[:, s, 0:1, :], mtmp[:, s, 1:2, :],
                                      ALU.add).then_inc(m_ready, 1)
            dve_own.loop_end(KD // 2)
            for n in range(2 * NT):
                dve.wait_ge(wo_done, 2 * NT + n + 1)
                half = xres[:, n // 2, (n % 2) * 512:(n % 2 + 1) * 512]
                dve.scalar_tensor_tensor(half, half, ALPHA, bank[n % 4][:, :], ALU.mult, ALU.add).then_inc(x1_ready, 1)

        def layer_norm_act(act, r):
            act.wait_ge(var_ready, r + 1)
            act.activation(stat[:, 0:NT], stat[:, 0:NT], ACT.Sqrt).then_inc(root_ready, 1)

        def layer_norm_dve(dve, r, rows, rows_in):
            for i in range(NT):
                for h in range(2):
                    dve.bn_stats(bn[:, i, h, :], xres[:, i, h * 512:(h + 1) * 512]).then_inc(*dve_own.up())
            dve.wait_ge(*dve_own.now())
            for i in range(NT):
                dve.bn_aggr(mv[:, i, :], bn[:, i, :, :]).then_inc(*dve_own.up())
            dve.wait_ge(*dve_own.now())
            dve.tensor_scalar(stat[:, 0:NT], mv[:, :, 1], LN_EPS, None, ALU.add).then_inc(var_ready, 1)
            dve.wait_ge(root_ready, r + 1)
            dve.reciprocal(stat[:, 0:NT], stat[:, 0:NT]).then_inc(*dve_own.up())
            dve.wait_ge(*dve_own.now())
            rows_in()
            for i in range(NT):
                x = xres[:, i, :]
                dve.tensor_scalar(x, x, mv[:, i, 0:1], stat[:, i:i + 1], ALU.subtract, ALU.mult).then_inc(*dve_own.up())
                dve.wait_ge(*dve_own.now())
                dve.tensor_tensor(x, x, rows[0], ALU.mult).then_inc(*dve_own.up())
                dve.wait_ge(*dve_own.now())
                dve.tensor_tensor(x, x, rows[1], ALU.add).then_inc(ln_ready, 1)

        @block.sync
        def _(sp):
            sp.dma_start(ident[:, :], A["c_ident"]).then_inc(bias_in, 16)
            for i in range(NT):
                sp.dma_start(xres[:, i, :], A["x"][i * P:(i + 1) * P, :]).then_inc(x_in[i], 16)
            sp.dma_start(onehot, A["c_bucket"]).then_inc(bias_in, 16)
            sp.dma_start(masks_wide, A["c_masks"].rearrange("p a b -> p (a b)")).then_inc(gains_in, 16)
            sp.dma_start(relb[0:REL_BUCKETS, :], A["rel_bias"]).then_inc(bias_in, 16)
            for n, g in enumerate(("g_attn_norm", "g_ffn_norm")):
                sp.dma_start(gains[:, 2 * n, :], A[g].rearrange("a (p k) -> (a p) k", k=KD)).then_inc(gains_in, 16)
            sp.dma_start(gains[0:64, 1, :], A["g_out_a"].rearrange("a (p k) -> (a p) k", k=KD)).then_inc(gains_in, 16)
            sp.dma_start(gains[64:P, 1, :], A["g_out_b"].rearrange("a (p k) -> (a p) k", k=KD)).then_inc(gains_in, 16)
            for c in range(2):
                sp.dma_start(gains_c[:, c:c + 1], A["g_q_latent"][:, c * P:(c + 1) * P].rearrange("a (p k) -> (a p) k", k=1)).then_inc(gains_in, 16)
            sp.dma_start(gains_c[:, 2:3], A["g_kv_latent"].rearrange("a (p k) -> (a p) k", k=1)).then_inc(gains_in, 16)
            w_in = A["w_in"].rearrange("(p k) n -> p k n", k=KD)
            w_heads = w_in[:, :, 0:3 * A_WIDTH].rearrange("p k (c n) -> p k c n", c=3)

            def load_pair(pair):
                for c in range(3):
                    sp.dma_start(w_pair[:, :, c, :], w_heads[:, :, c, bass.ds(pair * P, P)]).then_inc(w_pair_in, 16)

            def load_toep(pair):
                for j in range(2):
                    row = bass.AP(table_dram.tensor, (pair * 2 + j) * (2 * SEQ), [[1, P], [1, TOEP]])
                    sp.dma_start(toep[:, j, :], row).then_inc(toep_in, 16)

            load_pair(0)
            sp.wait_ge(zeros_ready, 1)
            clear_spare_rows(sp, moe1)
            clear_spare_rows(sp, moe2)
            sp.dma_start(w_c, w_in[:, :, 3 * A_WIDTH:]).then_inc(w_c_in, 16)
            sp.dma_start(rope_q[:, :], A["c_rope_q"]).then_inc(rope_in, 16)
            sp.dma_start(rope_k[:, :, :, :], A["c_rope_k"]).then_inc(rope_in, 16)
            w_qu = A["w_q_up_rows"].rearrange("(c p) h m -> p c h m", c=2)
            w_kvu = A["w_kv_up"].rearrange("p (h m) -> p h m", h=B_HEADS)
            sp.dma_start(w_up_v, w_kvu[:, :, NOPE:]).then_inc(w_c_in, 16)

            def load_up(pair):
                for c in range(2):
                    sp.dma_start(w_up_q[:, c, :, :], w_qu[:, c, bass.ds(pair * 2, 2), :]).then_inc(w_up_in, 16)
                sp.dma_start(w_up_k, w_kvu[:, bass.ds(pair * 2, 2), 0:NOPE]).then_inc(w_up_in, 16)

            load_up(0)
            sp.dma_start(w_o, A["w_out"].rearrange("(p k) n -> p k n", k=KD)).then_inc(w_o_in, 16)
            sp.wait_ge(table_ready, 2)
            sp.dma_start(table_dram, table).then_inc(table_out, 16)
            sp.wait_ge(table_out, 16)
            load_toep(0)
            with sp.Fori(0, PAIRS - 1) as last:
                sp.wait_ge(proj_done, last * 3 + 3)
                load_pair(last + 1)
                sp.wait_ge(biased, last * STEPS + STEPS)
                load_toep(last + 1)
            with sp.Fori(0, PAIRS - 1) as last:
                sp.wait_ge(up_done, last * 4 + 4)
                load_up(last + 1)
            if stop == "S1":
                sp.wait_ge(o_ready, 2 * PAIRS * STEPS)
                sp.dma_start(out.rearrange("(i p) d -> p i d", p=P), outAB).then_inc(final_out, 16)
                sp.wait_ge(final_out, 16)
                return
            for n, r in ((0, "w_router_group"), (GROUPS, "w_router_expert")):
                cols = A[r].shape[1]
                sp.dma_start(w_r1[:, :, n:n + cols], A[r].rearrange("(p k) n -> p k n", k=KD)).then_inc(r_in, 16)
            sp.dma_start(b_r1, A["b_router"].partition_broadcast(P).rearrange("p a n -> p (a n)")).then_inc(r_in, 16)
            sp.dma_start(before, A["c_before"]).then_inc(route_in, 16)
            sp.dma_start(route, A["c_route"]).then_inc(route_in, 16)
            sp.dma_start(token[:, :], A["c_token"]).then_inc(route_in, 16)
            sp.dma_start(g_row, A["g_final"].partition_broadcast(P)).then_inc(g_row_in, 16)
            load_expert(sp, moe1, 0, 0)
            load_expert(sp, moe1, 1, 1)
            for i in range(NT):
                sp.wait_ge(normed, 2 * NT + i + 1)
                sp.dma_start(moe1.x_dram[i * P:(i + 1) * P, :], xn[:, i % 2, :]).then_inc(x_out[i], 16)
            w_in2 = A["w_in_2"].rearrange("(p k) n -> p k n", k=KD)

            def load_hg(h, c):
                sp.dma_start(w_hg[:, c, :, :], w_in2[:, :, bass.ds(h * P + HG_COLS[c], P)]).then_inc(hg_in[c], 16)

            def load_ret(h, c):
                sp.dma_start(w_ret[:, c, :, :], w_in2[:, :, bass.ds(h * R_DIM + R_COLS[c], R_DIM)]).then_inc(ret_in[c], 16)

            def load_decay(h):
                sp.dma_start(decay.unsqueeze(1), A["c_decay"][bass.ds(h, 1)].rearrange("a p n -> p a n")).then_inc(decay_in, 16)

            def load_merge(j, s):
                for c in range(2):
                    sp.dma_start(w_mrg[:, s, c, :, :], w_in2[:, :, bass.ds(j * P + M_COLS[c], P)]).then_inc(mrg_in[s], 16)
                for c, w in ((2, "w_branch_hg_2"), (3, "w_branch_ret_2")):
                    sp.dma_start(w_mrg[:, s, c, :, :], A[w].rearrange("(c p) n -> p c n", p=P)[:, :, bass.ds(j * P, P)]).then_inc(mrg_in[s], 16)

            col = lambda a: a.rearrange("a (h p) -> p (a h)", p=P)
            for r, g in ((2, "hg_norm_g_2"), (3, "ret_norm_g_2")):
                sp.dma_start(head_row[:, r, :], col(A[g]), allow_slow_non_contiguous=True).then_inc(lb_in, 16)
            sp.dma_start(head_row[:, 4:6, :].rearrange("p a h -> p (a h)"), col(A["hg_lb_logits_2"]),
                         allow_slow_non_contiguous=True).then_inc(lb_in, 16)
            sp.dma_start(rates[:, :], A["c_rates"]).then_inc(lb_in, 16)
            for c in range(5):
                load_hg(0, c)
            list_sp(sp, moe1)
            experts_sp(sp, moe1)
            if stop == "S6":
                sp.wait_ge(fin_ready, NT)
                sp.dma_start(out.rearrange("(i p) d -> p i d", p=P), xres[:, :, :]).then_inc(final_out, 16)
                sp.wait_ge(final_out, 16)
                return
            for c in range(4):
                load_ret(0, c)
            with sp.Fori(0, G_HEADS - 1) as h:
                for c in range(5):
                    sp.wait_ge(hp_done, h * 5 + c + 1)
                    load_hg(h + 1, c)
            sp.dma_start(w_r1[:, :, 0:GROUPS], A["w_group_2"].rearrange("(p k) n -> p k n", k=KD)).then_inc(r_in, 16)
            sp.dma_start(w_r1[:, :, GROUPS:], A["w_router_2"].rearrange("(p k) n -> p k n", k=KD)).then_inc(r_in, 16)
            sp.dma_start(b_r1, A["b_route_2"].partition_broadcast(P).rearrange("p a n -> p (a n)")).then_inc(r_in, 16)
            for row, g in zip(ln_row, ("ln1_g_2", "ln1_b_2")):
                sp.dma_start(row, A[g].partition_broadcast(P).rearrange("p a n -> p (a n)")).then_inc(ln_in, 16)
            sp.wait_ge(hp_done, 5 * G_HEADS)
            for s in range(2):
                load_merge(s, s)
            sp.wait_ge(h_fin, G_HEADS)
            sp.dma_start(rroot.bitcast(I32), A["positions_2"].partition_broadcast(P).rearrange("p a n -> p (a n)")).then_inc(pos_in, 16)
            load_decay(0)
            with sp.Fori(0, R_HEADS - 1) as h:
                for c, n in enumerate((2, 4, 6, 7)):
                    sp.wait_ge(rp_done, h * 7 + n)
                    load_ret(h + 1, c)
                sp.wait_ge(r_dec, h * 4 + 4)
                load_decay(h + 1)
            sp.wait_ge(rp_done, 7 * R_HEADS)
            sp.dma_start(w_o2, A["w_out_2"].rearrange("(k p) n -> p k n", p=P)).then_inc(w_o2_in, 16)
            with sp.Fori(0, KD // 2 - 1) as i:
                for s in range(2):
                    sp.wait_ge(m_done, i * 8 + 4 * s + 4)
                    load_merge(i * 2 + s + 2, s)
            sp.wait_ge(wo_done, 4 * NT)
            load_expert(sp, moe2, 0, 0)
            sp.wait_ge(x1_ready, 4 * NT)
            for c, g in enumerate(("ln2_g_2", "ln2_b_2")):
                sp.dma_start(moe2.rows[:, c, :], A[g].partition_broadcast(P).rearrange("p a n -> p (a n)")).then_inc(ln2_in, 16)
            for i in range(NT):
                sp.wait_ge(ln_ready, i + 1)
                sp.dma_start(moe2.x_dram[i * P:(i + 1) * P, :], xres[:, i, :]).then_inc(x_out[i], 16)
            sp.wait_ge(routed, 2)
            load_expert(sp, moe2, 1, 1)
            list_sp(sp, moe2)
            experts_sp(sp, moe2)
            for i in range(NT):
                sp.wait_ge(ln_ready, NT + i + 1)
                sp.dma_start(out[i * P:(i + 1) * P, :], xres[:, i, :]).then_inc(final_out, 16)
            sp.wait_ge(final_out, 16 * NT)

        @block.tensor
        def _(pe):
            pe.wait_ge(bias_in, 48)
            pe.wait_ge(ones_row, 1)
            for half in range(2):
                last = pe.matmul(bank[half][0:A_HEADS, :], relb, onehot[:, half * SEQ:(half + 1) * SEQ],
                                 start=True, stop=True)
            last.then_inc(table_mm, 1)
            norm_pe(pe, 0, lambda i: xn[:, i % 2, :], xn_ready(0))
            pe.wait_ge(hT_ready, 2 * NT)
            with pe.Fori(0, PAIRS) as pair:
                pe.wait_ge(w_pair_in, pair * 48 + 48)
                for c in range(2):
                    for k in range(KD):
                        last = pe.matmul(bank[6 + c][:, :], w_pair[:, k, c, :], hT[:, k, :], start=k == 0, stop=k == KD - 1)
                    last.then_inc(proj_done, 1)
                pe.wait_ge(q_ready, pair + 1)
                for i in range(NT):
                    for k in range(KD):
                        last = pe.matmul(bank[6][:, i * P:(i + 1) * P], hT[:, k, i * P:(i + 1) * P], w_pair[:, k, 2, :],
                                         start=k == 0, stop=k == KD - 1)
                last.then_inc(proj_done, 1)
                core_pe(pe, pair, 0, (
                    lambda j, i: qT[64 * j:64 * j + 64, 0, i * P:(i + 1) * P],
                    lambda j: kT[64 * j:64 * j + 64, 0, :],
                    lambda j, kc: v_pair[:, kc, j * A_DIM:(j + 1) * A_DIM]),
                    lambda: (pe.wait_ge(k_ready, pair + 1), pe.wait_ge(v_ready, pair + 1)))
            pe.wait_ge(w_c_in, 32)
            for i in range(NT):
                if i >= 2:
                    pe.wait_ge(c_ready, i - 1)
                for k in range(KD):
                    last = pe.matmul(bank[6 + i % 2][:, 0:C_WIDTH], hT[:, k, i * P:(i + 1) * P], w_c[:, k, :],
                                     start=k == 0, stop=k == KD - 1)
                last.then_inc(c_done, 1)
            for i in range(NT):
                pe.wait_ge(cn_ready, i + 1)
                for c, (start, wide) in enumerate(((0, P), (P, P), (2 * P, P), (3 * P, 96))):
                    last = pe.transpose(bank[c][0:wide, i * P:(i + 1) * P], cn[:, i, start:start + wide], ident[:, :])
            last.then_inc(ct_done, 1)
            pe.wait_ge(ct_ready, 1)
            pe.wait_ge(c_ready, NT)
            for i in range(NT):
                pe.matmul(bank[4 + i][:, :], cqT[:, 2, i * P:(i + 1) * P], w_up_v, start=True, stop=True).then_inc(vb_done, 1)
            pe.wait_ge(vb_ready, NT)
            with pe.Fori(0, PAIRS) as pair:
                pe.wait_ge(w_up_in, pair * 48 + 48)
                for j in range(2):
                    for c in range(2):
                        last = pe.matmul(bank[6 + j][:, :], w_up_q[:, c, j, :], cqT[:, c, :], start=c == 0, stop=c == 1)
                    last.then_inc(up_done, 1)
                for j in range(2):
                    pe.wait_ge(q_ready, pair * 2 + PAIRS + j + 1)
                    pe.wait_ge(rope_done, pair * 2 + j + 1)
                    pe.matmul(bank[6 + j][0:NOPE, :], w_up_k[:, j, :], cqT[:, 2, :], start=True, stop=True).then_inc(up_done, 1)
                core_pe(pe, pair, PAIRS * STEPS, (
                    lambda j, i: qT[0:96, j, i * P:(i + 1) * P],
                    lambda j: kT[0:96, j, :],
                    lambda j, kc: v_mla(pair, j, kc)),
                    lambda: (pe.wait_ge(k_ready, pair * 2 + PAIRS + 2), pe.wait_ge(q_roped, pair * 2 + 2)))
            norm_pe(pe, 1, lambda i: xn[:, i % 2, :], xn_ready(1))
            pe.wait_ge(hT_ready, 4 * NT)
            pe.wait_ge(w_o_in, 16)
            for i in range(NT):
                for h in range(2):
                    n = 2 * i + h
                    if n >= 4:
                        pe.wait_ge(x1_ready, n - 3)
                    for k in range(KD):
                        last = pe.matmul(bank[n % 4][:, :], hT[:, k, i * P:(i + 1) * P], w_o[:, k, h * 512:(h + 1) * 512],
                                         start=k == 0, stop=k == KD - 1)
                    last.then_inc(wo_done, 1)
            norm_pe(pe, 2, lambda i: xn[:, i % 2, :], xn_ready(2))
            pe.wait_ge(hT_ready, 6 * NT)
            pe.wait_ge(route_in, 48)
            pe.wait_ge(ones_ready, 1)
            route_pe(pe, moe1)
            experts_pe(pe, moe1)
            if stop == "S6":
                return
            norm_pe(pe, 3, lambda i: xres[:, i, :], lambda pe, i: pe.wait_ge(fin_ready, i + 1))
            pe.wait_ge(hT_ready, 8 * NT)
            hg_pe(pe)
            ret_pe(pe)
            merge_pe(pe)
            norm_pe(pe, 4, lambda i: xres[:, i, :], lambda pe, i: pe.wait_ge(ln_ready, i + 1))
            pe.wait_ge(hT_ready, 10 * NT)
            route_pe(pe, moe2)
            experts_pe(pe, moe2)

        @block.gpsimd
        def _(pool):
            route_pool(pool, moe1)
            experts_pool(pool, moe1)
            if stop == "S6":
                return
            route_pool(pool, moe2)
            experts_pool(pool, moe2)

        @block.scalar
        def _(act):
            norm_act(act, 0, lambda i: xres[:, i, :], 1, lambda e, i: e.wait_ge(x_in[i], 16))
            with act.Fori(0, PAIRS) as pair:
                act.wait_ge(proj_done, pair * 3 + 1)
                act.activation(qT[:, 0, :], bank[6][:, :], ACT.Copy, scale=A_DIM ** -0.5).then_inc(q_ready, 1)
                act.wait_ge(proj_done, pair * 3 + 3)
                act.activation(v_pair[:, :, :], bank[6][:, :].rearrange("p (a b) -> p a b", a=NT), ACT.Copy).then_inc(v_ready, 1)
                core_act(act, pair, 0, pair * P)
            for i in range(NT):
                act.wait_ge(c_done, i + 1)
                act.activation(ctok[:, i, :], bank[6 + i % 2][:, 0:C_WIDTH], ACT.Copy).then_inc(c_ready, 1)
                act.wait_ge(c_ready, i + 1)
                act.activation(junk[:, 0:Q_LORA], ctok[:, i, 0:Q_LORA], ACT.Square, scale=(KV_LORA / Q_LORA) ** 0.5,
                               accum_out=stat[:, 2 * i:2 * i + 1]).then_inc(*act_own.up())
                act.wait_ge(*act_own.now())
                act.activation(junk[:, 0:KV_LORA], ctok[:, i, Q_LORA:Q_LORA + KV_LORA], ACT.Square,
                               accum_out=stat[:, 2 * i + 1:2 * i + 2]).then_inc(*act_own.up())
                act.wait_ge(*act_own.now())
            act.sem_inc(sq_ready, 1)
            root_act(act, 1, 2 * NT)
            for i in range(NT):
                act.wait_ge(vb_done, i + 1)
                act.activation(v[:, i, :], bank[4 + i][:, :], ACT.Copy).then_inc(vb_ready, 1)
            with act.Fori(0, PAIRS) as pair:
                for j in range(2):
                    act.wait_ge(up_done, pair * 4 + j + 1)
                    act.activation(qT[0:NOPE, j, :], bank[6 + j][0:NOPE, :], ACT.Copy).then_inc(q_ready, 1)
                core_act(act, pair, PAIRS * STEPS, pair * P + A_WIDTH)
            norm_act(act, 2, lambda i: outAB[:, i, :], 2, lambda e, i: e.wait_ge(o_ready, 2 * PAIRS * STEPS))
            norm_act(act, 3, lambda i: xres[:, i, :], 1, lambda e, i: e.wait_ge(x1_ready, 2 * i + 2))
            route_act(act, moe1)
            experts_act(act, moe1)
            norm_act(act, 4, lambda i: xres[:, i, :], 1, lambda e, i: e.wait_ge(mixed, i + 1), moe1.xg[:, 0, :])
            if stop == "S6":
                return
            hg_act(act)
            ret_act(act)
            merge_act(act)
            layer_norm_act(act, 5)
            route_act(act, moe2)
            experts_act(act, moe2)
            layer_norm_act(act, 6)

        @block.vector
        def _(dve):
            dve.memset(relb[REL_BUCKETS:REL_BUCKETS + 1, :], 1.0).then_inc(ones_row, 1)
            dve.memset(zeros[:, :], 0.0).then_inc(zeros_ready, 1)
            dve.memset(ones[:, :], 1.0).then_inc(ones_ready, 1)
            dve.memset(cn[:, :, 3 * P:3 * P + 64], 0.0)
            for half in range(2):
                dve.wait_ge(table_mm, 1)
                dve.tensor_copy(table[:, half * SEQ:(half + 1) * SEQ], bank[half][0:A_HEADS, :]).then_inc(table_ready, 1)
            dve.wait_ge(gains_in, 16 * 8)
            dve.tensor_copy(masks[:, :, :].rearrange("p a b -> p (a b)"), masks_wide).then_inc(*dve_own.up())
            dve.wait_ge(*dve_own.now())
            norm_dve(dve, 0, 0, lambda i: xres[:, i, :], 1, gains[:, 0, :])
            with dve.Fori(0, PAIRS) as pair:
                dve.wait_ge(proj_done, pair * 3 + 2)
                dve.tensor_copy(kT[:, 0, :], bank[7][:, :]).then_inc(k_ready, 1)
                dve.wait_ge(toep_in, pair * 32 + 32)
                core_dve(dve, pair, 0, toep_tile, 1.0)
            dve.wait_ge(rope_in, 32)
            dve.wait_ge(c_ready, NT)
            for i in range(NT):
                x1, x2 = ctok[:, i, 384:400], ctok[:, i, 400:416]
                cos, sin = rope_k[:, i, 0, :], rope_k[:, i, 1, :]
                for n, (x, t) in enumerate(((x1, cos), (x2, sin), (x1, sin), (x2, cos))):
                    dve.tensor_tensor(rope_t[:, i, n, :], x, t, ALU.mult).then_inc(*dve_own.up())
            dve.wait_ge(*dve_own.now())
            dve.tensor_tensor(cn[:, :, 448:464], rope_t[:, :, 0, :], rope_t[:, :, 1, :], ALU.subtract)
            dve.tensor_tensor(cn[:, :, 464:480], rope_t[:, :, 2, :], rope_t[:, :, 3, :], ALU.add)
            root_dve(dve, 1, 2 * NT, KV_LORA, EPS)
            for i in range(NT):
                dve.tensor_scalar(cn[:, i, 0:Q_LORA], ctok[:, i, 0:Q_LORA], stat[:, 2 * i:2 * i + 1], None, ALU.mult)
                dve.tensor_scalar(cn[:, i, Q_LORA:3 * P], ctok[:, i, Q_LORA:3 * P], stat[:, 2 * i + 1:2 * i + 2], None,
                                  ALU.mult).then_inc(cn_ready, 1)
            dve.wait_ge(ct_done, 1)
            for c in range(3):
                dve.tensor_scalar(cqT[:, c, :], bank[c][:, :], gains_c[:, c:c + 1], None, ALU.mult)
            for j in range(2):
                last = dve.tensor_copy(kT[64:96, j, :], bank[3][64:96, :])
            last.then_inc(ct_ready, 1)
            with dve.Fori(0, PAIRS) as pair:
                dve_own.loop(pair, 2)
                for j in range(2):
                    dve.wait_ge(up_done, pair * 4 + j + 1)
                    dve.tensor_tensor(rope_s[64:96, j, :], bank[6 + j][96:P, :], rope_q[96:P, :], ALU.mult).then_inc(*dve_own.up())
                    dve.tensor_tensor(qT[64:96, j, :], bank[6 + j][64:96, :], rope_q[64:96, :], ALU.mult).then_inc(rope_done, 1)
                    dve.wait_ge(*dve_own.now())
                    dve.wait_ge(rope_done, pair * 2 + j + 1)
                    dve.tensor_tensor(qT[64:96, j, :], qT[64:96, j, :], rope_s[64:96, j, :], ALU.add).then_inc(q_roped, 1)
                for j in range(2):
                    dve.wait_ge(up_done, pair * 4 + j + 3)
                    dve.tensor_copy(kT[0:NOPE, j, :], bank[6 + j][0:NOPE, :]).then_inc(k_ready, 1)
                core_dve(dve, pair, PAIRS * STEPS, lambda j, i: zeros[:, :], (NOPE + ROPE) ** -0.5)
            dve_own.loop_end(PAIRS)
            norm_dve(dve, 1, 2, lambda i: outAB[:, i, :], 2, gains[:, 1, :])
            for n in range(2 * NT):
                dve.wait_ge(wo_done, n + 1)
                half = xres[:, n // 2, (n % 2) * 512:(n % 2 + 1) * 512]
                dve.tensor_tensor(half, half, bank[n % 4][:, :], ALU.add).then_inc(x1_ready, 1)
            norm_dve(dve, 2, 3, lambda i: xres[:, i, :], 1, gains[:, 2, :], lambda i: dve.wait_ge(x_out[i - 2], 16))
            dve.memset(moe1.zero_i, 0).then_inc(zero_ready, 1)
            dve.wait_ge(route_in, 48)
            route_dve(dve, moe1)
            experts_dve(dve, moe1)
            dve.wait_ge(yg_in, 16 * 2 * NT)
            for i in range(NT):
                for c in range(2):
                    dve.scalar_tensor_tensor(xres[:, i, :], moe1.yg[:, c * NT + i, :], moe1.gate[:, c, i:i + 1], xres[:, i, :],
                                             ALU.mult, ALU.add).then_inc(*dve_own.up())
                    dve.wait_ge(*dve_own.now())
                dve.sem_inc(mixed, 1)
            root_dve(dve, 4, NT, D, EPS)
            dve.wait_ge(g_row_in, 16)
            for i in range(NT):
                dve.scalar_tensor_tensor(xres[:, i, :], xres[:, i, :], stat[:, i:i + 1], g_row, ALU.mult,
                                         ALU.mult).then_inc(fin_ready, 1)
            if stop == "S6":
                return
            for i in range(NT):
                fold_dve(dve, 3, i, None)
            hg_dve(dve)
            ret_dve(dve)
            merge_dve(dve)
            dve.wait_ge(x1_ready, 4 * NT)
            layer_norm_dve(dve, 5, ln_row, lambda: dve.wait_ge(ln_in, 32))
            for i in range(NT):
                fold_dve(dve, 4, i, None)
            dve.memset(moe2.zero_i, 0).then_inc(zero_ready, 1)
            route_dve(dve, moe2)
            experts_dve(dve, moe2)
            dve.wait_ge(yg_in, 64 * NT)
            for i in range(NT):
                dve.tensor_scalar(xres[:, i, :], xres[:, i, :], ALPHA, None, ALU.mult).then_inc(*dve_own.up())
                dve.wait_ge(*dve_own.now())
                for c in range(2):
                    dve.scalar_tensor_tensor(xres[:, i, :], moe2.yg[:, c * NT + i, :], moe2.gate[:, c, i:i + 1], xres[:, i, :],
                                             ALU.mult, ALU.add).then_inc(*dve_own.up())
                    dve.wait_ge(*dve_own.now())
            layer_norm_dve(dve, 6, (moe2.rows[:, 0, :], moe2.rows[:, 1, :]), lambda: dve.wait_ge(ln2_in, 32))



def kernel(**inputs):
    import numpy as _np
    import concourse.bacc as _bacc
    from concourse import mybir as _mybir
    from concourse.bass_utils import run_bass_kernel_spmd as _run

    arrays = {}
    for name, a in inputs.items():
        a = _np.ascontiguousarray(a)
        if name not in ("g_final", "rel_bias", "hg_lb_logits_2"):
            a = a.reshape(a.shape[1:]) if a.ndim > 2 else a
        arrays[name] = a
    up = arrays.pop("w_q_up").reshape(Q_LORA, B_HEADS, NOPE + ROPE)
    arrays["w_q_up_rows"] = _np.ascontiguousarray(_np.concatenate([up, up[:, :, 80:96], up[:, :, 64:80]], 2))
    arrays["b_router"] = _np.concatenate([arrays.pop("b_router_group"), arrays.pop("b_router_expert")], 1)
    arrays["b_route_2"] = _np.concatenate([arrays.pop("b_group_2"), arrays.pop("b_router_2")], 1)
    arrays.update(constants())
    nc = _bacc.Bacc("TRN2", target_bir_lowering=False, num_devices=1)
    aps = {n: nc.dram_tensor(f"in_{n}", a.shape, _mybir.dt.from_np(a.dtype), kind="ExternalInput").ap()
           for n, a in arrays.items()}
    out = nc.dram_tensor("out", (SEQ, D), F32, kind="ExternalOutput").ap()
    build(nc, aps, out)
    r = _run(nc, [{f"in_{n}": a for n, a in arrays.items()}], core_ids=[0])
    return r.results[0]["out"].reshape(1, SEQ, D)
```

```python
from contextlib import ExitStack

import numpy as np
import concourse.bass as bass
from concourse import mybir

F32 = mybir.dt.float32
I32 = mybir.dt.int32
ALU = mybir.AluOpType
ACT = mybir.ActivationFunctionType
AX_X = mybir.AxisListType.X

P = 128
SEQ = 512
NT = SEQ // P
D = 1024
KD = D // P
EPS = 1e-6
LN_EPS = 1e-5
HUGE = 3.0e38
NEG = -1.0e30

A_HEADS, A_DIM = 8, 64
A_WIDTH = A_HEADS * A_DIM
PATTERNS = ((128, 1), (512, 4), (2048, 16))
REL_BUCKETS, REL_MAX = 32, 1024
B_HEADS, Q_LORA, KV_LORA, NOPE, ROPE, V_DIM = 8, 256, 128, 64, 32, 64
C_WIDTH = Q_LORA + KV_LORA + ROPE
PAIRS = A_HEADS // 2

G_HEADS = 8
LEVELS = 7
R_HEADS, R_DIM = 4, 256
ALPHA = 2.0 ** 0.25
HG_COLS = (0, D, 2 * D, 4 * D, 3 * D)
HG_ORDER = (0, 4, 1, 2, 3)
R_COLS = (5 * D, 6 * D, 8 * D, 7 * D)
M_COLS = (9 * D, 10 * D)
TWO_PI = (6.28125, 1.9350051879882812e-3, 3.0199159819567e-7)
ROUND = 12582912.0
PI_BELOW = 3.1415925

GROUPS, PER_GROUP = 4, 8
EXPERTS = GROUPS * PER_GROUP
LOGITS = GROUPS + EXPERTS
SLOTS = 96
BLOCKS_PER_EXPERT = -(-SEQ // SLOTS)
MOST_SPARE = 2 * SEQ // (SLOTS + 1)
SPARE = MOST_SPARE + MOST_SPARE % 2
ROWS = (EXPERTS + SPARE) * SLOTS
STEPS = 2 * NT
TOEP = SEQ + SEQ - P


class Count:

    def __init__(self, sem):
        self.sem, self.base, self.n = sem, 0, 0

    def up(self, k=1):
        self.n += k
        return self.sem, k

    def now(self):
        return self.sem, self.base + self.n

    def loop(self, i, per_turn):
        self.start, self.per_turn = self.base + self.n, per_turn
        self.base, self.n = i * per_turn + self.start, 0

    def loop_end(self, turns):
        assert self.n == self.per_turn, (self.n, self.per_turn)
        self.base, self.n = 0, self.start + turns * self.per_turn



def bucket_table():
    rel = (SEQ - 1) - np.arange(2 * SEQ)
    half, exact = REL_BUCKETS // 2, REL_BUCKETS // 4
    n = np.abs(rel)
    large = exact + (np.log(np.maximum(n, 1) / exact) / np.log(REL_MAX / exact) * (half - exact)).astype(np.int32)
    bucket = np.where(rel > 0, half, 0) + np.where(n < exact, n, np.minimum(large, half - 1))
    reach = sum(((rel % d == 0) & (n <= w // 2)).astype(np.float64) for w, d in PATTERNS)
    out = np.zeros((REL_BUCKETS + 1, 2 * SEQ), np.float32)
    out[bucket, np.arange(2 * SEQ)] = 1.0
    out[REL_BUCKETS] = np.where(reach > 0, np.log(np.maximum(reach, 1)), NEG)
    return out


def rope_tables():
    half = ROPE // 2
    inv = (10000.0 ** (-(np.arange(half) / half))).astype(np.float32)
    ang = (np.arange(SEQ, dtype=np.float32)[:, None] * inv).astype(np.float64)
    cos, sin = np.cos(ang).astype(np.float32), np.sin(ang).astype(np.float32)
    q = np.zeros((P, SEQ), np.float32)
    q[64:80], q[80:96], q[96:112], q[112:128] = cos.T, cos.T, -sin.T, sin.T
    k = np.stack([cos, sin], 1).reshape(NT, P, 2, half).transpose(1, 0, 2, 3)
    return q, np.ascontiguousarray(k)


def route_rows():
    e = np.arange(EXPERTS)
    row = np.concatenate([EXPERTS - e, GROUPS - np.arange(GROUPS), e * SLOTS,
                          np.arange(1, BLOCKS_PER_EXPERT) * SLOTS, np.arange(SPARE)]).astype(np.float32)
    return np.broadcast_to(row, (P, row.size)).copy()


def level_masks():
    x = np.arange(P)
    out = np.zeros((P, LEVELS, P), np.int32)
    for n in range(LEVELS):
        b = 1 << n
        out[:, n] = (x[:, None] // (2 * b) == x // (2 * b)) & (x[:, None] // b != x // b)
    return out


def retention_decay():
    away = np.abs(np.arange(TOEP) - (SEQ - P) - np.arange(P)[:, None])
    gamma = 1.0 - 2.0 ** (-5.0 - np.arange(R_HEADS))
    d = gamma[:, None, None] ** away * np.where(away == 0, 2.0, 1.0) * R_DIM ** -0.5
    return d.astype(np.float32)


def rotary_rates():
    rate = np.float32(1.0) / (np.float32(10000.0) ** np.linspace(0.0, 1.0, R_DIM // 2).astype(np.float32))
    return rate.astype(np.float32).reshape(P, 1)


def constants():
    rope_q, rope_k = rope_tables()
    return {
        "c_before": np.triu(np.ones((P, P), np.float32), 1),
        "c_route": route_rows(),
        "c_token": np.arange(SEQ, dtype=np.int32).reshape(NT, P).T.copy(),
        "c_masks": level_masks(),
        "c_decay": retention_decay(),
        "c_rates": rotary_rates(),
        "c_ident": np.eye(P, dtype=np.float32),
        "c_bucket": bucket_table(),
        "c_rope_q": rope_q,
        "c_rope_k": rope_k,
    }


def build(nc, A, out):
    ctx = ExitStack()
    with ctx:
        def sb(name, shape, dt=F32):
            return ctx.enter_context(nc.sbuf_tensor(name, shape, dt))

        def sem(name):
            return ctx.enter_context(nc.semaphore(name))

        bank = [ctx.enter_context(nc.psum_tensor(f"bank{b}", [P, 512], F32)) for b in range(8)]
        table_dram = nc.dram_tensor("bias_table_dram", (A_HEADS, 2 * SEQ), F32, kind="Internal").ap()

        ident = sb("ident", [P, P])
        xres = sb("xres", [P, NT, D])
        hT = sb("hT", [P, KD, SEQ])
        gains = sb("gains", [P, 3, KD])
        stat = sb("stat", [P, 64])
        stream = sb("stream", [P, 96 * 256])
        work = sb("work", [P, 19 * 1024])

        w_pair = stream[:, 0:KD * 3 * P].rearrange("p (k c n) -> p k c n", k=KD, c=3)
        w_c = stream[:, 3072:3072 + KD * C_WIDTH].rearrange("p (k n) -> p k n", k=KD)
        w_up_q = stream[:, 6400:6400 + 2 * 2 * P].rearrange("p (c j m) -> p c j m", c=2, j=2)
        w_up_k = stream[:, 6912:6912 + 2 * NOPE].rearrange("p (j m) -> p j m", j=2)
        w_up_v = stream[:, 7168:7168 + B_HEADS * V_DIM]
        w_o = stream[:, 8192:8192 + KD * D].rearrange("p (k n) -> p k n", k=KD)

        def cut(start, *shape):
            n = int(np.prod(shape))
            ap = work[:, start:start + n]
            if len(shape) == 1:
                return ap, start + n
            letters = "abcd"[:len(shape)]
            spec = f"p ({' '.join(letters)}) -> p {' '.join(letters)}"
            return ap.rearrange(spec, **{l: s for l, s in zip(letters, shape)}), start + n

        at = 0
        outAB, at = cut(at, NT, D)
        ctok, _ = cut(at, NT, C_WIDTH)
        toep, at = cut(at, 2, TOEP)
        qT, at = cut(at, 2, SEQ)
        kT, at = cut(at, 2, SEQ)
        v, at = cut(at, NT, A_WIDTH)
        xn_at = at
        sc, at = cut(at, 2, SEQ)
        prob, at = cut(at, 2, SEQ)
        probT, at = cut(at, 2, NT, P)
        cn, at = cut(at, NT, Q_LORA + KV_LORA + 96)
        cqT, at = cut(at, 3, SEQ)
        zeros, at = cut(at, SEQ)
        rope_q, at = cut(at, SEQ)
        rope_k, at = cut(at, NT, 2, ROPE // 2)
        rope_t, at = cut(at, NT, 4, ROPE // 2)
        rsum = sb("rsum", [P, 8])
        rinv = sb("rinv", [P, 8])
        held = sb("held", [P, STEPS])
        nmax = sb("nmax", [P, 8])
        xn = work[:, xn_at:xn_at + 2 * D].rearrange("p (a d) -> p a d", a=2)
        rope_s, at = cut(at, 2, SEQ)
        gains_c = sb("gains_c", [P, 3])
        v_pair = v[:, :, 0:P]

        def v_mla(pair, j, kc):
            return v[:, kc, bass.ds(pair * P + j * V_DIM, V_DIM)]

        def toep_tile(j, i):
            ap = toep[:, j, i * P:i * P + SEQ]
            return bass.AP(ap.tensor, ap.offset + SEQ - 1, [list(ap.ap[0]), [-1, SEQ]])

        onehot = work[0:REL_BUCKETS + 1, 0:2 * SEQ]
        table = work[0:A_HEADS, 2 * SEQ:4 * SEQ]
        relb = work[0:REL_BUCKETS + 1, 4 * SEQ:4 * SEQ + A_HEADS]
        junk = probT[:, :, :, :].rearrange("p a b c -> p (a b c)")

        ones = sb("ones", [P, P])
        before = stream[:, 22528:22656]
        route = stream[:, 22656:22656 + 121 + 1][:, 0:LOGITS + EXPERTS + BLOCKS_PER_EXPERT - 1 + SPARE]
        token = sb("token", [P, NT], I32)
        w_r1 = stream[:, 22784:22784 + KD * LOGITS].rearrange("p (k n) -> p k n", k=KD)
        b_r1 = stream[:, 23072:23072 + LOGITS]
        g_row = stream[:, 23552:24576]

        x_out = [sem(f"x_out{i}") for i in range(NT)]
        (r_in, lg_done, exp_in, exp_out, picked, rank_done, routed, list_zero, zero_ready, listed, list_in, rows_seen, yg_in0,
         cleared, passed, yg_in1, mixed) = (sem(n) for n in (
            "r_in lg_done exp_in exp_out picked rank_done routed list_zero zero_ready listed list_in rows_seen yg_in0 cleared"
            " passed yg_in1 mixed").split())
        masks = sb("masks", [P, LEVELS, P], mybir.dt.uint8)
        masks_wide = hT[:, 0:2, :].rearrange("p a b -> p (a b)")[:, 0:LEVELS * P].bitcast(I32)
        head_row = sb("head_row", [P, 6, G_HEADS])

        oTh, at = cut(0, G_HEADS, SEQ)
        oTr, at = cut(at, 2 * R_HEADS, SEQ)
        stage_at = at
        x_at = at
        X, at = cut(at, 4, SEQ)
        t_at = at
        T, at = cut(at, 2, SEQ)
        ksum, at = cut(at, SEQ)
        Q, at = cut(at, SEQ)
        F, at = cut(at, 2, SEQ)
        sig, at = cut(at, SEQ)
        sqr, at = cut(at, SEQ)
        root, at = cut(at, SEQ)
        gate, at = cut(at, SEQ)
        V, at = cut(at, NT, P)
        attn_at = at
        attnT, at = cut(at, NT, SEQ)
        assert at <= 19 * 1024
        rq, at = cut(x_at, 2, SEQ)
        rk, at = cut(at, 2, SEQ)
        assert at == t_at
        rV, at = cut(at, NT, R_DIM)
        rgate, at = cut(at, 2, SEQ)
        rtmp, at = cut(at, 2, SEQ)
        decay, _ = cut(at, TOEP)
        rsq, at = cut(at + 2 * SEQ, 2, SEQ)
        rroot, at = cut(at, SEQ)
        assert at == attn_at
        rattn, at = cut(at, NT, SEQ)
        cosr, sinr, ang, turns_ = (stream[:, 20480 + n * SEQ:20480 + (n + 1) * SEQ] for n in range(4))
        merged, at = cut(stage_at, KD, SEQ)
        msig, at = cut(at, 2, 2, SEQ)
        mtmp, at = cut(at, 2, 2, SEQ)
        w_hg = stream[:, 6144:6144 + 5 * D].rearrange("p (c k n) -> p c k n", c=5, k=KD)
        w_ret = stream[:, 11264:11264 + 8 * D].rearrange("p (c k n) -> p c k n", c=4, k=KD)
        w_mrg = stream[:, 0:8 * D].rearrange("p (s c k n) -> p s c k n", s=2, c=4, k=KD)
        w_o2 = stream[:, 8192:8192 + 8 * D].rearrange("p (k n) -> p k n", k=KD)
        ln_row = [g_row, stream[:, 19456:20480]]
        bn = sb("bn", [P, NT, 2, 6])
        mv = sb("mv", [P, NT, 2])
        rates = sb("rates", [P, 1])

        lb_in, h_copy, r_tmp = sem("lb_in"), sem("h_copy"), sem("r_tmp")
        hg_in = [sem(f"hg_in{c}") for c in range(5)]
        lb_ready = sem("lb_ready")
        (hp_done, h_sig, h_F, h_V, h_q, h_gate, h_init, l_done, h_upd, h_base, h_far, h_av, h_sq, h_nm, h_var,
         h_root, h_fin) = (sem(n) for n in ("hp_done h_sig h_F h_V h_q h_gate h_init l_done h_upd h_base h_far h_av"
                                            " h_sq h_nm h_var h_root h_fin").split())
        ret_in = [sem(f"ret_in{c}") for c in range(4)]
        (decay_in, pos_in, ang_ready, rot_ready, rp_done, rr_q, rr_k, r_sig, r_gate, r_V, rs_done, r_dec, r_av, r_sq, r_nm,
         r_var, r_root, r_fin) = (sem(n) for n in ("decay_in pos_in ang_ready rot_ready rp_done rr_q rr_k r_sig r_gate r_V"
                                  " rs_done r_dec r_av r_sq r_nm r_var r_root r_fin").split())
        mrg_in = [sem("mrg_in0"), sem("mrg_in1")]
        w_o2_in, ln_in, ln2_in, m_done, m_sig, m_ready, ln_ready = (
            sem(n) for n in "w_o2_in ln_in ln2_in m_done m_sig m_ready ln_ready".split())
        zeros_ready = sem("zeros_ready")
        route_in, g_row_in, ones_ready, fin_ready = sem("route_in"), sem("g_row_in"), sem("ones_ready"), sem("fin_ready")
        x_in = [sem(f"x_in{i}") for i in range(NT)]
        gains_in, rope_in = sem("gains_in"), sem("rope_in")
        bias_in, table_out, toep_in = sem("bias_in"), sem("table_out"), sem("toep_in")
        w_pair_in, w_c_in, w_up_in, w_o_in = (sem(n) for n in ("w_pair_in", "w_c_in", "w_up_in", "w_o_in"))
        dve_own, act_own = Count(sem("dve_own")), Count(sem("act_own"))
        ones_row, table_mm, table_ready = sem("ones_row"), sem("table_mm"), sem("table_ready")
        sq_ready, normed, tr_done, hT_ready = (sem(n) for n in ("sq_ready", "normed", "tr_done", "hT_ready"))
        var_ready, root_ready = sem("var_ready"), sem("root_ready")
        proj_done, q_ready, k_ready, v_ready = (sem(n) for n in ("proj_done", "q_ready", "k_ready", "v_ready"))
        s_done, biased, exp_done, pT_done, pT_ready, av_done, o_ready = (
            sem(n) for n in ("s_done", "biased", "exp_done", "pT_done", "pT_ready", "av_done", "o_ready"))
        c_done, c_ready, cn_ready, ct_done, ct_ready = (
            sem(n) for n in ("c_done", "c_ready", "cn_ready", "ct_done", "ct_ready"))
        rope_done, q_roped = sem("rope_done"), sem("q_roped")
        up_done, vb_done, vb_ready = sem("up_done"), sem("vb_done"), sem("vb_ready")
        wo_done, x1_ready, final_out = sem("wo_done"), sem("x1_ready"), sem("final_out")

        block = ctx.enter_context(nc.Block())


        def core_pe(pe, pair, done, keys, inputs):
            lhs, rhs, vcols = keys
            for m in range(STEPS + 3):
                if m < STEPS:
                    j, i = divmod(m, NT)
                    base = pair * STEPS + done
                    if m == 0:
                        inputs()
                    if m >= 2:
                        pe.wait_ge(biased, base + m - 1)
                    pe.matmul(bank[m % 2][:, :], lhs(j, i), rhs(j), start=True, stop=True).then_inc(s_done, 1)
                n = m - 2
                if 0 <= n < STEPS:
                    pe.wait_ge(exp_done, base + n + 1)
                    if n >= 2:
                        pe.wait_ge(pT_ready, base + n - 1)
                    for kc in range(NT):
                        last = pe.transpose(bank[2 + n % 2][:, kc * P:(kc + 1) * P],
                                            prob[:, n % 2, kc * P:(kc + 1) * P], ident[:, :])
                    last.then_inc(pT_done, 1)
                n = m - 3
                if 0 <= n < STEPS:
                    pe.wait_ge(pT_ready, base + n + 1)
                    if n >= 2:
                        pe.wait_ge(o_ready, base + n - 1)
                    for kc in range(NT):
                        last = pe.matmul(bank[4 + n % 2][:, 0:A_DIM], probT[:, n % 2, kc, :], vcols(n // NT, kc),
                                         start=kc == 0, stop=kc == NT - 1)
                    last.then_inc(av_done, 1)

        def core_dve(dve, pair, done, bias, scale):
            base = pair * STEPS + done
            for m in range(STEPS + 2):
                if m < STEPS:
                    dve.wait_ge(s_done, base + m + 1)
                    if m >= 2:
                        dve.wait_ge(exp_done, base + m - 1)
                    dve.memset(held[:, m:m + 1], 0.0)
                    dve.tensor_tensor_reduce(sc[:, m % 2, :], bank[m % 2][:, :], bias(m // NT, m % NT),
                                             -scale, HUGE, ALU.add, ALU.min,
                                             nmax[:, m:m + 1]).then_inc(biased, 1)
                n = m - 2
                if 0 <= n < STEPS:
                    dve.wait_ge(exp_done, base + n + 1)
                    dve.reciprocal(rinv[:, n:n + 1], rsum[:, n:n + 1])
                    dve.wait_ge(pT_done, base + n + 1)
                    if n >= 2:
                        dve.wait_ge(av_done, base + n - 1)
                    dve.tensor_copy(probT[:, n % 2, :, :],
                                    bank[2 + n % 2][:, :].rearrange("p (a b) -> p a b", a=NT)).then_inc(pT_ready, 1)

        def core_act(act, pair, done, col):
            base = pair * STEPS + done
            for m in range(STEPS + 2):
                if m < STEPS:
                    act.wait_ge(biased, base + m + 1)
                    if m >= 2:
                        act.wait_ge(pT_done, base + m - 1)
                    act.activation(prob[:, m % 2, :], sc[:, m % 2, :], ACT.Exp, bias=nmax[:, m:m + 1], scale=-1.0,
                                   accum_out=rsum[:, m:m + 1]).then_inc(exp_done, 1)
                n = m - 2
                if 0 <= n < STEPS:
                    act.wait_ge(av_done, base + n + 1)
                    act.wait_ge(pT_ready, base + n + 1)
                    act.activation(outAB[:, n % NT, bass.ds(col + (n // NT) * A_DIM, A_DIM)], bank[4 + n % 2][:, 0:A_DIM],
                                   ACT.Copy, scale=rinv[:, n:n + 1]).then_inc(o_ready, 1)


        roots_before = (0, 1, 2, 3, 3 + NT, 4 + NT, 4 + 2 * NT)

        def norm_act(act, r, src, groups, waits, junk=junk):
            w = D // groups
            for i in range(NT):
                waits(act, i)
                for g in range(groups):
                    act.activation(junk[:, 0:w], src(i)[:, g * w:(g + 1) * w], ACT.Square,
                                   accum_out=stat[:, i * groups + g:i * groups + g + 1]).then_inc(*act_own.up())
                    act.wait_ge(*act_own.now())
            act.sem_inc(sq_ready, 1)
            root_act(act, r, NT * groups)

        def root_act(act, s, cols):
            act.wait_ge(var_ready, roots_before[s] + 1)
            act.activation(stat[:, 0:cols], stat[:, 0:cols], ACT.Sqrt).then_inc(root_ready, 1)

        def root_dve(dve, s, cols, w, eps):
            dve.wait_ge(sq_ready, roots_before[s] + 1)
            dve.tensor_scalar(stat[:, 0:cols], stat[:, 0:cols], 1.0 / w, eps, ALU.mult, ALU.add).then_inc(var_ready, 1)
            dve.wait_ge(root_ready, roots_before[s] + 1)
            dve.reciprocal(stat[:, 0:cols], stat[:, 0:cols]).then_inc(*dve_own.up())
            dve.wait_ge(*dve_own.now())

        def norm_dve(dve, s, r, src, groups, gain, free=lambda i: None):
            w = D // groups
            root_dve(dve, r, NT * groups, w, EPS)
            for i in range(NT):
                if i >= 2:
                    dve.wait_ge(tr_done, (s * NT + i - 2) * 2 + 2)
                    free(i)
                for g in range(groups):
                    last = dve.tensor_scalar(xn[:, i % 2, g * w:(g + 1) * w], src(i)[:, g * w:(g + 1) * w],
                                             stat[:, i * groups + g:i * groups + g + 1], None, ALU.mult)
                last.then_inc(normed, 1)
                if i >= 1:
                    fold_dve(dve, s, i - 1, gain)
            fold_dve(dve, s, NT - 1, gain)

        def fold_dve(dve, s, i, gain):
            for h in range(2):
                dve.wait_ge(tr_done, (s * NT + i) * 2 + h + 1)
                src = bank[4 + (i % 2) * 2 + h][:, :].rearrange("p (a b) -> p a b", a=NT)
                dst = hT[:, 4 * h:4 * h + 4, i * P:(i + 1) * P]
                if gain is None:
                    dve.tensor_copy(dst, src).then_inc(hT_ready, 1)
                else:
                    dve.tensor_tensor(dst, src, gain[:, 4 * h:4 * h + 4].unsqueeze(2).to_broadcast([P, 4, P]),
                                      ALU.mult).then_inc(hT_ready, 1)

        def transposes_pe(pe, s, i, src, waits):
            waits(pe, i)
            for h in range(2):
                if i >= 2:
                    pe.wait_ge(hT_ready, (s * NT + i - 2) * 2 + h + 1)
                for k in range(4):
                    last = pe.transpose(bank[4 + (i % 2) * 2 + h][:, k * P:(k + 1) * P],
                                        src(i)[:, 4 * h + k:D:KD], ident[:, :])
                last.then_inc(tr_done, 1)

        def norm_pe(pe, s, src, waits):
            for i in range(NT):
                transposes_pe(pe, s, i, src, waits)

        def xn_ready(s):
            return lambda pe, i: pe.wait_ge(normed, s * NT + i + 1)


        class Moe:

            def __init__(m, layer, ff, weights, slot_at, smalls, pool_at):
                m.layer, m.ff, m.fc = layer, ff, ff // P
                m.w_gate, m.w_up, m.w_down = (A[w] for w in weights)
                size = 3 * KD * ff
                m.wg = [stream[:, a:a + KD * ff].rearrange("p (k f) -> p k f", k=KD) for a in slot_at]
                m.wu = [stream[:, a + KD * ff:a + 2 * KD * ff].rearrange("p (k f) -> p k f", k=KD) for a in slot_at]
                m.wd = [stream[:, a + 2 * KD * ff:a + size].rearrange("p (c n) -> p c n", c=m.fc) for a in slot_at]
                m.w_r, m.b_r = smalls
                at = pool_at
                m.xg, at = cut(at, 2, D)
                m.xgT, at = cut(at, 2, KD, SLOTS)
                m.sg, at = cut(at, 2, SLOTS)
                m.h, at = cut(at, 2, m.fc, SLOTS)
                m.y, at = cut(at, 2, D)
                m.yg, at = cut(at, 2 * NT, D)
                m.lg, at = cut(at, NT, LOGITS)
                m.a1, at = cut(at, NT, EXPERTS)
                m.a2, at = cut(at, NT, EXPERTS)
                m.aa, at = cut(at, NT, EXPERTS)
                m.me, at = cut(at, NT, EXPERTS)
                m.t1, at = cut(at, NT, EXPERTS)
                m.goh, at = cut(at, NT, GROUPS)
                m.gt, at = cut(at, NT, GROUPS)
                m.ex, at = cut(at, NT, 5)
                m.mx, at = cut(at, 8, NT)
                m.gate, at = cut(at, 2, NT)
                m.cnt, at = cut(at, EXPERTS)
                m.nov, at = cut(at, EXPERTS)
                m.ove, at = cut(at, EXPERTS)
                m.dif, at = cut(at, EXPERTS)
                m.cmp, at = cut(at, EXPERTS, BLOCKS_PER_EXPERT - 1)
                m.cmb, at = cut(at, SPARE, EXPERTS)
                m.dest, at = cut(at, 2, NT)
                m.blk, at = cut(at, SPARE + 3)
                m.one, at = cut(at, EXPERTS)
                m.dest_i, at = cut(at, 2 * NT)
                m.blk_i, at = cut(at, SPARE + 3)
                m.list_i, at = cut(at, EXPERTS + SPARE)
                m.zero_i, at = cut(at, SLOTS)
                m.rows, at = cut(at, 2, D)
                assert at <= 19 * 1024, at
                m.dest_i, m.blk_i, m.list_i, m.zero_i = (x.bitcast(I32) for x in (m.dest_i, m.blk_i, m.list_i, m.zero_i))
                m.x_dram = nc.dram_tensor(f"x_rows{layer}", (SEQ, D), F32, kind="Internal").ap()
                m.y_dram = nc.dram_tensor(f"y_rows{layer}", (ROWS, D), F32, kind="Internal").ap()
                m.list_dram = nc.dram_tensor(f"token_list{layer}", (ROWS, 1), I32, kind="Internal").ap()
                (m.xt_done, m.xt_ready, m.gu_done, m.sg_ready, m.h_ready, m.d_done, m.y_ready) = (
                    sem(f"{n}_{layer}") for n in "xt_done xt_ready gu_done sg_ready h_ready d_done y_ready".split())
                m.xg_in, m.gu_in, m.y_out = ([sem(f"{n}{i}_{layer}") for i in range(2)] for n in ("xg_in", "gu_in", "y_out"))
                m.down_in = x_in[2 * layer - 2:2 * layer]
                m.past = layer - 1

        moe1 = Moe(1, 256, ("w_gate", "w_up", "w_down"), (16384, 0), (w_r1, b_r1), 0)
        moe1.gain = gains[:, 2, :]
        moe2 = Moe(2, 512, ("w1_2", "w3_2", "w2_2"), (0, 12288), (w_r1, b_r1), 0)
        moe2.gain = None
        r_key = route[:, 0:EXPERTS]
        r_gkey = route[:, EXPERTS:LOGITS]
        r_first = route[:, LOGITS:LOGITS + EXPERTS]
        r_limit = route[:, LOGITS + EXPERTS:LOGITS + EXPERTS + BLOCKS_PER_EXPERT - 1]
        r_block = route[:, LOGITS + EXPERTS + BLOCKS_PER_EXPERT - 1:]

        def route_pe(pe, m):
            pe.wait_ge(picked, m.past + 1)
            for i in range(NT):
                for j in range(i + 1):
                    pe.matmul(bank[1][:, i * EXPERTS:(i + 1) * EXPERTS], before[:, :] if j == i else ones[:, :],
                              m.aa[:, j, :], start=j == 0, stop=j == i)
            for j in range(NT):
                last = pe.matmul(bank[1][:, NT * EXPERTS:(NT + 1) * EXPERTS], ones[:, :], m.aa[:, j, :], start=j == 0,
                                 stop=j == NT - 1)
            last.then_inc(rank_done, 1)

        def route_act(act, m):
            act.wait_ge(exp_in, m.past + 1)
            act.activation(m.ex[:, :, :], m.ex[:, :, :], ACT.Exp).then_inc(exp_out, 1)

        def route_dve(dve, m):
            def step(ins):
                ins.then_inc(*dve_own.up())
                dve.wait_ge(*dve_own.now())

            def over(x, n):
                return x.unsqueeze(2).to_broadcast([P, NT, n])

            def rows(r, n):
                return r.unsqueeze(1).to_broadcast([P, NT, n])

            def first_of_equals(out, x, top, key, n, tmp):
                step(dve.tensor_reduce(top, x, AX_X, ALU.max))
                step(dve.tensor_tensor(tmp, x, over(top, n), ALU.is_equal))
                step(dve.tensor_tensor(tmp, tmp, rows(key, n), ALU.mult))
                step(dve.tensor_reduce(m.mx[:, 7, :], tmp, AX_X, ALU.max))
                step(dve.tensor_tensor(out, rows(key, n), over(m.mx[:, 7, :], n), ALU.is_equal))

            gl, el = m.lg[:, :, 0:GROUPS], m.lg[:, :, GROUPS:]
            dve.wait_ge(lg_done, m.past + 1)
            dve.wait_ge(r_in, 48 * m.past + 48)
            step(dve.tensor_tensor(m.lg[:, :, :], bank[0][:, 0:NT * LOGITS].rearrange("p (a b) -> p a b", a=NT),
                                   rows(m.b_r, LOGITS), ALU.add))
            first_of_equals(m.goh, gl, m.mx[:, 0, :], r_gkey, GROUPS, m.gt)
            step(dve.tensor_tensor(m.ex[:, :, 0:GROUPS], gl, over(m.mx[:, 0, :], GROUPS), ALU.subtract))
            step(dve.tensor_scalar(m.gt, m.goh, -NEG, NEG, ALU.mult, ALU.add))
            four = lambda x: x.rearrange("p a (g e) -> p a g e", g=GROUPS)
            wide = lambda x: x.unsqueeze(3).to_broadcast([P, NT, GROUPS, PER_GROUP])
            step(dve.tensor_tensor(four(m.me), four(el), wide(m.goh), ALU.mult))
            step(dve.tensor_tensor(four(m.me), four(m.me), wide(m.gt), ALU.add))
            first_of_equals(m.a1, m.me, m.mx[:, 1, :], r_key, EXPERTS, m.t1)
            step(dve.tensor_scalar(m.t1, m.a1, 2 * NEG, None, ALU.mult))
            step(dve.tensor_tensor(m.me, m.me, m.t1, ALU.add))
            first_of_equals(m.a2, m.me, m.mx[:, 2, :], r_key, EXPERTS, m.t1)
            dve.tensor_tensor(m.aa, m.a1, m.a2, ALU.add).then_inc(picked, 1)
            dve.tensor_tensor(m.ex[:, :, GROUPS], m.mx[:, 2, :], m.mx[:, 1, :], ALU.subtract).then_inc(exp_in, 1)
            dve.wait_ge(exp_out, m.past + 1)
            step(dve.tensor_reduce(m.mx[:, 3, :], m.ex[:, :, 0:GROUPS], AX_X, ALU.add))
            step(dve.tensor_scalar(m.mx[:, 4, :], m.ex[:, :, GROUPS], 1.0, None, ALU.add))
            step(dve.tensor_tensor(m.mx[:, 3, :], m.mx[:, 3, :], m.mx[:, 4, :], ALU.mult))
            step(dve.reciprocal(m.gate[:, 0, :], m.mx[:, 3, :]))
            step(dve.tensor_tensor(m.gate[:, 1, :], m.gate[:, 0, :], m.ex[:, :, GROUPS], ALU.mult))
            dve.wait_ge(rank_done, m.past + 1)
            rank = bank[1][:, 0:NT * EXPERTS].rearrange("p (a b) -> p a b", a=NT)
            step(dve.tensor_copy(m.cnt, bank[1][:, NT * EXPERTS:(NT + 1) * EXPERTS]))
            lim = BLOCKS_PER_EXPERT - 1
            step(dve.tensor_tensor(m.cmp, m.cnt.unsqueeze(2).to_broadcast([P, EXPERTS, lim]),
                                   r_limit.unsqueeze(1).to_broadcast([P, EXPERTS, lim]), ALU.is_gt))
            step(dve.tensor_reduce(m.nov, m.cmp, AX_X, ALU.add))
            step(dve.memset(m.one, 1.0))
            step(dve.tensor_tensor_scan(m.ove, m.one, m.nov, 0.0, ALU.mult, ALU.add))
            step(dve.tensor_tensor(m.dif, m.ove, m.nov, ALU.subtract))
            step(dve.tensor_scalar(m.dif, m.dif, float(SLOTS), float((EXPERTS - 1) * SLOTS), ALU.mult, ALU.add))
            step(dve.tensor_tensor(m.dif, m.dif, r_first, ALU.subtract))
            step(dve.tensor_scalar(m.t1, rank, float(SLOTS), None, ALU.is_ge))
            step(dve.tensor_tensor(m.t1, m.t1, rows(m.dif, EXPERTS), ALU.mult))
            step(dve.tensor_tensor(m.t1, m.t1, rank, ALU.add))
            step(dve.tensor_tensor(m.t1, m.t1, rows(r_first, EXPERTS), ALU.add))
            for c, a in enumerate((m.a1, m.a2)):
                step(dve.tensor_tensor(m.me, m.t1, a, ALU.mult))
                step(dve.tensor_reduce(m.dest[:, c, :], m.me, AX_X, ALU.add))
            dve.tensor_copy(m.dest_i, m.dest.rearrange("p a b -> p (a b)")).then_inc(routed, 1)
            step(dve.tensor_tensor(m.cmb, m.ove.unsqueeze(1).to_broadcast([P, SPARE, EXPERTS]),
                                   r_block.unsqueeze(2).to_broadcast([P, SPARE, EXPERTS]), ALU.is_le))
            step(dve.tensor_reduce(m.blk[:, 0:SPARE], m.cmb, AX_X, ALU.add))
            step(dve.tensor_scalar(m.blk[:, 0:SPARE], m.blk[:, 0:SPARE], EXPERTS - 1.0, None, ALU.min))
            step(dve.tensor_copy(m.blk[:, SPARE:SPARE + 1], m.ove[:, EXPERTS - 1:EXPERTS]))
            dve.tensor_copy(m.blk_i[:, 0:SPARE + 1], m.blk[:, 0:SPARE + 1]).then_inc(routed, 1)

        def route_pool(pool, m):
            pool.wait_ge(routed, 2 * m.past + 1)
            pool.wait_ge(list_zero, 16 * m.past + 16)
            pool.wait_ge(route_in, 48)
            for c in range(2):
                for i in range(NT):
                    pool.indirect_dma_start(
                        out=m.list_dram, out_offset=bass.IndirectOffsetOnAxis(ap=m.dest_i[:, c * NT + i:c * NT + i + 1], axis=0),
                        in_=token[:, i:i + 1], in_offset=None).then_inc(listed, 16)

        def clear_list(sp, m):
            sp.wait_ge(zero_ready, m.past + 1)
            sp.dma_start(m.list_dram.rearrange("(e s) a -> e (s a)", s=SLOTS), m.zero_i[0:EXPERTS + SPARE, :]).then_inc(list_zero, 16)

        def list_sp(sp, m):
            sp.wait_ge(listed, 32 * NT * (m.past + 1))
            sp.dma_start(m.list_i[0:SLOTS, :], m.list_dram.rearrange("(e s) a -> s (e a)", s=SLOTS),
                         allow_slow_non_contiguous=True).then_inc(list_in, 16)

        def clear_spare_rows(sp, m):
            rows = m.y_dram[EXPERTS * SLOTS:, :].rearrange("(p r) (a n) -> p (r a n)", p=P // 2, n=SEQ)
            sp.dma_start(rows.rearrange("p (r n) -> p r n", n=SEQ),
                         zeros[0:P // 2, :].unsqueeze(1).to_broadcast([P // 2, SPARE * SLOTS * D // SEQ * 2 // P, SEQ])
                         ).then_inc(cleared, 16)

        def load_gate_up(sp, m, e, s):
            for slot, w in ((m.wg[s], m.w_gate), (m.wu[s], m.w_up)):
                sp.dma_start(slot, w[bass.ds(e, 1)].rearrange("a (p k) f -> (a p) k f", k=KD)).then_inc(m.gu_in[s], 16)

        def load_down(sp, m, e, s):
            sp.dma_start(m.wd[s], m.w_down[bass.ds(e, 1)].rearrange("a (p c) n -> (a p) c n", c=m.fc)).then_inc(m.down_in[s], 16)

        def load_expert(sp, m, e, s):
            load_gate_up(sp, m, e, s)
            load_down(sp, m, e, s)

        def turns(eng, body):
            for s in range(2):
                body(0, s, True, False)
            with eng.Fori(1, EXPERTS // 2 - 1) as i:
                for s in range(2):
                    body(i, s, False, False)
            for s in range(2):
                body(EXPERTS // 2 - 1, s, False, True)

        def blocks_needed(eng, m):
            eng.wait_ge(routed, 2 * m.past + 2)
            return eng.value_load(m.blk_i[0:1, SPARE:SPARE + 1], min_val=0, max_val=MOST_SPARE)

        def spare(eng, need, body):
            with eng.Fori(0, SPARE // 2) as j:
                for s in range(2):
                    with eng.If(need > j * 2 + s):
                        body(j + EXPERTS // 2, s)

        def experts_sp(sp, m):
            def reload(n, s, expert):
                e = expert()
                sp.wait_ge(m.gu_done, n * m.fc + m.fc)
                load_gate_up(sp, m, e, s)
                sp.wait_ge(m.d_done, n + 1)
                load_down(sp, m, e, s)

            def store(n, s):
                sp.wait_ge(m.y_ready, n * 2 + 2)
                sp.dma_start(m.y_dram[bass.ds(n * SLOTS, SLOTS), :], m.y[0:SLOTS, s, :]).then_inc(m.y_out[s], 16)

            def spare_expert(b):
                return sp.value_load(m.blk_i[0:1, bass.ds(b, 1)], min_val=0, max_val=EXPERTS - 1)

            def body(i, s, first, last):
                n = i * 2 + s
                if last:
                    with sp.If(need > s):
                        reload(n, s, lambda: spare_expert(s))
                else:
                    reload(n, s, lambda: n + 2)
                store(n, s)

            def further(i, s):
                n = i * 2 + s
                with sp.If(need > n - (EXPERTS - 2)):
                    reload(n, s, lambda: spare_expert(n - (EXPERTS - 2)))
                store(n, s)

            need = blocks_needed(sp, m)
            sp.wait_ge(cleared, 32)
            turns(sp, body)
            spare(sp, need, further)

        def experts_pool(pool, m):
            pool.wait_ge(list_in, 16 * m.past + 16)
            for tile_out in x_out:
                pool.wait_ge(tile_out, 16 * m.past + 16)
            for n in range(EXPERTS):
                if n >= 2:
                    pool.wait_ge(m.xt_done, n - 1)
                pool.indirect_dma_start(
                    out=m.xg[0:SLOTS, n % 2, :], out_offset=None, in_=m.x_dram,
                    in_offset=bass.IndirectOffsetOnAxis(ap=m.list_i[0:SLOTS, n:n + 1], axis=0)).then_inc(m.xg_in[n % 2], 16)
            pool.wait_ge(routed, 2 * m.past + 2)
            need = pool.value_load(m.blk_i[0:1, SPARE:SPARE + 1], min_val=0, max_val=MOST_SPARE)
            for b in range(MOST_SPARE):
                with pool.If(need > b):
                    pool.wait_ge(m.xt_done, EXPERTS + b - 1)
                    pool.indirect_dma_start(
                        out=m.xg[0:SLOTS, b % 2, :], out_offset=None, in_=m.x_dram,
                        in_offset=bass.IndirectOffsetOnAxis(ap=m.list_i[0:SLOTS, EXPERTS + b:EXPERTS + b + 1],
                                                            axis=0)).then_inc(m.xg_in[b % 2], 16)
            for s in range(2):
                pool.wait_ge(m.y_out[s], 16 * EXPERTS // 2)
                pool.sem_inc(rows_seen, 1)
            for b in reversed(range(MOST_SPARE)):
                with pool.If(need > b):
                    pool.wait_ge(m.y_out[b % 2], 16 * (EXPERTS // 2 + b // 2 + 1))
                    pool.sem_inc(rows_seen, 1)
            for i in range(NT):
                for c in range(2):
                    pool.indirect_dma_start(
                        out=m.yg[:, c * NT + i, :], out_offset=None, in_=m.y_dram,
                        in_offset=bass.IndirectOffsetOnAxis(ap=m.dest_i[:, c * NT + i:c * NT + i + 1], axis=0)
                    ).then_inc((yg_in0, yg_in1)[i // 2], 16)

        def tokens_pe(pe, m, s):
            for k in range(KD):
                last = pe.transpose(bank[s + 6 * (k // 4)][:, k % 4 * SLOTS:(k % 4 + 1) * SLOTS], m.xg[0:SLOTS, s, k:D:KD],
                                    ident[0:SLOTS, 0:SLOTS])
            last.then_inc(m.xt_done, 1)

        def hidden_pe(pe, m, s, n, waited):
            for c in range(m.fc):
                if not (waited and c < 2):
                    pe.wait_ge(m.h_ready, n * m.fc + c - 1)
                for w, at in ((m.wg, 0), (m.wu, 256)):
                    for k in range(KD):
                        last = pe.matmul(bank[2 + c % 2][:, at:at + SLOTS], w[s][:, k, c::m.fc], m.xgT[:, s, k, :],
                                         start=k == 0, stop=k == KD - 1)
                last.then_inc(m.gu_done, 1)

        def down_pe(pe, m, i, s, waited):
            n = i * 2 + s
            pe.wait_ge(m.down_in[s], i * 16 + 32)
            if not waited:
                pe.wait_ge(m.y_ready, n * 2)
            for c in range(m.fc):
                pe.wait_ge(m.h_ready, n * m.fc + c + 1)
                for half in range(2):
                    last = pe.matmul(bank[4 + half][0:SLOTS, :], m.h[:, s, c, :], m.wd[s][:, c, half * 512:(half + 1) * 512],
                                     start=c == 0, stop=c == m.fc - 1)
            last.then_inc(m.d_done, 1)

        def experts_pe(pe, m):
            pe.wait_ge(m.xg_in[0], 16)
            tokens_pe(pe, m, 0)

            def body(i, s, first, last):
                e = i * 2 + s
                if not (last and s == 1):
                    pe.wait_ge(m.xg_in[1 - s], (i + s) * 16 + 16)
                pe.wait_ge(m.xt_ready, e + 1)
                pe.wait_ge(m.gu_in[s], i * 32 + 32)
                hidden_pe(pe, m, s, e, first and s == 0)
                if not (last and s == 1):
                    tokens_pe(pe, m, 1 - s)
                down_pe(pe, m, i, s, first and s == 0)

            turns(pe, body)

            def further(i, s):
                n = i * 2 + s
                pe.wait_ge(m.xg_in[s], i * 16 + 16)
                pe.sem_inc(passed, 1)
                tokens_pe(pe, m, s)
                pe.wait_ge(m.xt_ready, n + 1)
                pe.wait_ge(m.gu_in[s], i * 32 + 32)
                hidden_pe(pe, m, s, n, False)
                down_pe(pe, m, i, s, False)

            spare(pe, blocks_needed(pe, m), further)

        def block_act(act, m, s, n, y_free, waited):
            for c in range(m.fc):
                act.wait_ge(m.gu_done, n * m.fc + c + 1)
                if not (waited and c < 2):
                    act.wait_ge(m.h_ready, n * m.fc + c - 1)
                act.activation(m.sg[:, c % 2, :], bank[2 + c % 2][:, 0:SLOTS], ACT.Silu).then_inc(m.sg_ready, 1)
            act.wait_ge(m.d_done, n + 1)
            y_free(act)
            act.activation(m.y[0:SLOTS, s, 0:512], bank[4][0:SLOTS, :], ACT.Copy).then_inc(m.y_ready, 1)

        def tokens_dve(dve, m, s, n):
            dve.wait_ge(m.xt_done, n + 1)
            for half in range(2):
                src = bank[s + 6 * half][:, 0:4 * SLOTS].rearrange("p (k t) -> p k t", k=4)
                dst = m.xgT[:, s, 4 * half:4 * half + 4, :]
                if m.gain is None:
                    last = dve.tensor_copy(dst, src)
                else:
                    last = dve.tensor_tensor(dst, src, m.gain[:, 4 * half:4 * half + 4].unsqueeze(2).to_broadcast([P, 4, SLOTS]),
                                             ALU.mult)
            last.then_inc(m.xt_ready, 1)

        def block_dve(dve, m, s, n, y_free, tokens):
            for c in range(m.fc):
                dve.wait_ge(m.sg_ready, n * m.fc + c + 1)
                dve.tensor_tensor(m.h[:, s, c, :], bank[2 + c % 2][:, 256:256 + SLOTS], m.sg[:, c % 2, :],
                                  ALU.mult).then_inc(m.h_ready, 1)
            tokens()
            dve.wait_ge(m.d_done, n + 1)
            y_free(dve)
            dve.tensor_copy(m.y[0:SLOTS, s, 512:D], bank[5][0:SLOTS, :]).then_inc(m.y_ready, 1)

        def experts_act(act, m):
            def body(i, s, first, last):
                free = (lambda e: None) if first else (lambda e: e.wait_ge(m.y_out[s], i * 16))
                block_act(act, m, s, i * 2 + s, free, first and s == 0)

            turns(act, body)
            spare(act, blocks_needed(act, m),
                  lambda i, s: block_act(act, m, s, i * 2 + s, lambda e: e.wait_ge(m.y_out[s], i * 16), False))

        def experts_dve(dve, m):
            tokens_dve(dve, m, 0, 0)

            def body(i, s, first, last):
                free = (lambda e: None) if first else (lambda e: e.wait_ge(m.y_out[s], i * 16))
                e = i * 2 + s
                block_dve(dve, m, s, e, free, (lambda: None) if last and s == 1 else lambda: tokens_dve(dve, m, 1 - s, e + 1))

            turns(dve, body)

            def further(i, s):
                tokens_dve(dve, m, s, i * 2 + s)
                block_dve(dve, m, s, i * 2 + s, lambda e: e.wait_ge(m.y_out[s], i * 16), lambda: None)

            spare(dve, blocks_needed(dve, m), further)


        def view(start, *dims):
            one = work[:, start:start + 1]
            return bass.AP(one.tensor, one.offset, [list(one.ap[0])] + [list(d) for d in dims])

        def half(ap, b, tile, h):
            return ap[:, tile * P:(tile + 1) * P].rearrange("p (m h b) -> p m h b", h=2, b=b)[:, :, h, :]

        def all_halves(start, b, step):
            return view(start, (SEQ, 2), (2 * b, SEQ // (2 * b)), (step, b))

        tiles_diag = view(attn_at, (SEQ + P, NT), (1, P))
        pairs_off = view(attn_at + P, (2 * SEQ + 2 * P, 2), (SEQ - P, 2), (1, P))
        four_tiles = lambda b: b[:, :].rearrange("p (a t) -> p a t", a=NT)

        def hg_proj(pe, x, c, part, parts):
            if part == 0:
                pe.wait_ge(hg_in[c], x * 16 + 16)
            if c < 4:
                n = KD // parts
                for k in range(part * n, part * n + n):
                    last = pe.matmul(bank[4 + c % 2][:, :], w_hg[:, c, k, :], hT[:, k, :], start=k == 0, stop=k == KD - 1)
            else:
                n = NT // parts
                for i in range(part * n, part * n + n):
                    for k in range(KD):
                        last = pe.matmul(bank[6][:, i * P:(i + 1) * P], hT[:, k, i * P:(i + 1) * P], w_hg[:, c, k, :],
                                         start=k == 0, stop=k == KD - 1)
            if part == parts - 1:
                last.then_inc(hp_done, 1)

        def hg_pe(pe):
            hg_proj(pe, 0, 0, 0, 1)
            hg_proj(pe, 0, 4, 0, 1)
            hg_proj(pe, 0, 1, 0, 1)
            pe.wait_ge(h_q, 1)
            hg_proj(pe, 0, 2, 0, 1)
            pe.wait_ge(h_F, 1)
            hg_proj(pe, 0, 3, 0, 1)

            def head(h, more):
                x = h + 1
                pe.wait_ge(h_F, x * 2)
                if more:
                    hg_proj(pe, x, 0, 0, 2)
                else:
                    ret_proj(pe, 0, 0, 0, 2)
                pe.wait_ge(h_init, h + 1)
                for i in range(NT):
                    last = pe.matmul(bank[0][:, i * P:(i + 1) * P], ksum[:, i * P:(i + 1) * P], Q[:, i * P:(i + 1) * P],
                                     start=True, stop=True)
                last.then_inc(l_done, 1)
                if more:
                    hg_proj(pe, x, 0, 1, 2)
                else:
                    ret_proj(pe, 0, 0, 1, 2)
                for n in range(1, LEVELS + 1):
                    b = 1 << (n - 1)
                    if n == 2:
                        pe.wait_ge(h_base, h + 1)
                    if n >= 2:
                        pe.wait_ge(h_upd, h * 8 + n - 1)
                    for i in range(NT):
                        pe.matmul(half(bank[n % 2][:, :], b, i, 1), X[:, 0, i * P:(i + 1) * P], half(X[:, 2, :], b, i, 1),
                                  start=True, stop=True)
                        last = pe.matmul(half(bank[n % 2][:, :], b, i, 0), X[:, 3, i * P:(i + 1) * P],
                                         half(X[:, 1, :], b, i, 0), start=True, stop=True)
                    last.then_inc(l_done, 1)
                    if more:
                        c, part = HG_ORDER[(n + 1) // 2], (n + 1) % 2
                        if n == 1:
                            pe.wait_ge(h_V, x)
                        if n == 3:
                            pe.wait_ge(h_gate, h + 1)
                        if n == 5:
                            pe.wait_ge(h_q, x + 1)
                        if n == 7:
                            pe.wait_ge(h_F, x * 2 + 1)
                            hg_proj(pe, x, 3, 0, 4)
                            hg_proj(pe, x, 3, 1, 4)
                        else:
                            hg_proj(pe, x, c, part, 2)
                    elif n < LEVELS:
                        if n == 1:
                            pe.wait_ge(h_gate, x)
                        if n == 3:
                            pe.wait_ge(h_V, x)
                        ret_proj(pe, 0, (n + 1) // 2, (n + 1) % 2, 2)
                pe.wait_ge(h_upd, h * 8 + 7)
                for m, (a, t, arrays) in enumerate(((0, 1, (0, 2)), (1, 0, (3, 1)), (2, 3, (0, 2)), (3, 2, (3, 1)))):
                    last = pe.matmul(bank[0][:, m * P:(m + 1) * P], X[:, arrays[0], a * P:(a + 1) * P],
                                     X[:, arrays[1], t * P:(t + 1) * P], start=True, stop=True)
                last.then_inc(l_done, 1)
                if more:
                    hg_proj(pe, x, 3, 2, 4)
                pe.wait_ge(h_upd, h * 8 + 8)
                for a in range(NT):
                    back = a // 2
                    last = pe.matmul(bank[1 + back][:, (a % 2) * 256:(a % 2 + 1) * 256], X[:, 3 * back, a * P:(a + 1) * P],
                                     X[:, 2 - back, (1 - back) * 256:(2 - back) * 256], start=True, stop=True)
                    if a % 2:
                        last.then_inc(l_done, 1)
                pe.wait_ge(h_copy, h * LEVELS + LEVELS)
                pe.wait_ge(h_far, h * 3 + 3)
                pe.wait_ge(h_V, h + 1)
                for a in range(NT):
                    last = pe.matmul(bank[3][:, :], V[:, a, :], attnT[:, a, :], start=a == 0, stop=a == NT - 1)
                last.then_inc(h_av, 1)
                if more:
                    hg_proj(pe, x, 3, 3, 4)
                pe.wait_ge(h_sq, h + 1)
                pe.matmul(bank[2][:, :], ones[:, :], sqr, start=True, stop=True).then_inc(h_nm, 1)

            with pe.Fori(0, G_HEADS - 1) as h:
                head(h, True)
            head(G_HEADS - 1, False)

        def hg_act(act):
            act.wait_ge(lb_ready, 1)
            act.activation(head_row[:, 0, :], head_row[:, 4, :], ACT.Sigmoid).then_inc(lb_ready, 1)
            act.wait_ge(ang_ready, 1)
            act.activation(sinr, sinr, ACT.Sin)
            act.activation(cosr, cosr, ACT.Sin).then_inc(rot_ready, 1)

            def sig_q(x, first):
                if not first:
                    act.wait_ge(h_gate, x)
                act.wait_ge(hp_done, x * 5 + 1)
                act.activation(sig, bank[4][:, :], ACT.Sigmoid).then_inc(h_sig, 1)

            def sig_f(x, c):
                act.wait_ge(hp_done, x * 5 + 3 + c)
                act.activation(F[:, c, :], bank[5 - c][:, :], ACT.Sigmoid).then_inc(h_F, 1)

            def sig_gate(x):
                act.wait_ge(h_q, x + 1)
                act.wait_ge(hp_done, x * 5 + 5)
                act.activation(sig, bank[5][:, :], ACT.Sigmoid).then_inc(h_sig, 1)

            def values(x):
                act.wait_ge(hp_done, x * 5 + 2)
                act.activation(V, four_tiles(bank[6]), ACT.Copy).then_inc(h_V, 1)

            sig_q(0, True)
            values(0)
            sig_f(0, 0)
            sig_f(0, 1)
            sig_gate(0)

            def head(h, more):
                act.wait_ge(l_done, h * 11 + 1)
                act.activation(tiles_diag, four_tiles(bank[0]), ACT.Copy).then_inc(h_base, 1)
                if more:
                    sig_q(h + 1, False)
                    sig_f(h + 1, 0)
                    sig_f(h + 1, 1)
                act.wait_ge(l_done, h * 11 + 9)
                act.activation(pairs_off, bank[0][:, :].rearrange("p (a b t) -> p a b t", a=2, b=2), ACT.Copy).then_inc(h_far, 1)
                for back in range(2):
                    act.wait_ge(l_done, h * 11 + 10 + back)
                    act.activation(attnT[:, 2 * back:2 * back + 2, (1 - back) * 256:(2 - back) * 256],
                                   bank[1 + back][:, :].rearrange("p (a t) -> p a t", a=2), ACT.Copy).then_inc(h_far, 1)
                act.wait_ge(h_av, h + 1)
                act.activation(sqr, bank[3][:, :], ACT.Square).then_inc(h_sq, 1)
                if more:
                    values(h + 1)
                act.wait_ge(h_var, h + 1)
                act.activation(root, root, ACT.Sqrt).then_inc(h_root, 1)
                if more:
                    sig_gate(h + 1)

            with act.Fori(0, G_HEADS - 1) as h:
                head(h, True)
            head(G_HEADS - 1, False)

        def angles_dve(dve):
            def step(ins):
                ins.then_inc(*dve_own.up())
                dve.wait_ge(*dve_own.now())

            dve.wait_ge(pos_in, 16)
            step(dve.tensor_copy(cosr, sinr.bitcast(I32)))
            step(dve.tensor_scalar(ang, cosr, rates[:, 0:1], None, ALU.mult))
            step(dve.tensor_scalar(turns_, ang, 1.0 / (2.0 * np.pi), None, ALU.mult))
            step(dve.tensor_scalar(turns_, turns_, ROUND, None, ALU.add))
            step(dve.tensor_scalar(turns_, turns_, -ROUND, None, ALU.add))
            for part in TWO_PI:
                step(dve.scalar_tensor_tensor(ang, turns_, -part, ang, ALU.mult, ALU.add))
            step(dve.tensor_scalar(sinr, ang, PI_BELOW, -PI_BELOW, ALU.min, ALU.max))
            step(dve.tensor_scalar(cosr, ang, float(np.pi / 2), None, ALU.add))
            step(dve.tensor_scalar(turns_, cosr, PI_BELOW, float(2.0 * np.pi), ALU.is_gt, ALU.mult))
            step(dve.tensor_tensor(cosr, cosr, turns_, ALU.subtract))
            dve.tensor_scalar(cosr, cosr, PI_BELOW, -PI_BELOW, ALU.min, ALU.max).then_inc(ang_ready, 1)

        def rotate(dve, x, own, first, out, done, is_k):
            even, odd = bank[first], bank[first + 1]
            dve.wait_ge(rp_done, x * 7 + 2 + 2 * is_k)
            for o, (ce, co, op) in enumerate(((cosr, sinr, ALU.subtract), (sinr, cosr, ALU.add))):
                dve.tensor_tensor(out[:, o, :], even[:, :], ce, ALU.mult).then_inc(*own.up())
                dve.tensor_tensor(rtmp[:, o, :], odd[:, :], co, ALU.mult).then_inc(*own.up())
                dve.wait_ge(*own.now())
                last = dve.tensor_tensor(out[:, o, :], out[:, o, :], rtmp[:, o, :], op)
                if o == 0:
                    last.then_inc(*own.up())
            last.then_inc(done, 1)
            dve.wait_ge(done, x + 1)

        def hg_dve(dve):
            dve.wait_ge(lb_in, 64)
            dve.tensor_tensor(head_row[:, 4, :], head_row[:, 5, :], head_row[:, 4, :], ALU.subtract).then_inc(lb_ready, 1)
            dve.wait_ge(lb_ready, 2)
            dve.tensor_scalar(head_row[:, 1, :], head_row[:, 0, :], -1.0, 1.0, ALU.mult, ALU.add).then_inc(*dve_own.up())
            dve.wait_ge(*dve_own.now())

            def query(x):
                dve.wait_ge(h_sig, x * 2 + 1)
                dve.tensor_tensor(Q, bank[4][:, :], sig, ALU.mult).then_inc(h_q, 1)

            def gates(x):
                dve.wait_ge(h_sig, x * 2 + 2)
                dve.scalar_tensor_tensor(gate, bank[5][:, :], head_row[:, 2, bass.ds(x, 1)], sig, ALU.mult,
                                         ALU.mult).then_inc(h_gate, 1)

            def arrays(x, own):
                dve.wait_ge(h_F, x * 2 + 2)
                dve.wait_ge(h_q, x + 1)
                dve.tensor_scalar(T, F, head_row[:, 1, bass.ds(x, 1)], head_row[:, 0, bass.ds(x, 1)], ALU.mult,
                                  ALU.add).then_inc(*own.up())
                dve.wait_ge(*own.now())
                dve.tensor_scalar(view(x_at, (3 * SEQ, 2), (1, SEQ)), T, -1.0, 1.0, ALU.mult, ALU.add).then_inc(*own.up())
                dve.tensor_tensor(X[:, 2, :], T[:, 0, :], Q, ALU.mult)
                dve.tensor_tensor(X[:, 1, :], T[:, 1, :], Q, ALU.mult)
                dve.wait_ge(*own.now())
                dve.tensor_tensor(ksum, X[:, 0, :], X[:, 3, :], ALU.add).then_inc(h_init, 1)

            angles_dve(dve)
            query(0)
            arrays(0, dve_own)
            gates(0)

            def head(h, more, own):
                for n in range(1, LEVELS + 2):
                    b = 1 << (n - 1)
                    dve.wait_ge(l_done, h * 11 + n + 1)
                    if n >= 2:
                        dve.wait_ge(*own.now())
                        dve.wait_ge(h_upd, h * 8 + n - 1)
                    else:
                        dve.wait_ge(h_init, h + 1)
                    if n == 1:
                        dve.wait_ge(h_base, h + 1)
                    elif n <= LEVELS:
                        dve.wait_ge(h_copy, h * LEVELS + n - 1)
                    up, low = x_at + 2 * SEQ + b, x_at
                    dve.tensor_tensor(all_halves(up, b, 1), all_halves(up, b, 1), all_halves(t_at, b, 0), ALU.mult)
                    dve.tensor_tensor(all_halves(low, b, 1), all_halves(low, b, 1), all_halves(t_at + b, b, 0),
                                      ALU.mult).then_inc(h_upd, 1)
                    if n <= LEVELS:
                        dve.copy_predicated(tiles_diag, masks[:, n - 1, :].unsqueeze(1).to_broadcast([P, NT, P]),
                                            four_tiles(bank[n % 2])).then_inc(h_copy, 1)
                        dve.wait_ge(h_upd, h * 8 + n)
                        starts = view(t_at, (SEQ, 2), (2 * b, SEQ // (2 * b)))
                        dve.tensor_tensor(starts, starts, view(t_at + b, (SEQ, 2), (2 * b, SEQ // (2 * b))),
                                          ALU.mult).then_inc(*own.up())
                    if n == 3 and more:
                        query(h + 1)
                dve.wait_ge(h_upd, h * 8 + 8)
                dve.wait_ge(l_done, h * 11 + 11)
                if more:
                    arrays(h + 1, own)
                else:
                    dve.wait_ge(rot_ready, 1)
                    rotate(dve, 0, own, 4, rq, rr_q, 0)
                    rotate(dve, 0, own, 6, rk, rr_k, 1)
                dve.wait_ge(h_nm, h + 1)
                dve.tensor_scalar(root, bank[2][:, :], 1.0 / P, EPS, ALU.mult, ALU.add).then_inc(h_var, 1)
                dve.tensor_tensor(sqr, bank[3][:, :], gate, ALU.mult).then_inc(*own.up())
                dve.wait_ge(h_root, h + 1)
                dve.reciprocal(root, root).then_inc(*own.up())
                dve.wait_ge(*own.now())
                dve.tensor_tensor(oTh[:, bass.ds(h, 1), :], sqr.unsqueeze(1), root.unsqueeze(1), ALU.mult).then_inc(h_fin, 1)
                if more:
                    gates(h + 1)

            with dve.Fori(0, G_HEADS - 1) as h:
                dve_own.loop(h, 4 + LEVELS)
                head(h, True, dve_own)
            dve_own.loop_end(G_HEADS - 1)
            head(G_HEADS - 1, False, dve_own)


        def ret_proj(pe, x, n, part=0, parts=1):
            c = (0, 0, 1, 1, 2, 2, 3)[n]
            if n in (0, 2, 4, 6) and part == 0:
                pe.wait_ge(ret_in[c], x * 16 + 16)
            if n < 6:
                cols = slice(n % 2, R_DIM, 2) if n < 4 else slice((n - 4) * P, (n - 3) * P)
                for k in range(part * KD // parts, (part + 1) * KD // parts):
                    last = pe.matmul(bank[4 + n % 4][:, :], w_ret[:, c, k, cols], hT[:, k, :], start=k == 0, stop=k == KD - 1)
            else:
                for i in range(NT):
                    for k in range(KD):
                        last = pe.matmul(bank[6 + i // 2][:, (i % 2) * R_DIM:(i % 2 + 1) * R_DIM], hT[:, k, i * P:(i + 1) * P],
                                         w_ret[:, c, k, :], start=k == 0, stop=k == KD - 1)
            if part == parts - 1:
                last.then_inc(rp_done, 1)

        def ret_pe(pe):
            pe.wait_ge(rr_q, 1)
            ret_proj(pe, 0, 4)
            ret_proj(pe, 0, 5)
            pe.wait_ge(rr_k, 1)
            ret_proj(pe, 0, 6)

            def head(h, more):
                x = h + 1
                if more:
                    pe.wait_ge(r_gate, x * 2)
                    ret_proj(pe, x, 0)
                pe.wait_ge(rr_k, h + 1)
                pe.wait_ge(r_fin, h + 1)
                for a in range(NT):
                    for e in range(2):
                        last = pe.matmul(bank[a][:, :], rk[:, e, a * P:(a + 1) * P], rq[:, e, :], start=e == 0, stop=e == 1)
                    last.then_inc(rs_done, 1)
                if more:
                    ret_proj(pe, x, 1)
                    pe.wait_ge(r_V, x)
                    ret_proj(pe, x, 2)
                    ret_proj(pe, x, 3)
                pe.wait_ge(r_dec, h * 4 + 4)
                pe.wait_ge(r_V, h + 1)
                for v in range(2):
                    for a in range(NT):
                        last = pe.matmul(bank[v][:, :], rV[:, a, v * P:(v + 1) * P], rattn[:, a, :], start=a == 0,
                                         stop=a == NT - 1)
                    last.then_inc(r_av, 1)
                if more:
                    pe.wait_ge(rr_q, x + 1)
                    ret_proj(pe, x, 4)
                    ret_proj(pe, x, 5)
                pe.wait_ge(r_sq, h * 2 + 2)
                for v in range(2):
                    last = pe.matmul(bank[2][:, :], ones[:, :], rtmp[:, v, :], start=v == 0, stop=v == 1)
                last.then_inc(r_nm, 1)
                if more:
                    pe.wait_ge(rr_k, x + 1)
                    ret_proj(pe, x, 6)

            with pe.Fori(0, R_HEADS - 1) as h:
                head(h, True)
            head(R_HEADS - 1, False)

        def ret_act(act):
            def sig_gates(x):
                for v in range(2):
                    act.wait_ge(rp_done, x * 7 + 5 + v)
                    act.activation(rsq[:, v, :], bank[4 + v][:, :], ACT.Sigmoid).then_inc(r_sig, 1)

            def values(x):
                act.wait_ge(rp_done, x * 7 + 7)
                for v in range(2):
                    last = act.activation(rV[:, 2 * v:2 * v + 2, :], bank[6 + v][:, :].rearrange("p (a n) -> p a n", a=2), ACT.Copy)
                last.then_inc(r_V, 1)

            act.wait_ge(h_fin, G_HEADS)
            sig_gates(0)
            values(0)

            def head(h, more):
                for v in range(2):
                    act.wait_ge(r_av, h * 2 + 1 + v)
                    if v == 0:
                        act.wait_ge(r_tmp, h + 1 + more)
                    act.activation(rtmp[:, v, :], bank[v][:, :], ACT.Square).then_inc(r_sq, 1)
                if more:
                    sig_gates(h + 1)
                act.wait_ge(r_var, h + 1)
                act.activation(rroot, rroot, ACT.Sqrt).then_inc(r_root, 1)
                if more:
                    values(h + 1)

            with act.Fori(0, R_HEADS - 1) as h:
                head(h, 1)
            head(R_HEADS - 1, 0)

        def ret_dve(dve):
            dve.sem_inc(r_fin, 1)
            dve.sem_inc(r_tmp, 1)

            def gates(x):
                for v in range(2):
                    dve.wait_ge(r_sig, x * 2 + 1 + v)
                    dve.scalar_tensor_tensor(rgate[:, v, :], bank[4 + v][:, :], head_row[:, 3, bass.ds(x * 2 + v, 1)],
                                             rsq[:, v, :], ALU.mult, ALU.mult).then_inc(r_gate, 1)

            gates(0)

            def head(h, more, own):
                if not more:
                    dve.wait_ge(r_V, R_HEADS)
                    dve.sem_inc(m_ready, 1)
                dve.wait_ge(decay_in, h * 16 + 16)
                for a in range(NT):
                    dve.wait_ge(rs_done, h * 4 + a + 1)
                    dve.tensor_tensor(rattn[:, a, :], bank[a][:, :], decay[:, SEQ - P - a * P:2 * SEQ - P - a * P],
                                      ALU.mult).then_inc(r_dec, 1)
                if more:
                    rotate(dve, h + 1, own, 4, rq, rr_q, 0)
                    rotate(dve, h + 1, own, 6, rk, rr_k, 1)
                    dve.sem_inc(r_tmp, 1)
                dve.wait_ge(r_nm, h + 1)
                dve.tensor_scalar(rroot, bank[2][:, :], 1.0 / R_DIM, EPS, ALU.mult, ALU.add).then_inc(r_var, 1)
                for v in range(2):
                    dve.tensor_tensor(rtmp[:, v, :], bank[v][:, :], rgate[:, v, :], ALU.mult).then_inc(*own.up())
                dve.wait_ge(r_root, h + 1)
                dve.reciprocal(rroot, rroot).then_inc(*own.up())
                dve.wait_ge(*own.now())
                dve.tensor_tensor(oTr[:, bass.ds(h * 2, 2), :], rtmp, rroot.unsqueeze(1).to_broadcast([P, 2, SEQ]),
                                  ALU.mult).then_inc(r_fin, 1)
                if more:
                    dve.wait_ge(r_fin, h + 2)
                    gates(h + 1)

            with dve.Fori(0, R_HEADS - 1) as h:
                dve_own.loop(h, 13)
                head(h, True, dve_own)
            dve_own.loop_end(R_HEADS - 1)
            head(R_HEADS - 1, False, dve_own)


        def merge_pe(pe):
            pe.wait_ge(h_fin, G_HEADS)
            with pe.Fori(0, KD // 2) as i:
                for s in range(2):
                    pe.wait_ge(mrg_in[s], i * 64 + 64)
                    pe.wait_ge(m_ready, i * 2 + s + 1)
                    for c, src in enumerate((hT, hT, oTh, oTr)):
                        if c == 3 and s == 0:
                            pe.wait_ge(r_fin, R_HEADS + 1)
                        for k in range(KD):
                            last = pe.matmul(bank[4 * (1 - s) + c][:, :], w_mrg[:, s, c, k, :], src[:, k, :], start=k == 0,
                                             stop=k == KD - 1)
                        last.then_inc(m_done, 1)
            pe.wait_ge(m_ready, KD + 2)
            pe.wait_ge(w_o2_in, 16)

        def merge_act(act):
            act.wait_ge(r_fin, R_HEADS + 1)
            with act.Fori(0, KD // 2) as i:
                for s in range(2):
                    for c in range(2):
                        act.wait_ge(m_done, i * 8 + 4 * s + c + 1)
                        act.wait_ge(m_ready, i * 2 + s + 1)
                        act.activation(msig[:, s, c, :], bank[4 * (1 - s) + c][:, :], ACT.Sigmoid).then_inc(m_sig, 1)

        def merge_dve(dve):
            dve.sem_inc(m_ready, 1)
            with dve.Fori(0, KD // 2) as i:
                dve_own.loop(i, 4)
                for s in range(2):
                    for c in range(2):
                        dve.wait_ge(m_done, i * 8 + 4 * s + c + 3)
                        dve.wait_ge(m_sig, i * 4 + 2 * s + c + 1)
                        dve.tensor_tensor(mtmp[:, s, c, :], bank[4 * (1 - s) + 2 + c][:, :], msig[:, s, c, :], ALU.mult).then_inc(*dve_own.up())
                    dve.wait_ge(*dve_own.now())
                    dve.tensor_tensor(merged[:, bass.ds(i * 2 + s, 1), :], mtmp[:, s, 0:1, :], mtmp[:, s, 1:2, :],
                                      ALU.add).then_inc(m_ready, 1)
            dve_own.loop_end(KD // 2)
            for i in range(NT):
                for n in (2 * i, 2 * i + 1):
                    dve.wait_ge(wo_done, 2 * NT + n + 1)
                    half = xres[:, i, (n % 2) * 512:(n % 2 + 1) * 512]
                    dve.scalar_tensor_tensor(half, half, ALPHA, bank[n % 4][:, :], ALU.mult, ALU.add).then_inc(x1_ready, 1)
                dve.wait_ge(x1_ready, 2 * NT + 2 * i + 2)
                if i == 0:
                    dve.wait_ge(ln_in, 32)
                layer_norm_tile(dve, 5, i, ln_row)
                if i >= 1:
                    fold_dve(dve, 4, i - 1, None)
            fold_dve(dve, 4, NT - 1, None)

        def layer_norm_tile(dve, r, i, rows):
            x = xres[:, i, :]
            for h in range(2):
                dve.bn_stats(bn[:, i, h, :], x[:, h * 512:(h + 1) * 512]).then_inc(*dve_own.up())
            dve.wait_ge(*dve_own.now())
            dve.bn_aggr(mv[:, i, :], bn[:, i, :, :]).then_inc(*dve_own.up())
            dve.wait_ge(*dve_own.now())
            dve.tensor_scalar(stat[:, i:i + 1], mv[:, i, 1:2], LN_EPS, None, ALU.add).then_inc(var_ready, 1)
            dve.scalar_tensor_tensor(x, x, mv[:, i, 0:1], rows[0], ALU.subtract, ALU.mult).then_inc(*dve_own.up())
            root_tile_dve(dve, r, i)
            dve.scalar_tensor_tensor(x, x, stat[:, i:i + 1], rows[1], ALU.mult, ALU.add).then_inc(ln_ready, 1)


        def root_tile_act(act, r, i):
            act.wait_ge(var_ready, roots_before[r] + i + 1)
            act.activation(stat[:, i:i + 1], stat[:, i:i + 1], ACT.Sqrt).then_inc(root_ready, 1)

        def root_tile_dve(dve, r, i):
            dve.wait_ge(root_ready, roots_before[r] + i + 1)
            dve.reciprocal(stat[:, i:i + 1], stat[:, i:i + 1]).then_inc(*dve_own.up())
            dve.wait_ge(*dve_own.now())

        def out_pe(pe, m, s, src, w, norm_src, ready):
            def project(i):
                for h in range(2):
                    n = 2 * i + h
                    if n >= 4:
                        pe.wait_ge(x1_ready, 2 * NT * m.past + n - 3)
                    for k in range(KD):
                        last = pe.matmul(bank[n % 4][:, :], src[:, k, i * P:(i + 1) * P], w[:, k, h * 512:(h + 1) * 512],
                                         start=k == 0, stop=k == KD - 1)
                    last.then_inc(wo_done, 1)

            def logits(i):
                pe.wait_ge(hT_ready, (s * NT + i) * 2 + 2)
                if i == 0:
                    pe.wait_ge(r_in, 48 * m.past + 48)
                    pe.wait_ge(x1_ready, 2 * NT * m.past + 5)
                for k in range(KD):
                    last = pe.matmul(bank[0][:, i * LOGITS:(i + 1) * LOGITS], hT[:, k, i * P:(i + 1) * P], m.w_r[:, k, :],
                                     start=k == 0, stop=k == KD - 1)
                if i == NT - 1:
                    last.then_inc(lg_done, 1)

            project(0)
            for i in range(1, NT):
                project(i)
                transposes_pe(pe, s, i - 1, norm_src, ready)
            logits(0)
            logits(1)
            transposes_pe(pe, s, NT - 1, norm_src, ready)
            for i in range(2, NT):
                logits(i)

        @block.sync
        def _(sp):
            sp.dma_start(ident[:, :], A["c_ident"]).then_inc(bias_in, 16)
            for i in range(NT):
                sp.dma_start(xres[:, i, :], A["x"][i * P:(i + 1) * P, :]).then_inc(x_in[i], 16)
            sp.dma_start(onehot, A["c_bucket"]).then_inc(bias_in, 16)
            sp.dma_start(masks_wide, A["c_masks"].rearrange("p a b -> p (a b)")).then_inc(gains_in, 16)
            sp.dma_start(relb[0:REL_BUCKETS, :], A["rel_bias"]).then_inc(bias_in, 16)
            for n, g in enumerate(("g_attn_norm", "g_ffn_norm")):
                sp.dma_start(gains[:, 2 * n, :], A[g].rearrange("a (p k) -> (a p) k", k=KD)).then_inc(gains_in, 16)
            sp.dma_start(gains[0:64, 1, :], A["g_out_a"].rearrange("a (p k) -> (a p) k", k=KD)).then_inc(gains_in, 16)
            sp.dma_start(gains[64:P, 1, :], A["g_out_b"].rearrange("a (p k) -> (a p) k", k=KD)).then_inc(gains_in, 16)
            for c in range(2):
                sp.dma_start(gains_c[:, c:c + 1], A["g_q_latent"][:, c * P:(c + 1) * P].rearrange("a (p k) -> (a p) k", k=1)).then_inc(gains_in, 16)
            sp.dma_start(gains_c[:, 2:3], A["g_kv_latent"].rearrange("a (p k) -> (a p) k", k=1)).then_inc(gains_in, 16)
            w_in = A["w_in"].rearrange("(p k) n -> p k n", k=KD)
            w_heads = w_in[:, :, 0:3 * A_WIDTH].rearrange("p k (c n) -> p k c n", c=3)

            def load_pair(pair):
                for c in range(3):
                    sp.dma_start(w_pair[:, :, c, :], w_heads[:, :, c, bass.ds(pair * P, P)]).then_inc(w_pair_in, 16)

            def load_toep(pair):
                for j in range(2):
                    row = bass.AP(table_dram.tensor, (pair * 2 + j) * (2 * SEQ), [[1, P], [1, TOEP]])
                    sp.dma_start(toep[:, j, :], row).then_inc(toep_in, 16)

            load_pair(0)
            sp.wait_ge(table_ready, 2)
            sp.dma_start(table_dram, table).then_inc(table_out, 16)
            sp.wait_ge(table_out, 16)
            load_toep(0)
            sp.dma_start(w_c, w_in[:, :, 3 * A_WIDTH:]).then_inc(w_c_in, 16)
            sp.dma_start(rope_q[:, :], A["c_rope_q"]).then_inc(rope_in, 16)
            sp.dma_start(rope_k[:, :, :, :], A["c_rope_k"]).then_inc(rope_in, 16)
            w_qu = A["w_q_up_rows"].rearrange("(c p) h m -> p c h m", c=2)
            w_kvu = A["w_kv_up"].rearrange("p (h m) -> p h m", h=B_HEADS)
            sp.dma_start(w_up_v, w_kvu[:, :, NOPE:]).then_inc(w_c_in, 16)

            def load_up(pair):
                for c in range(2):
                    sp.dma_start(w_up_q[:, c, :, :], w_qu[:, c, bass.ds(pair * 2, 2), :]).then_inc(w_up_in, 16)
                sp.dma_start(w_up_k, w_kvu[:, bass.ds(pair * 2, 2), 0:NOPE]).then_inc(w_up_in, 16)

            load_up(0)
            sp.dma_start(w_o, A["w_out"].rearrange("(p k) n -> p k n", k=KD)).then_inc(w_o_in, 16)
            sp.wait_ge(zeros_ready, 1)
            clear_spare_rows(sp, moe1)
            clear_spare_rows(sp, moe2)
            with sp.Fori(0, PAIRS - 1) as last:
                sp.wait_ge(proj_done, last * 3 + 3)
                load_pair(last + 1)
                sp.wait_ge(biased, last * STEPS + STEPS)
                load_toep(last + 1)
            with sp.Fori(0, PAIRS - 1) as last:
                sp.wait_ge(up_done, last * 4 + 4)
                load_up(last + 1)
            for n, r in ((0, "w_router_group"), (GROUPS, "w_router_expert")):
                cols = A[r].shape[1]
                sp.dma_start(w_r1[:, :, n:n + cols], A[r].rearrange("(p k) n -> p k n", k=KD)).then_inc(r_in, 16)
            sp.dma_start(b_r1, A["b_router"].partition_broadcast(P).rearrange("p a n -> p (a n)")).then_inc(r_in, 16)
            sp.dma_start(before, A["c_before"]).then_inc(route_in, 16)
            sp.dma_start(route, A["c_route"]).then_inc(route_in, 16)
            sp.dma_start(token[:, :], A["c_token"]).then_inc(route_in, 16)
            sp.dma_start(g_row, A["g_final"].partition_broadcast(P)).then_inc(g_row_in, 16)
            load_expert(sp, moe1, 0, 0)
            load_expert(sp, moe1, 1, 1)
            for i in range(NT):
                sp.wait_ge(normed, 2 * NT + i + 1)
                sp.dma_start(moe1.x_dram[i * P:(i + 1) * P, :], xn[:, i % 2, :]).then_inc(x_out[i], 16)
            w_in2 = A["w_in_2"].rearrange("(p k) n -> p k n", k=KD)

            def load_hg(h, c):
                sp.dma_start(w_hg[:, c, :, :], w_in2[:, :, bass.ds(h * P + HG_COLS[c], P)]).then_inc(hg_in[c], 16)

            def load_ret(h, c):
                sp.dma_start(w_ret[:, c, :, :], w_in2[:, :, bass.ds(h * R_DIM + R_COLS[c], R_DIM)]).then_inc(ret_in[c], 16)

            def load_decay(h):
                sp.dma_start(decay.unsqueeze(1), A["c_decay"][bass.ds(h, 1)].rearrange("a p n -> p a n")).then_inc(decay_in, 16)

            def load_merge(j, s):
                for c in range(2):
                    sp.dma_start(w_mrg[:, s, c, :, :], w_in2[:, :, bass.ds(j * P + M_COLS[c], P)]).then_inc(mrg_in[s], 16)
                for c, w in ((2, "w_branch_hg_2"), (3, "w_branch_ret_2")):
                    sp.dma_start(w_mrg[:, s, c, :, :], A[w].rearrange("(c p) n -> p c n", p=P)[:, :, bass.ds(j * P, P)]).then_inc(mrg_in[s], 16)

            col = lambda a: a.rearrange("a (h p) -> p (a h)", p=P)
            for r, g in ((2, "hg_norm_g_2"), (3, "ret_norm_g_2")):
                sp.dma_start(head_row[:, r, :], col(A[g]), allow_slow_non_contiguous=True).then_inc(lb_in, 16)
            sp.dma_start(head_row[:, 4:6, :].rearrange("p a h -> p (a h)"), col(A["hg_lb_logits_2"]),
                         allow_slow_non_contiguous=True).then_inc(lb_in, 16)
            sp.dma_start(rates[:, :], A["c_rates"]).then_inc(lb_in, 16)
            for c in range(5):
                load_hg(0, c)
            clear_list(sp, moe1)
            list_sp(sp, moe1)
            experts_sp(sp, moe1)
            sp.wait_ge(mixed, NT)
            sp.dma_start(sinr.bitcast(I32), A["positions_2"].partition_broadcast(P).rearrange("p a n -> p (a n)")).then_inc(pos_in, 16)
            for c in range(4):
                load_ret(0, c)
            with sp.Fori(0, G_HEADS - 1) as h:
                for n, c in enumerate(HG_ORDER):
                    sp.wait_ge(hp_done, h * 5 + n + 1)
                    load_hg(h + 1, c)
            sp.dma_start(w_r1[:, :, 0:GROUPS], A["w_group_2"].rearrange("(p k) n -> p k n", k=KD)).then_inc(r_in, 16)
            sp.dma_start(w_r1[:, :, GROUPS:], A["w_router_2"].rearrange("(p k) n -> p k n", k=KD)).then_inc(r_in, 16)
            sp.dma_start(b_r1, A["b_route_2"].partition_broadcast(P).rearrange("p a n -> p (a n)")).then_inc(r_in, 16)
            for row, g in zip(ln_row, ("ln1_g_2", "ln1_b_2")):
                sp.dma_start(row, A[g].partition_broadcast(P).rearrange("p a n -> p (a n)")).then_inc(ln_in, 16)
            sp.wait_ge(hp_done, 5 * G_HEADS)
            for s in range(2):
                load_merge(s, s)
            sp.wait_ge(h_fin, G_HEADS)
            load_decay(0)
            with sp.Fori(0, R_HEADS - 1) as h:
                for c, n in enumerate((2, 4, 6, 7)):
                    sp.wait_ge(rp_done, h * 7 + n)
                    load_ret(h + 1, c)
                sp.wait_ge(r_dec, h * 4 + 4)
                load_decay(h + 1)
            sp.wait_ge(rp_done, 7 * R_HEADS)
            sp.dma_start(w_o2, A["w_out_2"].rearrange("(k p) n -> p k n", p=P)).then_inc(w_o2_in, 16)
            with sp.Fori(0, KD // 2 - 1) as i:
                for s in range(2):
                    sp.wait_ge(m_done, i * 8 + 4 * s + 4)
                    load_merge(i * 2 + s + 2, s)
            sp.wait_ge(wo_done, 4 * NT)
            load_expert(sp, moe2, 0, 0)
            sp.wait_ge(x1_ready, 4 * NT)
            for c, g in enumerate(("ln2_g_2", "ln2_b_2")):
                sp.dma_start(moe2.rows[:, c, :], A[g].partition_broadcast(P).rearrange("p a n -> p (a n)")).then_inc(ln2_in, 16)
            for i in range(NT):
                sp.wait_ge(ln_ready, i + 1)
                sp.dma_start(moe2.x_dram[i * P:(i + 1) * P, :], xres[:, i, :]).then_inc(x_out[i], 16)
            clear_list(sp, moe2)
            sp.wait_ge(routed, 4)
            list_sp(sp, moe2)
            for arrived in moe2.xg_in:
                sp.wait_ge(arrived, 16)
            load_expert(sp, moe2, 1, 1)
            experts_sp(sp, moe2)
            for i in range(NT):
                sp.wait_ge(ln_ready, NT + i + 1)
                sp.dma_start(out[i * P:(i + 1) * P, :], xres[:, i, :]).then_inc(final_out, 16)
            sp.wait_ge(final_out, 16 * NT)

        @block.tensor
        def _(pe):
            pe.wait_ge(bias_in, 48)
            pe.wait_ge(ones_row, 1)
            for half in range(2):
                last = pe.matmul(bank[half][0:A_HEADS, :], relb, onehot[:, half * SEQ:(half + 1) * SEQ],
                                 start=True, stop=True)
            last.then_inc(table_mm, 1)
            norm_pe(pe, 0, lambda i: xn[:, i % 2, :], xn_ready(0))
            pe.wait_ge(hT_ready, 2 * NT)
            with pe.Fori(0, PAIRS) as pair:
                pe.wait_ge(w_pair_in, pair * 48 + 48)
                for c in range(2):
                    for k in range(KD):
                        last = pe.matmul(bank[6 + c][:, :], w_pair[:, k, c, :], hT[:, k, :], start=k == 0, stop=k == KD - 1)
                    last.then_inc(proj_done, 1)
                pe.wait_ge(q_ready, pair + 1)
                for i in range(NT):
                    for k in range(KD):
                        last = pe.matmul(bank[6][:, i * P:(i + 1) * P], hT[:, k, i * P:(i + 1) * P], w_pair[:, k, 2, :],
                                         start=k == 0, stop=k == KD - 1)
                last.then_inc(proj_done, 1)
                core_pe(pe, pair, 0, (
                    lambda j, i: qT[64 * j:64 * j + 64, 0, i * P:(i + 1) * P],
                    lambda j: kT[64 * j:64 * j + 64, 0, :],
                    lambda j, kc: v_pair[:, kc, j * A_DIM:(j + 1) * A_DIM]),
                    lambda: (pe.wait_ge(k_ready, pair + 1), pe.wait_ge(v_ready, pair + 1)))
            pe.wait_ge(w_c_in, 32)
            for i in range(NT):
                if i >= 2:
                    pe.wait_ge(c_ready, i - 1)
                for k in range(KD):
                    last = pe.matmul(bank[6 + i % 2][:, 0:C_WIDTH], hT[:, k, i * P:(i + 1) * P], w_c[:, k, :],
                                     start=k == 0, stop=k == KD - 1)
                last.then_inc(c_done, 1)
            for i in range(NT):
                pe.wait_ge(cn_ready, i + 1)
                for c, (start, wide) in enumerate(((0, P), (P, P), (2 * P, P), (3 * P, 96))):
                    last = pe.transpose(bank[c][0:wide, i * P:(i + 1) * P], cn[:, i, start:start + wide], ident[:, :])
            last.then_inc(ct_done, 1)
            pe.wait_ge(ct_ready, 1)
            pe.wait_ge(c_ready, NT)
            for i in range(NT):
                pe.matmul(bank[4 + i][:, :], cqT[:, 2, i * P:(i + 1) * P], w_up_v, start=True, stop=True).then_inc(vb_done, 1)
            pe.wait_ge(vb_ready, NT)
            with pe.Fori(0, PAIRS) as pair:
                pe.wait_ge(w_up_in, pair * 48 + 48)
                for j in range(2):
                    for c in range(2):
                        last = pe.matmul(bank[6 + j][:, :], w_up_q[:, c, j, :], cqT[:, c, :], start=c == 0, stop=c == 1)
                    last.then_inc(up_done, 1)
                for j in range(2):
                    pe.wait_ge(q_ready, pair * 2 + PAIRS + j + 1)
                    pe.wait_ge(rope_done, pair * 2 + j + 1)
                    pe.matmul(bank[6 + j][0:NOPE, :], w_up_k[:, j, :], cqT[:, 2, :], start=True, stop=True).then_inc(up_done, 1)
                core_pe(pe, pair, PAIRS * STEPS, (
                    lambda j, i: qT[0:96, j, i * P:(i + 1) * P],
                    lambda j: kT[0:96, j, :],
                    lambda j, kc: v_mla(pair, j, kc)),
                    lambda: (pe.wait_ge(k_ready, pair * 2 + PAIRS + 2), pe.wait_ge(q_roped, pair * 2 + 2)))
            norm_pe(pe, 1, lambda i: xn[:, i % 2, :], xn_ready(1))
            pe.wait_ge(hT_ready, 4 * NT)
            pe.wait_ge(w_o_in, 16)
            out_pe(pe, moe1, 2, hT, w_o, lambda i: xn[:, i % 2, :], xn_ready(2))
            pe.wait_ge(route_in, 48)
            pe.wait_ge(ones_ready, 1)
            route_pe(pe, moe1)
            experts_pe(pe, moe1)
            norm_pe(pe, 3, lambda i: xres[:, i, :], lambda pe, i: pe.wait_ge(fin_ready, i + 1))
            pe.wait_ge(hT_ready, 8 * NT)
            hg_pe(pe)
            ret_pe(pe)
            merge_pe(pe)
            out_pe(pe, moe2, 4, merged, w_o2, lambda i: xres[:, i, :], lambda pe, i: pe.wait_ge(ln_ready, i + 1))
            route_pe(pe, moe2)
            experts_pe(pe, moe2)

        @block.gpsimd
        def _(pool):
            route_pool(pool, moe1)
            experts_pool(pool, moe1)
            route_pool(pool, moe2)
            experts_pool(pool, moe2)

        @block.scalar
        def _(act):
            norm_act(act, 0, lambda i: xres[:, i, :], 1, lambda e, i: e.wait_ge(x_in[i], 16))
            with act.Fori(0, PAIRS) as pair:
                act.wait_ge(proj_done, pair * 3 + 1)
                act.activation(qT[:, 0, :], bank[6][:, :], ACT.Copy, scale=A_DIM ** -0.5).then_inc(q_ready, 1)
                act.wait_ge(proj_done, pair * 3 + 3)
                act.activation(v_pair[:, :, :], bank[6][:, :].rearrange("p (a b) -> p a b", a=NT), ACT.Copy).then_inc(v_ready, 1)
                core_act(act, pair, 0, pair * P)
            for i in range(NT):
                act.wait_ge(c_done, i + 1)
                act.activation(ctok[:, i, :], bank[6 + i % 2][:, 0:C_WIDTH], ACT.Copy).then_inc(c_ready, 1)
                act.wait_ge(c_ready, i + 1)
                act.activation(junk[:, 0:Q_LORA], ctok[:, i, 0:Q_LORA], ACT.Square, scale=(KV_LORA / Q_LORA) ** 0.5,
                               accum_out=stat[:, 2 * i:2 * i + 1]).then_inc(*act_own.up())
                act.wait_ge(*act_own.now())
                act.activation(junk[:, 0:KV_LORA], ctok[:, i, Q_LORA:Q_LORA + KV_LORA], ACT.Square,
                               accum_out=stat[:, 2 * i + 1:2 * i + 2]).then_inc(*act_own.up())
                act.wait_ge(*act_own.now())
            act.sem_inc(sq_ready, 1)
            root_act(act, 1, 2 * NT)
            for i in range(NT):
                act.wait_ge(vb_done, i + 1)
                act.activation(v[:, i, :], bank[4 + i][:, :], ACT.Copy).then_inc(vb_ready, 1)
            with act.Fori(0, PAIRS) as pair:
                for j in range(2):
                    act.wait_ge(up_done, pair * 4 + j + 1)
                    act.activation(qT[0:NOPE, j, :], bank[6 + j][0:NOPE, :], ACT.Copy).then_inc(q_ready, 1)
                core_act(act, pair, PAIRS * STEPS, pair * P + A_WIDTH)
            norm_act(act, 2, lambda i: outAB[:, i, :], 2, lambda e, i: e.wait_ge(o_ready, 2 * PAIRS * STEPS))
            for i in range(NT):
                act.wait_ge(x1_ready, 2 * i + 2)
                act.activation(junk, xres[:, i, :], ACT.Square, accum_out=stat[:, i:i + 1]).then_inc(sq_ready, 1)
                root_tile_act(act, 3, i)
            route_act(act, moe1)
            experts_act(act, moe1)
            norm_act(act, 4, lambda i: xres[:, i, :], 1, lambda e, i: e.wait_ge(mixed, i + 1), moe1.xg[:, 0, :])
            hg_act(act)
            ret_act(act)
            merge_act(act)
            for i in range(NT):
                root_tile_act(act, 5, i)
            route_act(act, moe2)
            experts_act(act, moe2)
            for i in range(NT):
                root_tile_act(act, 6, i)

        @block.vector
        def _(dve):
            dve.memset(relb[REL_BUCKETS:REL_BUCKETS + 1, :], 1.0).then_inc(ones_row, 1)
            dve.memset(zeros[:, :], 0.0).then_inc(zeros_ready, 1)
            dve.memset(ones[:, :], 1.0).then_inc(ones_ready, 1)
            dve.memset(cn[:, :, 3 * P:3 * P + 64], 0.0)
            for half in range(2):
                dve.wait_ge(table_mm, 1)
                dve.tensor_copy(table[:, half * SEQ:(half + 1) * SEQ], bank[half][0:A_HEADS, :]).then_inc(table_ready, 1)
            dve.wait_ge(gains_in, 16 * 8)
            dve.tensor_copy(masks[:, :, :].rearrange("p a b -> p (a b)"), masks_wide).then_inc(*dve_own.up())
            dve.wait_ge(*dve_own.now())
            norm_dve(dve, 0, 0, lambda i: xres[:, i, :], 1, gains[:, 0, :])
            with dve.Fori(0, PAIRS) as pair:
                dve.wait_ge(proj_done, pair * 3 + 2)
                dve.tensor_copy(kT[:, 0, :], bank[7][:, :]).then_inc(k_ready, 1)
                dve.wait_ge(toep_in, pair * 32 + 32)
                core_dve(dve, pair, 0, toep_tile, 1.0)
            dve.wait_ge(rope_in, 32)
            dve.wait_ge(c_ready, NT)
            for i in range(NT):
                x1, x2 = ctok[:, i, 384:400], ctok[:, i, 400:416]
                cos, sin = rope_k[:, i, 0, :], rope_k[:, i, 1, :]
                for n, (x, t) in enumerate(((x1, cos), (x2, sin), (x1, sin), (x2, cos))):
                    dve.tensor_tensor(rope_t[:, i, n, :], x, t, ALU.mult).then_inc(*dve_own.up())
            dve.wait_ge(*dve_own.now())
            dve.tensor_tensor(cn[:, :, 448:464], rope_t[:, :, 0, :], rope_t[:, :, 1, :], ALU.subtract)
            dve.tensor_tensor(cn[:, :, 464:480], rope_t[:, :, 2, :], rope_t[:, :, 3, :], ALU.add)
            root_dve(dve, 1, 2 * NT, KV_LORA, EPS)
            for i in range(NT):
                dve.tensor_scalar(cn[:, i, 0:Q_LORA], ctok[:, i, 0:Q_LORA], stat[:, 2 * i:2 * i + 1], None, ALU.mult)
                dve.tensor_scalar(cn[:, i, Q_LORA:3 * P], ctok[:, i, Q_LORA:3 * P], stat[:, 2 * i + 1:2 * i + 2], None,
                                  ALU.mult).then_inc(cn_ready, 1)
            dve.wait_ge(ct_done, 1)
            for c in range(3):
                dve.tensor_scalar(cqT[:, c, :], bank[c][:, :], gains_c[:, c:c + 1], None, ALU.mult)
            for j in range(2):
                last = dve.tensor_copy(kT[64:96, j, :], bank[3][64:96, :])
            last.then_inc(ct_ready, 1)
            with dve.Fori(0, PAIRS) as pair:
                dve_own.loop(pair, 2)
                for j in range(2):
                    dve.wait_ge(up_done, pair * 4 + j + 1)
                    dve.tensor_tensor(rope_s[64:96, j, :], bank[6 + j][96:P, :], rope_q[96:P, :], ALU.mult).then_inc(*dve_own.up())
                    dve.tensor_tensor(qT[64:96, j, :], bank[6 + j][64:96, :], rope_q[64:96, :], ALU.mult).then_inc(rope_done, 1)
                    dve.wait_ge(*dve_own.now())
                    dve.wait_ge(rope_done, pair * 2 + j + 1)
                    dve.tensor_tensor(qT[64:96, j, :], qT[64:96, j, :], rope_s[64:96, j, :], ALU.add).then_inc(q_roped, 1)
                for j in range(2):
                    dve.wait_ge(up_done, pair * 4 + j + 3)
                    dve.tensor_copy(kT[0:NOPE, j, :], bank[6 + j][0:NOPE, :]).then_inc(k_ready, 1)
                core_dve(dve, pair, PAIRS * STEPS, lambda j, i: zeros[:, :], (NOPE + ROPE) ** -0.5)
            dve_own.loop_end(PAIRS)
            norm_dve(dve, 1, 2, lambda i: outAB[:, i, :], 2, gains[:, 1, :])
            for i in range(NT):
                for n in (2 * i, 2 * i + 1):
                    dve.wait_ge(wo_done, n + 1)
                    half = xres[:, i, (n % 2) * 512:(n % 2 + 1) * 512]
                    dve.tensor_tensor(half, half, bank[n % 4][:, :], ALU.add).then_inc(x1_ready, 1)
                dve.wait_ge(sq_ready, roots_before[3] + i + 1)
                dve.tensor_scalar(stat[:, i:i + 1], stat[:, i:i + 1], 1.0 / D, EPS, ALU.mult, ALU.add).then_inc(var_ready, 1)
                root_tile_dve(dve, 3, i)
                if i >= 2:
                    dve.wait_ge(tr_done, (2 * NT + i - 2) * 2 + 2)
                    dve.wait_ge(x_out[i - 2], 16)
                dve.tensor_scalar(xn[:, i % 2, :], xres[:, i, :], stat[:, i:i + 1], None, ALU.mult).then_inc(normed, 1)
                if i >= 1:
                    fold_dve(dve, 2, i - 1, gains[:, 2, :])
            fold_dve(dve, 2, NT - 1, gains[:, 2, :])
            dve.memset(moe1.zero_i, 0).then_inc(zero_ready, 1)
            dve.wait_ge(route_in, 48)
            route_dve(dve, moe1)
            experts_dve(dve, moe1)
            for i in range(NT):
                dve.wait_ge((yg_in0, yg_in1)[i // 2], 64)
                for c in range(2):
                    dve.scalar_tensor_tensor(xres[:, i, :], moe1.yg[:, c * NT + i, :], moe1.gate[:, c, i:i + 1], xres[:, i, :],
                                             ALU.mult, ALU.add).then_inc(*dve_own.up())
                    dve.wait_ge(*dve_own.now())
                dve.sem_inc(mixed, 1)
            root_dve(dve, 4, NT, D, EPS)
            dve.wait_ge(g_row_in, 16)
            for i in range(NT):
                dve.scalar_tensor_tensor(xres[:, i, :], xres[:, i, :], stat[:, i:i + 1], g_row, ALU.mult,
                                         ALU.mult).then_inc(fin_ready, 1)
            for i in range(NT):
                fold_dve(dve, 3, i, None)
            hg_dve(dve)
            ret_dve(dve)
            merge_dve(dve)
            dve.memset(moe2.zero_i, 0).then_inc(zero_ready, 1)
            route_dve(dve, moe2)
            for i in range(NT):
                dve.wait_ge(x_out[i], 32)
                dve.tensor_scalar(xres[:, i, :], xres[:, i, :], ALPHA, None, ALU.mult).then_inc(*dve_own.up())
            experts_dve(dve, moe2)
            dve.wait_ge(*dve_own.now())
            for i in range(NT):
                dve.wait_ge((yg_in0, yg_in1)[i // 2], 128)
                for c in range(2):
                    dve.scalar_tensor_tensor(xres[:, i, :], moe2.yg[:, c * NT + i, :], moe2.gate[:, c, i:i + 1], xres[:, i, :],
                                             ALU.mult, ALU.add).then_inc(*dve_own.up())
                    dve.wait_ge(*dve_own.now())
                if i == 0:
                    dve.wait_ge(ln2_in, 32)
                layer_norm_tile(dve, 6, i, (moe2.rows[:, 0, :], moe2.rows[:, 1, :]))



def kernel(**inputs):
    import numpy as _np
    import concourse.bacc as _bacc
    from concourse import mybir as _mybir
    from concourse.bass_utils import run_bass_kernel_spmd as _run

    arrays = {}
    for name, a in inputs.items():
        a = _np.ascontiguousarray(a)
        if name not in ("g_final", "rel_bias", "hg_lb_logits_2"):
            a = a.reshape(a.shape[1:]) if a.ndim > 2 else a
        arrays[name] = a
    up = arrays.pop("w_q_up").reshape(Q_LORA, B_HEADS, NOPE + ROPE)
    arrays["w_q_up_rows"] = _np.ascontiguousarray(_np.concatenate([up, up[:, :, 80:96], up[:, :, 64:80]], 2))
    arrays["b_router"] = _np.concatenate([arrays.pop("b_router_group"), arrays.pop("b_router_expert")], 1)
    arrays["b_route_2"] = _np.concatenate([arrays.pop("b_group_2"), arrays.pop("b_router_2")], 1)
    arrays.update(constants())
    nc = _bacc.Bacc("TRN2", target_bir_lowering=False, num_devices=1)
    aps = {n: nc.dram_tensor(f"in_{n}", a.shape, _mybir.dt.from_np(a.dtype), kind="ExternalInput").ap()
           for n, a in arrays.items()}
    out = nc.dram_tensor("out", (SEQ, D), F32, kind="ExternalOutput").ap()
    build(nc, aps, out)
    r = _run(nc, [{f"in_{n}": a for n, a in arrays.items()}], core_ids=[0])
    return r.results[0]["out"].reshape(1, SEQ, D)
```
